# Optimizing a Trainium2 kernel written in Bass

```python
import math
import jax, jax.numpy as jnp
from jax import lax
import numpy as np

D_MODEL = 1024
BATCH = 1
SEQ = 128
DEPTH = 1
DEC_BATCH = 1
DEC_SEQ = 512
PAST_LEN = 128

GRID_W = 64
CHUNK = 128
GMLP_WIDTH = 1024
GMLP_GROUPS = 8
GMLP_GROUP_DIM = GMLP_WIDTH // GMLP_GROUPS
SSD_INNER = 2 * D_MODEL
SSD_HEADDIM = 64
SSD_HEADS = SSD_INNER // SSD_HEADDIM
SSD_GROUPS = 4
SSD_HPG = SSD_HEADS // SSD_GROUPS
SSD_STATE = 128
SSD_CONV = 5
SSD_CONV_CH = SSD_INNER + 2 * SSD_GROUPS * SSD_STATE
N_EXPERTS = 16
N_EXPERT_GROUPS = 4
EXPERTS_PER_GROUP = N_EXPERTS // N_EXPERT_GROUPS
TOP_K = 2
D_EXPERT = 512
N_MOD = 6
EPS = 1e-6

IN_PROJ_DIM = 2 * D_MODEL + 2 * GMLP_WIDTH + SSD_INNER + SSD_CONV_CH + 2 * SSD_HEADS
IN_SPLITS = (
    D_MODEL,
    2 * D_MODEL,
    2 * D_MODEL + GMLP_WIDTH,
    2 * D_MODEL + 2 * GMLP_WIDTH,
    2 * D_MODEL + 2 * GMLP_WIDTH + SSD_INNER,
    2 * D_MODEL + 2 * GMLP_WIDTH + SSD_INNER + SSD_CONV_CH,
    2 * D_MODEL + 2 * GMLP_WIDTH + SSD_INNER + SSD_CONV_CH + SSD_HEADS,
)

kernel_name = 'hybrid_gmlp_ssd_moe_diffusion_step'

def _rmsnorm(x, w):
    xf = x.astype(jnp.float32)
    y = xf * lax.rsqrt(jnp.mean(xf * xf, axis=-1, keepdims=True) + EPS)
    return (y * w.astype(jnp.float32)).astype(x.dtype)

def _group_rmsnorm(x, w, groups):
    shp = x.shape
    xg = x.astype(jnp.float32).reshape(shp[:-1] + (groups, shp[-1] // groups))
    y = xg * lax.rsqrt(jnp.mean(xg * xg, axis=-1, keepdims=True) + EPS)
    return (y.reshape(shp) * w.astype(jnp.float32)).astype(x.dtype)

def _grid_pos_embed(n_tokens, dim, dtype):
    rows = n_tokens // GRID_W
    quarter = dim // 4
    omega = 1.0 / (10000.0 ** (jnp.arange(quarter, dtype=jnp.float32) / quarter))
    r = jnp.arange(rows, dtype=jnp.float32)[:, None] * omega
    col = jnp.arange(GRID_W, dtype=jnp.float32)[:, None] * omega
    r_emb = jnp.concatenate([jnp.sin(r), jnp.cos(r)], axis=-1)
    c_emb = jnp.concatenate([jnp.sin(col), jnp.cos(col)], axis=-1)
    emb = jnp.concatenate([
        jnp.broadcast_to(r_emb[:, None, :], (rows, GRID_W, dim // 2)),
        jnp.broadcast_to(c_emb[None, :, :], (rows, GRID_W, dim // 2))], axis=-1)
    return emb.reshape(rows * GRID_W, dim).astype(dtype)

def _modulation(cond, w_mod, b_mod):
    return jax.nn.silu(cond) @ w_mod + b_mod

def _dwconv_centered(x, w, b):
    ch = x.shape[-1]
    pad = SSD_CONV // 2
    y = lax.conv_general_dilated(
        x, w[:, None, :].astype(x.dtype), window_strides=(1,), padding=[(pad, pad)],
        dimension_numbers=('NWC', 'WIO', 'NWC'), feature_group_count=ch)
    return y + b.astype(x.dtype)

def _flip_seq(t):
    return jnp.flip(t, axis=1)

def _ssd_chunked(x, dt, a_neg, bm, cm, h0):
    f32 = jnp.float32
    b, l = x.shape[:2]
    nc = l // CHUNK
    x = x.astype(f32)
    dt = dt.astype(f32)
    a = (dt * a_neg).reshape(b, nc, CHUNK, SSD_GROUPS, SSD_HPG)
    xdt = (x * dt[..., None]).reshape(b, nc, CHUNK, SSD_GROUPS, SSD_HPG, SSD_HEADDIM)
    bc = bm.astype(f32).reshape(b, nc, CHUNK, SSD_GROUPS, SSD_STATE)
    cc = cm.astype(f32).reshape(b, nc, CHUNK, SSD_GROUPS, SSD_STATE)
    a_cs = jnp.cumsum(a, axis=2)
    lower = jnp.tril(jnp.ones((CHUNK, CHUNK), dtype=bool))[:, :, None, None]
    seg = a_cs[:, :, :, None] - a_cs[:, :, None, :]
    decay = jnp.exp(jnp.where(lower, seg, -jnp.inf))
    cb = jnp.einsum('bctgn,bcsgn->bctsg', cc, bc)
    y_diag = jnp.einsum('bctsgh,bcsghp->bctghp', cb[..., None] * decay, xdt)
    decay_end = jnp.exp(a_cs[:, :, -1:] - a_cs)
    states = jnp.einsum('bcsgn,bcsghp->bcghpn', bc, xdt * decay_end[..., None])
    chunk_decay = jnp.exp(a_cs[:, :, -1])

    def step(h, inp):
        st, dec = inp
        return h * dec[..., None, None] + st, h

    h_last, h_in = lax.scan(step, h0.astype(f32),
                            (jnp.moveaxis(states, 1, 0), jnp.moveaxis(chunk_decay, 1, 0)))
    h_in = jnp.moveaxis(h_in, 0, 1)
    y_off = jnp.einsum('bctgn,bcghpn->bctghp', cc, h_in) * jnp.exp(a_cs)[..., None]
    y = (y_diag + y_off).reshape(b, l, SSD_GROUPS, SSD_HPG, SSD_HEADDIM)
    return y, h_last

def _bi_ssd(xbc, z, dt_f, dt_b, conv_w, conv_b, dt_bias, a_log, d_skip, norm_w, h0_f, h0_b):
    f32 = jnp.float32
    b, l, _ = xbc.shape
    xbc = jax.nn.silu(_dwconv_centered(xbc, conv_w, conv_b))
    xh, bm, cm = jnp.split(xbc, [SSD_INNER, SSD_INNER + SSD_GROUPS * SSD_STATE], axis=-1)
    xh = xh.reshape(b, l, SSD_GROUPS, SSD_HPG, SSD_HEADDIM)
    bm = bm.reshape(b, l, SSD_GROUPS, SSD_STATE)
    cm = cm.reshape(b, l, SSD_GROUPS, SSD_STATE)
    dt = jax.nn.softplus(jnp.stack([dt_f, dt_b], axis=0).astype(f32)
                         + dt_bias.astype(f32)[:, None, None, :])
    dt = dt.reshape(2, b, l, SSD_GROUPS, SSD_HPG)
    a_neg = -jnp.exp(a_log.astype(f32)).reshape(2, SSD_GROUPS, SSD_HPG)
    y_f, h_f = _ssd_chunked(xh, dt[0], a_neg[0], bm, cm, h0_f)
    y_r, h_b = _ssd_chunked(_flip_seq(xh), _flip_seq(dt[1]), a_neg[1],
                            _flip_seq(bm), _flip_seq(cm), h0_b)
    y = (y_f + _flip_seq(y_r)
         + xh.astype(f32) * d_skip.astype(f32).reshape(SSD_GROUPS, SSD_HPG)[:, :, None])
    y = y.reshape(b, l, SSD_INNER).astype(z.dtype)
    y = _group_rmsnorm(y * jax.nn.silu(z), norm_w, SSD_GROUPS)
    return y, h_f, h_b

def _chunk_gmlp(u, v, norm_w, ws, bs):
    b, l, _ = u.shape
    u = jax.nn.gelu(u)
    v = _rmsnorm(jax.nn.gelu(v), norm_w)
    vc = v.reshape(b, l // CHUNK, CHUNK, GMLP_GROUPS, GMLP_GROUP_DIM)
    mixed = (jnp.einsum('gts,bcsgd->bctgd', ws, vc)
             + jnp.swapaxes(bs, 0, 1)[:, :, None])
    return u * mixed.reshape(b, l, GMLP_WIDTH)

def _moe(h, router_w, router_bias, w_gate, w_up, w_down):
    f32 = jnp.float32
    shp = h.shape
    t = h.reshape(-1, shp[-1])
    n = t.shape[0]
    scores = jax.nn.sigmoid((t @ router_w).astype(f32))
    sel = scores + router_bias.astype(f32)
    group_score = lax.top_k(sel.reshape(n, N_EXPERT_GROUPS, EXPERTS_PER_GROUP), TOP_K)[0].sum(-1)
    best = jnp.argmax(group_score, axis=-1)
    in_group = (jnp.arange(N_EXPERTS) // EXPERTS_PER_GROUP)[None, :] == best[:, None]
    _, idx = lax.top_k(jnp.where(in_group, sel, -jnp.inf), TOP_K)
    w = jnp.take_along_axis(scores, idx, axis=-1)
    w = w / jnp.sum(w, axis=-1, keepdims=True)
    gates = jnp.einsum('tk,tke->et', w, jax.nn.one_hot(idx, N_EXPERTS, dtype=f32)).astype(t.dtype)

    def expert(acc, inp):
        wg, wu, wd, g = inp
        y = (jax.nn.silu(t @ wg) * (t @ wu)) @ wd
        return acc + g[:, None] * y, None

    out, _ = lax.scan(expert, jnp.zeros_like(t), (w_gate, w_up, w_down, gates))
    return out.reshape(shp)

def _layer(x, mod, p, router_w, router_bias, h0_f, h0_b):
    sh1, sc1, g1, sh2, sc2, g2 = jnp.split(mod, N_MOD, axis=-1)
    h = _rmsnorm(x, p['norm1_w']) * (1 + sc1) + sh1
    proj = h @ p['w_in']
    gate_a, gate_b, u, v, z, xbc, dt_f, dt_b = jnp.split(proj, IN_SPLITS, axis=-1)
    y_a = _chunk_gmlp(u, v, p['gmlp_norm_w'], p['gmlp_ws'], p['gmlp_bs'])
    y_b, h_f, h_b = _bi_ssd(xbc, z, dt_f, dt_b, p['conv_w'], p['conv_b'], p['dt_bias'],
                            p['a_log'], p['d_skip'], p['ssd_norm_w'], h0_f, h0_b)
    merged = (jax.nn.sigmoid(gate_a) * (y_a @ p['w_branch_a'])
              + jax.nn.sigmoid(gate_b) * (y_b @ p['w_branch_b']))
    x = x + g1 * (merged @ p['w_out'])
    h2 = _rmsnorm(x, p['norm2_w']) * (1 + sc2) + sh2
    x = x + g2 * _moe(h2, router_w, router_bias, p['w_gate_e'], p['w_up_e'], p['w_down_e'])
    return x, h_f, h_b

def setup_inputs(seed: int = 0) -> dict:
    key = jax.random.key(seed)
    ks = jax.random.split(key, 32)
    nrm = jax.random.normal
    f32 = jnp.float32
    D = D_MODEL
    dt0 = jnp.exp(jax.random.uniform(ks[14], (DEPTH, 2, SSD_HEADS), f32,
                                     minval=math.log(1e-3), maxval=math.log(1e-1)))
    return {
        'x_prompt': nrm(ks[0], (BATCH, SEQ, D), f32),
        'x_sample': nrm(ks[1], (DEC_BATCH, DEC_SEQ, D), f32),
        'state_ssd': 0.1 * nrm(ks[2], (DEC_BATCH, DEPTH, 2, SSD_HEADS, SSD_HEADDIM, SSD_STATE), f32),
        'c': nrm(ks[3], (DEC_BATCH, D), f32),
        'c_ctx': nrm(ks[4], (D,), f32),
        'w_mod': 0.5 * D ** -0.5 * nrm(ks[5], (DEPTH, D, N_MOD * D), f32),
        'b_mod': 0.02 * nrm(ks[6], (DEPTH, N_MOD * D), f32),
        'norm1_w': 1.0 + 0.02 * nrm(ks[7], (DEPTH, D), f32),
        'w_in': D ** -0.5 * nrm(ks[8], (DEPTH, D, IN_PROJ_DIM), f32),
        'gmlp_norm_w': 1.0 + 0.02 * nrm(ks[9], (DEPTH, GMLP_WIDTH), f32),
        'gmlp_ws': CHUNK ** -0.5 * nrm(ks[10], (DEPTH, GMLP_GROUPS, CHUNK, CHUNK), f32),
        'gmlp_bs': 0.02 * nrm(ks[11], (DEPTH, GMLP_GROUPS, CHUNK), f32),
        'conv_w': SSD_CONV ** -0.5 * nrm(ks[12], (DEPTH, SSD_CONV, SSD_CONV_CH), f32),
        'conv_b': 0.02 * nrm(ks[13], (DEPTH, SSD_CONV_CH), f32),
        'dt_bias': dt0 + jnp.log(-jnp.expm1(-dt0)),
        'a_log': jnp.log(jax.random.uniform(ks[15], (DEPTH, 2, SSD_HEADS), f32, minval=1.0, maxval=16.0)),
        'd_skip': 1.0 + 0.02 * nrm(ks[16], (DEPTH, SSD_HEADS), f32),
        'ssd_norm_w': 1.0 + 0.02 * nrm(ks[17], (DEPTH, SSD_INNER), f32),
        'w_branch_a': GMLP_WIDTH ** -0.5 * nrm(ks[18], (DEPTH, GMLP_WIDTH, D), f32),
        'w_branch_b': SSD_INNER ** -0.5 * nrm(ks[19], (DEPTH, SSD_INNER, D), f32),
        'w_out': D ** -0.5 * nrm(ks[20], (DEPTH, D, D), f32),
        'norm2_w': 1.0 + 0.02 * nrm(ks[21], (DEPTH, D), f32),
        'router_w': D ** -0.5 * nrm(ks[22], (D, N_EXPERTS), f32),
        'router_bias': 0.01 * nrm(ks[23], (N_EXPERTS,), f32),
        'w_gate_e': D ** -0.5 * nrm(ks[24], (DEPTH, N_EXPERTS, D, D_EXPERT), f32),
        'w_up_e': D ** -0.5 * nrm(ks[25], (DEPTH, N_EXPERTS, D, D_EXPERT), f32),
        'w_down_e': D_EXPERT ** -0.5 * nrm(ks[26], (DEPTH, N_EXPERTS, D_EXPERT, D), f32),
        'final_norm_w': 1.0 + 0.02 * nrm(ks[27], (D,), f32),
    }

def reference(x_prompt, x_sample, state_ssd, c, c_ctx, w_mod, b_mod, norm1_w, w_in,
              gmlp_norm_w, gmlp_ws, gmlp_bs, conv_w, conv_b, dt_bias, a_log, d_skip,
              ssd_norm_w, w_branch_a, w_branch_b, w_out, norm2_w, router_w, router_bias,
              w_gate_e, w_up_e, w_down_e, final_norm_w):
    bp = x_prompt.shape[0]
    bs, ls = x_sample.shape[0], x_sample.shape[1]
    xp = x_prompt
    xs = x_sample + _grid_pos_embed(ls, D_MODEL, x_sample.dtype)[None]
    zero_state = jnp.zeros((bp, SSD_GROUPS, SSD_HPG, SSD_HEADDIM, SSD_STATE), jnp.float32)
    cache = state_ssd.reshape(bs, DEPTH, 2, SSD_GROUPS, SSD_HPG, SSD_HEADDIM, SSD_STATE)
    new_states = []
    for l in range(DEPTH):
        p = {
            'norm1_w': norm1_w[l], 'w_in': w_in[l], 'gmlp_norm_w': gmlp_norm_w[l],
            'gmlp_ws': gmlp_ws[l], 'gmlp_bs': gmlp_bs[l], 'conv_w': conv_w[l],
            'conv_b': conv_b[l], 'dt_bias': dt_bias[l], 'a_log': a_log[l],
            'd_skip': d_skip[l], 'ssd_norm_w': ssd_norm_w[l], 'w_branch_a': w_branch_a[l],
            'w_branch_b': w_branch_b[l], 'w_out': w_out[l], 'norm2_w': norm2_w[l],
            'w_gate_e': w_gate_e[l], 'w_up_e': w_up_e[l], 'w_down_e': w_down_e[l],
        }
        mod_ctx = _modulation(c_ctx[None, None, :], w_mod[l], b_mod[l])
        mod_lat = _modulation(c[:, None, :], w_mod[l], b_mod[l])
        xp, h_f, h_b = _layer(xp, mod_ctx, p, router_w, router_bias, zero_state, zero_state)
        new_states.append(jnp.stack([h_f, h_b], axis=1))
        xs, _, _ = _layer(xs, mod_lat, p, router_w, router_bias, cache[:, l, 0], cache[:, l, 1])
    new_state_ssd = jnp.stack(new_states, axis=1).reshape(
        bp, DEPTH, 2, SSD_HEADS, SSD_HEADDIM, SSD_STATE).astype(x_prompt.dtype)
    y_prompt = _rmsnorm(xp, final_norm_w)
    y_sample = _rmsnorm(xs, final_norm_w)
    return (y_prompt, y_sample, new_state_ssd)


_drawn_inputs = setup_inputs


def setup_inputs(seed=0):
    import zlib

    import numpy as np

    out = dict(_drawn_inputs(seed))
    spreads = {}
    factors = {'state_ssd': 3.011,
     'gmlp_norm_w': 37.7,
     'gmlp_bs': 26.204,
     'd_skip': 28.814,
     'ssd_norm_w': 22.072,
     'final_norm_w': 9.817,
     'norm2_w': 4.174}
    for name, (base, spread) in spreads.items():
        noise = np.random.default_rng([zlib.crc32(name.encode()), seed]).standard_normal(out[name].shape)
        drawn = base * np.exp(spread * noise) if base else spread * noise
        out[name] = __import__('jax').numpy.asarray(drawn.astype(out[name].dtype))
    for name, factor in factors.items():
        out[name] = (out[name] * factor).astype(out[name].dtype)
    return out
```

```python
import concourse.bass as bass
from concourse import mybir
from contextlib import ExitStack

F32 = mybir.dt.float32
F32R = mybir.dt.float32r
BF16 = mybir.dt.bfloat16
I32 = mybir.dt.int32
U32 = mybir.dt.uint32
ALU = mybir.AluOpType
ACT = mybir.ActivationFunctionType
AX = mybir.AxisListType

P = 128
D = 1024
KD = D // P
NC = 5
T = NC * P
LAT = T - P
HALF = T // 2
G = 4
HPG = 8
HEADS = G * HPG
HD = 64
GW = HPG * HD
INNER = G * GW
KI = INNER // P
NE = 16
NG = 4
FE = 512
EPS = 1e-6
TAPS = 5
UNIT = 2048
UC = 256
NMB = 26
BIG = 1.0e30

O_H = 0
O_X = 10240
O_BC = 20480
O_TMP = 28160
O_MG = 33280
O_RAW = 38400
O_HL = 42496
O_K = 50688
ARENA = 52992
REGIONS = (O_H, O_X, O_BC, O_TMP, O_MG, O_RAW, O_HL, O_K)
KOFF = dict(ident=0, le=128, ge=256, gt=384, lt=512, one=640, e128=768, pri16=784, pri4=800, thr=804, col=812, end=840)


def n_units(widths, col):
    return sum(widths[:col])


class Kit:

    def __init__(self, nc, ctx):
        self.nc, self.sems = nc, []
        self.arena = ctx.enter_context(nc.sbuf_tensor("arena", [P, ARENA], F32))
        self.base = nc.sbuf_base - 4 * ARENA
        self.tensors = {}
        self.ps = ctx.enter_context(nc.psum_tensor("banks", [P, 8, 512], F32))

    def sem(self, name):
        self.sems.append(self.nc.alloc_semaphore(name=name))
        return self.sems[-1]

    def recycle(self):
        self.nc.clear_and_free_semaphores(self.sems)
        self.nc.all_engine_barrier()
        self.sems = []

    def placed(self, name, off, n, dtype):
        if name not in self.tensors:
            self.tensors[name] = self.nc.alloc_sbuf_tensor_at(name, [P, n], dtype,
                                                              offset=self.base + 4 * off)
        return self.tensors[name]

    def at(self, off, *dims):
        n = 1
        for d in dims:
            n *= d
        first = max(o for o in REGIONS if o <= off)
        end = min(o for o in REGIONS + (ARENA,) if o >= off + n)
        t = self.placed(f"words_{first}_{end}", first, end - first, F32)
        return self.shaped(t[:, off - first:off - first + n], dims)

    def rnd(self, off, *dims):
        n = 1
        for d in dims:
            n *= d
        return self.shaped(self.placed(f"rounded_{off}_{n}", off, n, F32R)[:, :], dims)

    def shaped(self, v, dims):
        if len(dims) == 2:
            v = v.rearrange("p (a b) -> p a b", a=dims[0])
        if len(dims) == 3:
            v = v.rearrange("p (a b c) -> p a b c", a=dims[0], b=dims[1])
        return v

    def const(self, name, n=P):
        return self.at(O_K, KOFF["end"])[:, KOFF[name]:KOFF[name] + n]


class Chain:

    def __init__(self, eng, sem):
        self.eng, self.sem, self.n = eng, sem, 0

    def step(self, ins):
        ins.then_inc(self.sem, 1)
        self.n += 1

    def sync(self):
        self.eng.wait_ge(self.sem, self.n)


class Weights:

    def __init__(self, kit, stage, src):
        self.kit, self.nc, self.src = kit, kit.nc, src
        self.raw = kit.at(O_RAW, 2, UNIT)
        self.hi, self.lo = kit.rnd(O_HL, 2, UNIT), kit.rnd(O_HL + 2 * UNIT, 2, UNIT)
        self.raw_loaded = [kit.sem(f"{stage}_raw_loaded{s}") for s in range(2)]
        self.hi_ready = kit.sem(f"{stage}_hi_ready")
        self.lo_ready = kit.sem(f"{stage}_lo_ready")
        self.used = kit.sem(f"{stage}_unit_used")

    def load(self, sp, i):
        if i >= 2:
            sp.wait_ge(self.lo_ready, i - 1)
        sp.dma_start(self.raw[:, i % 2, :], self.src(i)).then_inc(self.raw_loaded[i % 2], 16)

    def split_hi(self, act, i):
        act.wait_ge(self.raw_loaded[i % 2], 16 * (i // 2 + 1))
        if i >= 2:
            act.wait_ge(self.used, i - 1)
        self.nc.scalar.activation(self.hi[:, i % 2, :], self.raw[:, i % 2, :],
                                  ACT.Copy).then_inc(self.hi_ready, 1)

    def split_lo(self, dve, i):
        dve.wait_ge(self.hi_ready, i + 1)
        if i >= 2:
            dve.wait_ge(self.used, i - 1)
        self.nc.vector.tensor_tensor(self.lo[:, i % 2, :], self.raw[:, i % 2, :],
                                     self.hi[:, i % 2, :].bitcast(F32), ALU.subtract).then_inc(self.lo_ready, 1)

    def parts(self, i, k):
        return [x[:, i % 2, :].rearrange("p (k n) -> p k n", k=k)
                for x in (self.hi, self.lo)]

    def ready(self, pe, i):
        pe.wait_ge(self.hi_ready, i + 1)
        pe.wait_ge(self.lo_ready, i + 1)


def split3(nc, out, lhs, rhs, nk):
    for k in range(nk):
        nc.tensor.matmul(out, lhs[0](k), rhs[0](k), start=(k == 0), stop=False)
        nc.tensor.matmul(out, lhs[0](k), rhs[1](k), start=False, stop=False)
        last = nc.tensor.matmul(out, lhs[1](k), rhs[0](k), start=False, stop=(k == nk - 1))
    return last


def feature_tile(nc, w, t, moving, out, nk, after_first_half=None):
    for h in range(2):
        last = split3(nc, out(h), [lambda k, x=x: x[:, k, t * P:(t + 1) * P] for x in w],
                      [lambda k, x=x: x[:, k, h * HALF:(h + 1) * HALF] for x in moving], nk)
    return last


def token_tile(nc, w, c, stationary, out):
    return split3(nc, out, [lambda k, x=x: x[:, k, c * P:(c + 1) * P] for x in stationary],
                  [lambda k, x=x: x[:, k, :] for x in w], KD)


def halves(kit, pair):
    return kit.ps[:, 2 * pair:2 * pair + 2, 0:HALF]


def two(ap):
    return ap.rearrange("p (h n) -> p h n", h=2)


def stage_modulate(kit, io, scr):
    nc, ps = kit.nc, kit.ps
    WM = kit.at(O_MG, 4, 4096)
    x = kit.at(O_X, NC, D)
    pos = kit.at(O_X + 5120, NC - 1, D)
    cond = kit.at(O_TMP, 16)
    sc = kit.at(O_TMP + 16, 16)
    row = kit.at(O_TMP + 32, 2048)
    brow = kit.at(O_TMP + 2080, 2048)
    n1 = kit.at(O_TMP + 4128, KD)
    AS = kit.at(O_TMP + 4136, 2, KD, 2)
    ssq = kit.at(O_TMP + 4168, NC)
    rr = kit.at(O_TMP + 4173, NC)
    sq = kit.at(O_BC, D)
    full = kit.at(O_BC + 1024, 2, T)
    hi, lo = kit.rnd(O_H, KD, T), kit.rnd(O_H + 5120, KD, T)
    ident = kit.const("ident")
    s_small, s_x, s_w = kit.sem("m_small"), kit.sem("m_x"), [kit.sem(f"m_w{j}") for j in range(4)]
    s_c = kit.sem("m_consts")
    s_act, s_dve, s_row, s_cols = kit.sem("m_act"), kit.sem("m_dve"), kit.sem("m_row"), kit.sem("m_cols")
    s_xt, s_full, s_split, s_xp = kit.sem("m_xt"), kit.sem("m_full"), kit.sem("m_split"), kit.sem("m_xp")

    with nc.Block() as block:
        @block.sync
        def _(sp):
            sp.dma_start(kit.at(O_K, KOFF["end"]), io["consts"]).then_inc(s_c, 16)
            sp.dma_start(cond, io["cond"]).then_inc(s_small, 16)
            sp.dma_start(x, io["x"].rearrange("(c p) d -> p c d", p=P)).then_inc(s_x, 16)
            sp.dma_start(pos, io["pos"].rearrange("(c p) d -> p c d", p=P)).then_inc(s_x, 16)
            sp.dma_start(n1, io["norm1"]).then_inc(s_small, 16)
            sp.dma_start(brow[0:2, :], io["b_mod"][:, 0:2048].partition_broadcast(2)).then_inc(s_small, 16)
            for j in range(4):
                sp.dma_start(WM[:, j, :], io["w_mod"][j]).then_inc(s_w[j], 16)
            sp.wait_ge(s_dve, 2)
            sp.dma_start(scr["xp"].rearrange("(c p) d -> p c d", p=P), x).then_inc(s_xp, 16)
            sp.wait_ge(s_xp, 16)

        @block.scalar
        def _(act):
            act.wait_ge(s_small, 48)
            nc.scalar.activation(sc, cond, ACT.Silu).then_inc(s_act, 1)
            act.wait_ge(s_dve, 2)
            for c in range(NC):
                if c:
                    act.wait_ge(s_act, c + 1)
                nc.scalar.activation(sq, x[:, c, :], ACT.Square, accum_out=ssq[:, c:c + 1]).then_inc(s_act, 1)
            act.wait_ge(s_dve, 4)
            nc.scalar.activation(rr, rr, ACT.Sqrt).then_inc(s_act, 1)
            for k in range(KD):
                act.wait_ge(s_xt, k + 1)
                act.wait_ge(s_cols, 2)
                if k >= 2:
                    act.wait_ge(s_split, 2 * (k - 1))
                for st, lo_, hi_ in ((0, 0, P), (1, P, T)):
                    b = 2 * (k % 2)
                    src = ps[:, b:b + 2, :].rearrange("p a b -> p (a b)")[:, lo_:hi_]
                    nc.scalar.activation(full[:, k % 2, lo_:hi_], src, ACT.Identity,
                                         scale=AS[:, 1, k, st:st + 1],
                                         bias=AS[:, 0, k, st:st + 1]).then_inc(s_full, 1)

        @block.vector
        def _(dve):
            ch = Chain(dve, s_dve)
            dve.wait_ge(s_x, 32)
            ch.step(nc.vector.tensor_tensor(x[:, 1:3, :], x[:, 1:3, :], pos[:, 0:2, :], ALU.add))
            ch.step(nc.vector.tensor_tensor(x[:, 3:5, :], x[:, 3:5, :], pos[:, 2:4, :], ALU.add))
            dve.wait_ge(s_act, 1 + NC)
            ch.step(nc.vector.tensor_scalar(ssq, ssq, 1.0 / D, EPS, ALU.mult, ALU.add))
            ch.sync()
            ch.step(nc.vector.reciprocal(rr, ssq))
            dve.wait_ge(s_act, 2 + NC)
            dve.wait_ge(s_xp, 16)
            for c in range(NC):
                ch.step(nc.vector.tensor_scalar(x[:, c, :], x[:, c, :], rr[:, c:c + 1], None, ALU.mult))
            for j in range(4):
                dve.wait_ge(s_row, j + 1)
                ch.step(nc.vector.tensor_tensor(row[0:2, j * 512:(j + 1) * 512], ps[0:2, 4 + j % 2, :],
                                                brow[0:2, j * 512:(j + 1) * 512], ALU.add))
            dve.wait_ge(s_row, 5)
            v = ps[:, 6, 0:32].rearrange("p (q k s) -> p q k s", q=2, k=KD)
            nc.vector.tensor_copy(AS[:, 0, :, :], v[:, 0, :, :]).then_inc(s_cols, 1)
            nc.vector.scalar_tensor_tensor(out=AS[:, 1, :, :], in0=v[:, 1, :, :], scalar=1.0,
                                           in1=n1.unsqueeze(2).broadcast_to([P, KD, 2]),
                                           op0=ALU.add, op1=ALU.mult).then_inc(s_cols, 1)
            for k in range(KD):
                dve.wait_ge(s_full, 2 * k + 2)
                nc.vector.tensor_copy(hi[:, k, :], full[:, k % 2, :]).then_inc(s_split, 1)
                dve.wait_ge(s_split, 2 * k + 1)
                nc.vector.tensor_tensor(lo[:, k, :], full[:, k % 2, :], hi[:, k, :].bitcast(F32),
                                        ALU.subtract).then_inc(s_split, 1)

        @block.tensor
        def _(pe):
            pe.wait_ge(s_c, 16)
            pe.wait_ge(s_act, 1)
            for j in range(4):
                pe.wait_ge(s_w[j], 16)
                if j >= 2:
                    pe.wait_ge(s_dve, 4 + NC + j - 1)
                for k in range(KD):
                    last = nc.tensor.matmul(ps[0:2, 4 + j % 2, :], sc.rearrange("p (k s) -> p k s", s=2)[:, k, :],
                                            WM[:, j, k * 512:(k + 1) * 512], start=(k == 0), stop=(k == KD - 1))
                last.then_inc(s_row, 1)
            pe.wait_ge(s_dve, 4 + NC + 4)
            for j in range(16):
                last = nc.tensor.transpose(ps[:, 6, 2 * j:2 * j + 2], row[0:2, j * P:(j + 1) * P], ident[0:2, 0:2])
            last.then_inc(s_row, 1)
            for k in range(KD):
                if k >= 2:
                    pe.wait_ge(s_full, 2 * (k - 1))
                b = 2 * (k % 2)
                for c in range(NC):
                    o = ps[:, b, c * P:(c + 1) * P] if c < 4 else ps[:, b + 1, 0:P]
                    last = nc.tensor.transpose(o, x[:, c, k * P:(k + 1) * P], ident)
                last.then_inc(s_xt, 1)
    return hi, lo


def stage_gmlp(kit, io, scr, ht):
    nc, ps = kit.nc, kit.ps
    V = kit.at(O_X, NC, D)
    ya = kit.at(O_X + 5120, KD, T)
    ya_hi, ya_lo = kit.rnd(O_X + 5120, KD, T), kit.rnd(O_X + 10240, KD, T)
    full = kit.at(O_TMP, 2, T)
    wsT = kit.at(O_TMP + 1280, KD, P)
    bsb = kit.at(O_TMP + 2304, KD, P)
    nw = kit.at(O_TMP + 3328, KD)
    ssq = kit.at(O_TMP + 3336, NC)
    rr = kit.at(O_TMP + 3341, NC)
    sq = kit.at(O_TMP + 3400, D)
    n = 8
    w = Weights(kit, "g", lambda i: io["units"][i])
    s_c = kit.sem("g_consts")
    s_v, s_vev = kit.sem("g_v"), kit.sem("g_v_taken")
    s_u, s_uev = kit.sem("g_u"), kit.sem("g_u_taken")
    s_sq, s_n = kit.sem("g_squares"), kit.sem("g_norm")
    s_mix, s_m, s_split = kit.sem("g_mixed"), kit.sem("g_product"), kit.sem("g_split")
    s_zero, s_zo = kit.sem("g_zero"), kit.sem("g_zeros_stored")

    with nc.Block() as block:
        @block.sync
        def _(sp):
            sp.dma_start(wsT, io["wsT"]).then_inc(s_c, 16)
            sp.dma_start(nw, io["gmlp_nw"]).then_inc(s_c, 16)
            sp.dma_start(bsb, io["gmlp_bs"].partition_broadcast(P)).then_inc(s_c, 16)
            for i in range(n):
                w.load(sp, i)

        @block.gpsimd
        def _(pool):
            zero = kit.at(O_TMP + 4600, 512)
            nc.gpsimd.memset(zero, 0.0).then_inc(s_zero, 1)
            pool.wait_ge(s_zero, 1)
            rows = [(scr["xs"], b) for b in range(NMB + 1)] + [(scr["ys"], b) for b in range(NE, NMB)]
            for dst, b in rows:
                pool.dma_start(dst[b * P:(b + 1) * P, :].rearrange("p (a d) -> p a d", a=2),
                               zero.unsqueeze(1).broadcast_to([P, 2, 512])).then_inc(s_zo, 16)
            pool.wait_ge(s_zo, 16 * len(rows))

        @block.tensor
        def _(pe):
            for i in range(4):
                w.ready(pe, i)
                for c in range(NC):
                    if i:
                        pe.wait_ge(s_vev, NC * (i - 1) + c + 1)
                    last = token_tile(nc, w.parts(i, KD), c, ht, ps[:, c, 0:UC])
                    if c < NC - 1:
                        last.then_inc(s_v, 1)
                last.then_inc(w.used, 1)
            pe.wait_ge(s_vev, NC * 4)
            for i in range(4, 8):
                w.ready(pe, i)
                for t in range(2):
                    if i > 4:
                        pe.wait_ge(s_uev, 2 * (i - 5) + t + 1)
                    last = feature_tile(nc, w.parts(i, KD), t, ht, lambda h: halves(kit, t)[:, h, :], KD)
                    if t == 0:
                        last.then_inc(s_u, 1)
                last.then_inc(w.used, 1)
            pe.wait_ge(s_c, 48)
            pe.wait_ge(s_n, 2 + NC)
            for g in range(KD):
                if g >= 2:
                    pe.wait_ge(s_m, 3 * (g - 2) + 1)
                b = 4 + 2 * (g % 2)
                for c in range(NC):
                    o = ps[:, b, c * P:(c + 1) * P] if c < 4 else ps[:, b + 1, 0:P]
                    last = nc.tensor.matmul(o, V[:, c, g * P:(g + 1) * P], wsT[:, g, :], start=True, stop=True)
                last.then_inc(s_mix, 1)

        @block.scalar
        def _(act):
            w.split_hi(act, 0)
            for i in range(4):
                w.split_hi(act, i + 1)
                for c in range(NC):
                    if c < NC - 1:
                        act.wait_ge(s_v, (NC - 1) * i + c + 1)
                    else:
                        act.wait_ge(w.used, i + 1)
                    nc.scalar.activation(V[:, c, i * UC:(i + 1) * UC], ps[:, c, 0:UC],
                                         ACT.Gelu_apprx_tanh).then_inc(s_vev, 1)
            act.wait_ge(s_vev, NC * 4)
            for i in range(4, 8):
                if i + 1 < 8:
                    w.split_hi(act, i + 1)
                for t in range(2):
                    if t == 0:
                        act.wait_ge(s_u, i - 4 + 1)
                    else:
                        act.wait_ge(w.used, i + 1)
                    nc.scalar.activation(two(ya[:, 2 * (i - 4) + t, :]), halves(kit, t),
                                         ACT.Gelu_apprx_tanh).then_inc(s_uev, 1)
                if i == 4:
                    for c in range(NC):
                        if c:
                            act.wait_ge(s_sq, c)
                        nc.scalar.activation(sq, V[:, c, :], ACT.Square,
                                             accum_out=ssq[:, c:c + 1]).then_inc(s_sq, 1)
            act.wait_ge(s_n, 2)
            nc.scalar.activation(rr, rr, ACT.Sqrt).then_inc(s_sq, 1)
            for g in range(KD):
                act.wait_ge(s_m, 3 * g + 3)
                nc.scalar.activation(ya_hi[:, g, :], full[:, g % 2, :], ACT.Copy).then_inc(s_split, 1)

        @block.vector
        def _(dve):
            w.split_lo(dve, 0)
            for i in range(4):
                w.split_lo(dve, i + 1)
            w.split_lo(dve, 5)
            dve.wait_ge(s_sq, NC)
            nc.vector.tensor_scalar(ssq, ssq, 1.0 / D, EPS, ALU.mult, ALU.add).then_inc(s_n, 1)
            dve.wait_ge(s_n, 1)
            nc.vector.reciprocal(rr, ssq).then_inc(s_n, 1)
            w.split_lo(dve, 6)
            w.split_lo(dve, 7)
            dve.wait_ge(s_sq, NC + 1)
            for c in range(NC):
                nc.vector.tensor_scalar(V[:, c, :], V[:, c, :], rr[:, c:c + 1], None, ALU.mult).then_inc(s_n, 1)
            dve.wait_ge(s_c, 48)
            dve.wait_ge(s_uev, 8)
            for g in range(KD):
                dve.wait_ge(s_mix, g + 1)
                b = 4 + 2 * (g % 2)
                mixed = ps[:, b:b + 2, :].rearrange("p a b -> p (a b)")[:, 0:T].rearrange("p (c t) -> p c t", c=NC)
                f = full[:, g % 2, :]
                nc.vector.scalar_tensor_tensor(out=f.rearrange("p (c t) -> p c t", c=NC), in0=mixed, scalar=nw[:, g:g + 1],
                                               in1=bsb[:, g, :].unsqueeze(1).broadcast_to([P, NC, P]),
                                               op0=ALU.mult, op1=ALU.add).then_inc(s_m, 1)
                dve.wait_ge(s_m, 3 * g + 1)
                nc.vector.tensor_tensor(f, f, ya[:, g, :], ALU.mult).then_inc(s_m, 2)
                dve.wait_ge(s_split, g + 1)
                nc.vector.tensor_tensor(ya_lo[:, g, :], f, ya_hi[:, g, :].bitcast(F32), ALU.subtract).then_inc(s_n, 1)
                dve.wait_ge(s_n, 2 + NC + g + 1)
    return ya_hi, ya_lo


def stage_branch_a(kit, io, scr, ht, ya):
    nc = kit.nc
    MG = kit.at(O_MG, KD, T)
    gate = kit.at(O_TMP, 2, T)
    w = Weights(kit, "a", lambda i: io["units"][8 + i])
    s_t0, s_gate, s_mg = kit.sem("a_tile0"), kit.sem("a_gate"), kit.sem("a_merged")
    with nc.Block() as block:
        @block.sync
        def _(sp):
            for i in range(8):
                w.load(sp, i)

        @block.tensor
        def _(pe):
            for i in range(8):
                w.ready(pe, i)
                for t in range(2):
                    j = i // 2
                    if i % 2 == 0 and j:
                        pe.wait_ge(s_mg, 2 * (j - 1) + t + 1)
                    if i % 2:
                        pe.wait_ge(s_gate, 2 * j + t + 1)
                    last = feature_tile(nc, w.parts(i, KD), t, ya if i % 2 else ht,
                                        lambda h: halves(kit, t)[:, h, :], KD)
                    if t == 0:
                        last.then_inc(s_t0, 1)
                last.then_inc(w.used, 1)

        @block.scalar
        def _(act):
            w.split_hi(act, 0)
            for i in range(8):
                if i + 1 < 8:
                    w.split_hi(act, i + 1)
                if i % 2 == 0:
                    for t in range(2):
                        act.wait_ge(s_t0 if t == 0 else w.used, i + 1)
                        if i:
                            act.wait_ge(s_mg, i - 2 + t + 1)
                        nc.scalar.activation(two(gate[:, t, :]), halves(kit, t), ACT.Sigmoid).then_inc(s_gate, 1)

        @block.vector
        def _(dve):
            w.split_lo(dve, 0)
            for i in range(8):
                if i + 1 < 8:
                    w.split_lo(dve, i + 1)
                if i % 2:
                    for t in range(2):
                        dve.wait_ge(s_t0 if t == 0 else w.used, i + 1)
                        nc.vector.tensor_tensor(two(MG[:, i - 1 + t, :]), halves(kit, t), two(gate[:, t, :]),
                                                ALU.mult).then_inc(s_mg, 1)


def stage_dt(kit, io):
    nc, ps = kit.nc, kit.ps
    raw, whi, wlo = kit.at(O_X, 512), kit.rnd(O_X + 512, 512), kit.rnd(O_X + 1024, 512)
    bias = kit.at(O_X + 1536, 1)[0:64]
    alog = kit.at(O_X + 1600, 64)
    dtT = kit.at(O_X + 1700, T)[0:64]
    x, e, r, sden, s, s2, q = (kit.at(O_X + 2400 + 320 * j, 320) for j in range(7))
    DT, A = kit.at(O_TMP + 4480, NC, 64), kit.at(O_TMP + 4800, NC, 64)
    ht = [kit.rnd(o, KD, T) for o in (O_H, O_H + 5120)]
    ident = kit.const("ident")
    s_in, s_hl, s_pe, s_act, s_dve = (kit.sem("d_" + x) for x in ("in", "split", "pe", "act", "dve"))
    with nc.Block() as block:
        @block.sync
        def _(sp):
            sp.dma_start(raw, io["w_dt"]).then_inc(s_in, 16)
            sp.dma_start(bias, io["dt_bias"]).then_inc(s_in, 16)
            sp.dma_start(alog, io["a_log"].partition_broadcast(P)).then_inc(s_in, 16)

        @block.scalar
        def _(act):
            act.wait_ge(s_in, 48)
            nc.scalar.activation(whi, raw, ACT.Copy).then_inc(s_hl, 1)
            act.wait_ge(s_pe, 1)
            nc.scalar.activation(dtT.rearrange("p (h n) -> p h n", h=2), ps[0:64, 0:2, 0:HALF], ACT.Identity,
                                 bias=bias).then_inc(s_act, 1)
            act.wait_ge(s_pe, 2)
            nc.scalar.activation(x, ps[:, 2, 0:320], ACT.Copy).then_inc(s_act, 1)
            nc.scalar.activation(e, ps[:, 2, 0:320], ACT.Abs).then_inc(s_act, 1)
            act.wait_ge(s_act, 3)
            nc.scalar.activation(e, e, ACT.Exp, scale=-1.0).then_inc(s_act, 1)
            nc.scalar.activation(alog, alog, ACT.Exp).then_inc(s_act, 1)

        @block.tensor
        def _(pe):
            pe.wait_ge(s_hl, 2)
            w = [v.rearrange("p (k n) -> p k n", k=KD) for v in (whi, wlo)]
            for h in range(2):
                last = split3(nc, ps[0:64, h, 0:HALF], [lambda k, v=v: v[:, k, :] for v in w],
                              [lambda k, v=v: v[:, k, h * HALF:(h + 1) * HALF] for v in ht], KD)
            last.then_inc(s_pe, 1)
            pe.wait_ge(s_act, 1)
            for c in range(NC):
                last = nc.tensor.transpose(ps[:, 2, c * 64:(c + 1) * 64], dtT[:, c * P:(c + 1) * P], ident[0:64, 0:64])
            last.then_inc(s_pe, 1)

        @block.vector
        def _(dve):
            ch = Chain(dve, s_dve)
            dve.wait_ge(s_hl, 1)
            nc.vector.tensor_tensor(wlo, raw, whi.bitcast(F32), ALU.subtract).then_inc(s_hl, 1)
            dve.wait_ge(s_act, 5)
            ch.step(nc.vector.tensor_scalar(r, x, 0.0, None, ALU.max))
            ch.step(nc.vector.tensor_scalar(sden, e, 2.0, None, ALU.add))
            ch.sync()
            ch.step(nc.vector.reciprocal(sden, sden))
            ch.sync()
            ch.step(nc.vector.tensor_tensor(s, e, sden, ALU.mult))
            ch.sync()
            ch.step(nc.vector.tensor_tensor(s2, s, s, ALU.mult))
            ch.sync()
            ch.step(nc.vector.tensor_scalar(q, s2, 1.0 / 17, None, ALU.mult))
            for n in range(15, 1, -2):
                ch.sync()
                ch.step(nc.vector.scalar_tensor_tensor(out=q, in0=q, scalar=1.0 / n, in1=s2, op0=ALU.add, op1=ALU.mult))
            ch.sync()
            ch.step(nc.vector.scalar_tensor_tensor(out=q, in0=q, scalar=1.0, in1=s, op0=ALU.add, op1=ALU.mult))
            ch.sync()
            dt = DT.rearrange("p c h -> p (c h)")
            ch.step(nc.vector.scalar_tensor_tensor(out=dt, in0=q, scalar=2.0, in1=r, op0=ALU.mult, op1=ALU.add))
            ch.sync()
            ch.step(nc.vector.scalar_tensor_tensor(out=A, in0=DT, scalar=-1.0,
                                                   in1=alog.unsqueeze(1).broadcast_to([P, NC, 64]),
                                                   op0=ALU.mult, op1=ALU.mult))


def stage_conv(kit, io):
    nc, ps = kit.nc, kit.ps
    nt = (INNER + 2 * G * P) // P
    n, W0 = nt // 2, 2 + T + 4
    pre, acc, post = kit.at(O_TMP, 2, W0), kit.at(O_TMP + 2 * W0, 2, W0 - 4), kit.at(O_TMP + 4 * W0 - 8, 2, T)
    cw, cb = kit.at(O_TMP + 4 * W0 + 1280, nt, TAPS), kit.at(O_TMP + 4 * W0 + 1400, nt)
    X, Bt = kit.at(O_X, NC, INNER), kit.at(O_BC + 5120, NC, G * P)
    BCT = kit.at(O_BC, 2 * G, T)
    ht = [kit.rnd(o, KD, T) for o in (O_H, O_H + 5120)]
    ident = kit.const("ident")
    w = Weights(kit, "c", lambda i: io["units"][16 + i])
    s_in, s_pad, s_t0 = kit.sem("c_in"), kit.sem("c_pad"), kit.sem("c_tile0")
    s_pre, s_cv, s_silu, s_tr, s_x = (kit.sem("c_" + x) for x in ("pre", "conv", "silu", "turned", "x"))
    turned = lambda tile: tile < 20
    dest = lambda tile: post[:, tile % 2, :] if tile < 16 else BCT[:, tile - 16, :]
    with nc.Block() as block:
        @block.sync
        def _(sp):
            sp.dma_start(cw, io["conv_w"].rearrange("p (t k) -> p t k", k=TAPS)).then_inc(s_in, 16)
            sp.dma_start(cb, io["conv_b"]).then_inc(s_in, 16)
            for i in range(n):
                w.load(sp, i)

        @block.tensor
        def _(pe):
            def turn(i):
                for t in range(2):
                    tile = 2 * i + t
                    if not turned(tile):
                        continue
                    pe.wait_ge(s_silu, 2 * tile + 2)
                    if tile >= 2:
                        pe.wait_ge(s_x, tile - 1)
                    for c in range(NC):
                        o = ps[:, 4 + 2 * t + c // 4, (c % 4) * P:(c % 4 + 1) * P]
                        last = nc.tensor.transpose(o, dest(tile)[:, c * P:(c + 1) * P], ident)
                    last.then_inc(s_tr, 1)

            for i in range(n):
                w.ready(pe, i)
                for t in range(2):
                    if i:
                        pe.wait_ge(s_pre, 3 * (2 * i + t - 1))
                    last = feature_tile(nc, w.parts(i, KD), t, ht, lambda h: halves(kit, t)[:, h, :], KD)
                    if t == 0:
                        last.then_inc(s_t0, 1)
                last.then_inc(w.used, 1)
                if i:
                    turn(i - 1)
            turn(n - 1)

        @block.scalar
        def _(act):
            act.wait_ge(s_in, 32)
            act.wait_ge(s_pad, 3)

            def take_turned(i):
                for t in range(2):
                    tile = 2 * i + t
                    if not turned(tile):
                        continue
                    act.wait_ge(s_tr, tile + 1)
                    src = ps[:, 4 + 2 * t:6 + 2 * t, :].rearrange("p a b -> p (a b)")[:, 0:T].rearrange("p (c n) -> p c n", c=NC)
                    d = X[:, :, tile * P:(tile + 1) * P] if tile < 16 else Bt[:, :, (tile - 16) * P:(tile - 15) * P]
                    nc.scalar.activation(d, src, ACT.Copy).then_inc(s_x, 1)

            w.split_hi(act, 0)
            for i in range(n):
                if i + 1 < n:
                    w.split_hi(act, i + 1)
                for t in range(2):
                    act.wait_ge(s_t0 if t == 0 else w.used, i + 1)
                    if i:
                        act.wait_ge(s_cv, TAPS * (2 * i + t - 1))
                    for a, b, o in ((0, P, 2), (P, HALF, 4)):
                        nc.scalar.activation(pre[:, t, a + o:b + o], ps[:, 2 * t, a:b], ACT.Copy).then_inc(s_pre, 1)
                    nc.scalar.activation(pre[:, t, HALF + 4:T + 4], ps[:, 2 * t + 1, 0:HALF], ACT.Copy).then_inc(s_pre, 1)
                if i:
                    take_turned(i - 1)
                for t in range(2):
                    tile = 2 * i + t
                    act.wait_ge(s_cv, TAPS * (tile + 1))
                    for a, b, o in ((0, P, 0), (P, T, 2)):
                        nc.scalar.activation(dest(tile)[:, a:b], acc[:, t, a + o:b + o], ACT.Silu,
                                             bias=cb[:, tile:tile + 1]).then_inc(s_silu, 1)
            take_turned(n - 1)

        @block.vector
        def _(dve):
            for a, b in ((0, 2), (P + 2, P + 4), (W0 - 2, W0)):
                nc.vector.memset(pre[:, :, a:b], 0.0).then_inc(s_pad, 1)
            dve.wait_ge(s_in, 32)
            dve.wait_ge(s_pad, 3)
            w.split_lo(dve, 0)
            for i in range(n):
                if i + 1 < n:
                    w.split_lo(dve, i + 1)
                for t in range(2):
                    tile = 2 * i + t
                    dve.wait_ge(s_pre, 3 * (tile + 1))
                    if i:
                        dve.wait_ge(s_silu, 2 * (tile - 1))
                    for k in range(TAPS):
                        src, tap = pre[:, t, k:k + W0 - 4], cw[:, tile, k:k + 1]
                        if k == 0:
                            nc.vector.tensor_scalar(acc[:, t, :], src, tap, None, ALU.mult).then_inc(s_cv, 1)
                        else:
                            dve.wait_ge(s_cv, TAPS * tile + k)
                            nc.vector.scalar_tensor_tensor(out=acc[:, t, :], in0=src, scalar=tap, in1=acc[:, t, :],
                                                           op0=ALU.mult, op1=ALU.add).then_inc(s_cv, 1)


def stage_gates(kit, io, scr):
    nc, ps = kit.nc, kit.ps
    zs = kit.at(O_TMP, NC, UC)
    gs = kit.at(O_TMP + NC * UC, 2, T)
    ht = [kit.rnd(o, KD, T) for o in (O_H, O_H + 5120)]
    w = Weights(kit, "z", lambda i: io["units"][28 + i])
    s_pe, s_silu, s_t0, s_sig = kit.sem("z_chunk"), kit.sem("z_silu"), kit.sem("z_tile0"), kit.sem("z_sigmoid")
    s_out = [kit.sem(f"z_stored{c}") for c in range(NC)]
    s_gout = [kit.sem(f"z_gate_stored{t}") for t in range(2)]
    nz, ng = 8, 4
    with nc.Block() as block:
        @block.sync
        def _(sp):
            for i in range(nz + ng):
                w.load(sp, i)

        @block.tensor
        def _(pe):
            for i in range(nz):
                w.ready(pe, i)
                for c in range(NC):
                    if i:
                        pe.wait_ge(s_silu, NC * (i - 1) + c + 1)
                    last = token_tile(nc, w.parts(i, KD), c, ht, ps[:, c, 0:UC])
                    if c < NC - 1:
                        last.then_inc(s_pe, 1)
                last.then_inc(w.used, 1)
            pe.wait_ge(s_silu, NC * nz)
            for i in range(nz, nz + ng):
                w.ready(pe, i)
                for t in range(2):
                    if i > nz:
                        pe.wait_ge(s_sig, 2 * (i - nz - 1) + t + 1)
                    last = feature_tile(nc, w.parts(i, KD), t, ht, lambda h: halves(kit, t)[:, h, :], KD)
                    if t == 0:
                        last.then_inc(s_t0, 1)
                last.then_inc(w.used, 1)

        @block.scalar
        def _(act):
            w.split_hi(act, 0)
            for i in range(nz):
                w.split_hi(act, i + 1)
                for c in range(NC):
                    act.wait_ge(s_pe if c < NC - 1 else w.used, (NC - 1) * i + c + 1 if c < NC - 1 else i + 1)
                    if i:
                        act.wait_ge(s_out[c], 16 * i)
                    nc.scalar.activation(zs[:, c, :], ps[:, c, 0:UC], ACT.Silu).then_inc(s_silu, 1)
            for i in range(nz, nz + ng):
                if i + 1 < nz + ng:
                    w.split_hi(act, i + 1)
                for t in range(2):
                    act.wait_ge(s_t0 if t == 0 else w.used, i + 1 - (nz if t == 0 else 0))
                    if i > nz:
                        act.wait_ge(s_gout[t], 16 * (i - nz))
                    nc.scalar.activation(two(gs[:, t, :]), halves(kit, t), ACT.Sigmoid).then_inc(s_sig, 1)

        @block.vector
        def _(dve):
            for i in range(nz + ng):
                w.split_lo(dve, i)

        @block.gpsimd
        def _(pool):
            for i in range(nz):
                for c in range(NC):
                    pool.wait_ge(s_silu, NC * i + c + 1)
                    pool.dma_start(scr["z"][c * P:(c + 1) * P, i * UC:(i + 1) * UC], zs[:, c, :]).then_inc(s_out[c], 16)
            for i in range(ng):
                for t in range(2):
                    pool.wait_ge(s_sig, 2 * i + t + 1)
                    pool.dma_start(scr["gb"][2 * i + t], gs[:, t, :]).then_inc(s_gout[t], 16)
            for c in range(NC):
                pool.wait_ge(s_out[c], 16 * nz)
            for t in range(2):
                pool.wait_ge(s_gout[t], 16 * ng)


def stage_ssd(kit, io, out):
    nc, ps = kit.nc, kit.ps
    hF, hB0 = kit.at(O_H, 4, INNER), kit.at(O_H + 4 * INNER, INNER)
    hB1 = kit.at(O_HL, INNER)
    R = kit.at(O_HL + 2048, 4, 512)
    GX, TT, M, XD = (kit.at(O_HL + 4096 + 1024 * j, 2, 512) for j in range(4))
    EX = kit.at(O_TMP, 6, NC, 32)
    DD = kit.at(O_TMP + 960, 2, NC, 32)
    CB = kit.at(O_TMP + 1280, 2, 2, P)
    OF = kit.at(O_TMP + 1792, 2, 2, 256)
    YK = kit.at(O_TMP + 2816, 2, 256)
    DSK = kit.at(O_TMP + 3328, 32)
    SO = kit.at(O_TMP + 3360, 2, 512)
    HT_ = kit.at(O_RAW, 2, 512)
    V1 = kit.at(O_RAW + 1024, 2, 256)
    DT, A = kit.at(O_TMP + 4480, NC, 64), kit.at(O_TMP + 4800, NC, 64)
    X, Bt = kit.at(O_X, NC, INNER), kit.at(O_BC + 5120, NC, G * P)
    BT, CT = kit.at(O_BC, G, T), kit.at(O_BC + 2560, G, T)
    sums = [(kit.const(m), d) for m, d in (("le", 0), ("gt", 0), ("one", 0), ("ge", 1), ("lt", 1), ("one", 1))]
    le, ge, gt, lt = (kit.const(m) for m in ("le", "ge", "gt", "lt"))

    names = ("in", "ex", "exa", "dd", "r", "seg", "g", "a1", "cbp", "cb", "t", "m", "y", "yk", "ev", "xd", "stp",
             "st", "cst")
    (s_in, s_ex, s_exa, s_dd, s_r, s_seg, s_g, s_a1, s_cbp, s_cb, s_t, s_m, s_y, s_yk, s_ev, s_xd, s_stp, s_st,
     s_cst) = (kit.sem("s_" + x) for x in names)
    s_so = [kit.sem(f"s_state_stored{j}") for j in range(2)]

    chunks = [4, 3, 2, 1, 0]
    subs = [(c, g, q) for c in chunks for g in range(G) for q in range(2)]
    NS, NL = len(subs), 32
    ev = lambda j: 6 * j if j <= NL else 6 * NL + 2 * (j - NL)
    ctx_states = [(d, 0, g) for d in range(2) for g in range(G)]
    fwd = [(0, c, g) for c in (1, 2, 3) for g in range(G)]
    bwd = [(1, c, g) for c in (4, 3, 2) for g in range(G)]
    states = ctx_states + fwd + bwd
    NX, NF = len(ctx_states), len(ctx_states) + len(fwd)
    bank_of = lambda x: 7 if x >= NF or x % 2 else 6
    hb = lambda c: (hB0, hB1)[(4 - c) % 2]
    x_at = {}
    for x, (d, c, g) in enumerate(bwd):
        x_at[subs.index((c, g, 0))] = NF + x
    cols = lambda g: slice(g * GW, (g + 1) * GW)
    heads4 = lambda g, q: slice(g * HPG + 4 * q, g * HPG + 4 * q + 4)
    byhead = lambda v, n: v.rearrange("p (h n) -> p h n", h=n)

    with nc.Block() as block:
        @block.sync
        def _(sp):
            sp.dma_start(hF[:, 0, :], io["state_t"][0]).then_inc(s_in, 16)
            sp.dma_start(hB0, io["state_t"][1]).then_inc(s_in, 16)
            sp.dma_start(DSK, io["d_skip"].partition_broadcast(P)).then_inc(s_in, 16)
            for x, (d, c, g) in enumerate(ctx_states):
                sp.wait_ge(s_cst, x + 1)
                sp.dma_start(out["state"][d, cols(g), :].rearrange("(q p) n -> p q n", p=P),
                             SO[:, x % 2, :].rearrange("p (q n) -> p q n", q=4)).then_inc(s_so[x % 2], 16)
            for j in range(2):
                sp.wait_ge(s_so[j], 16 * NX // 2)

        @block.gpsimd
        def _(pool):
            def decays(j):
                c, g, q = subs[j]
                if j >= 2:
                    pool.wait_ge(s_seg, j - 1)
                for d, mask in ((0, le), (1, ge)):
                    hs = heads4(g, q)
                    av = A[:, c, 32 * d + hs.start:32 * d + hs.stop]
                    nc.gpsimd.tensor_tensor(byhead(R[:, 2 * d + j % 2, :], 4), av.unsqueeze(2).broadcast_to([P, 4, P]),
                                            mask.unsqueeze(1).broadcast_to([P, 4, P]), ALU.mult).then_inc(s_r, 1)

            def weigh(x):
                d, c, g = states[x]
                if x >= 2:
                    pool.wait_ge(s_stp, x - 1)
                nc.gpsimd.tensor_tensor(byhead(XD[:, x % 2, :], HPG), byhead(X[:, c, cols(g)], HPG),
                                        DD[:, d, c, g * HPG:(g + 1) * HPG].unsqueeze(2).broadcast_to([P, HPG, HD]),
                                        ALU.mult).then_inc(s_xd, 1)

            pool.wait_ge(s_dd, 2)
            for x in range(NF):
                weigh(x)
            decays(0)
            decays(1)
            pool.wait_ge(s_in, 48)
            for j, (c, g, q) in enumerate(subs):
                if j + 2 < NS:
                    decays(j + 2)
                if j in x_at:
                    weigh(x_at[j])
                if j >= 2:
                    pool.wait_ge(s_ev, ev(j - 1))
                nc.gpsimd.tensor_tensor(byhead(YK[:, j % 2, :], 4), byhead(X[:, c, g * GW + q * 256:g * GW + (q + 1) * 256], 4),
                                        DSK[:, heads4(g, q)].unsqueeze(2).broadcast_to([P, 4, HD]),
                                        ALU.mult).then_inc(s_yk, 1)

        @block.tensor
        def _(pe):
            def state(x):
                d, c, g = states[x]
                pe.wait_ge(s_xd, x + 1)
                if x >= NF:
                    pe.wait_ge(s_st, x - NX)
                elif x >= NX + 2:
                    pe.wait_ge(s_st, x - NX - 1)
                elif x >= 2:
                    pe.wait_ge(s_cst, x - 1)
                b, bt = bank_of(x), Bt[:, c, g * P:(g + 1) * P]
                if x < NX:
                    for q in range(4):
                        last = nc.tensor.matmul(ps[:, b, q * P:(q + 1) * P], XD[:, x % 2, q * P:(q + 1) * P], bt,
                                                start=True, stop=True)
                else:
                    last = nc.tensor.matmul(ps[:, b, :], bt, XD[:, x % 2, :], start=True, stop=True)
                last.then_inc(s_stp, 1)

            def prepare(j):
                c, g, q = subs[j]
                pe.wait_ge(s_r, 2 * j + 2)
                if j >= 2:
                    pe.wait_ge(s_g, j - 1)
                nc.tensor.matmul(ps[:, j % 2, :], gt, R[:, j % 2, :], start=True, stop=False)
                nc.tensor.matmul(ps[:, j % 2, :], lt, R[:, 2 + j % 2, :], start=False, stop=True).then_inc(s_seg, 1)
                if q == 0:
                    gi = j // 2
                    if gi >= 2:
                        pe.wait_ge(s_cb, 2 * (gi - 1))
                    nc.tensor.matmul(ps[:, 4, (gi % 2) * P:(gi % 2 + 1) * P], BT[:, g, c * P:(c + 1) * P],
                                     CT[:, g, c * P:(c + 1) * P], start=True, stop=True).then_inc(s_cbp, 1)

            for n, (mask, d) in enumerate(sums):
                o = ps[:, n // 3, (n % 3) * 160:(n % 3 + 1) * 160]
                last = nc.tensor.matmul(o, mask, A[:, :, 32 * d:32 * d + 32], start=True, stop=True)
            last.then_inc(s_ex, 1)
            for x in range(NF):
                state(x)
            pe.wait_ge(s_exa, 2)
            prepare(0)
            for j, (c, g, q) in enumerate(subs):
                if j + 1 < NS:
                    prepare(j + 1)
                if j in x_at:
                    state(x_at[j])
                if j >= 2:
                    pe.wait_ge(s_ev, ev(j - 1))
                elif j == 0:
                    pe.wait_ge(s_in, 48)
                    pe.wait_ge(s_st, NF - NX)
                if c:
                    pe.wait_ge(s_st, NF - NX + 4 * (4 - c))
                    ct = CT[:, g, c * P:(c + 1) * P]
                    w4 = slice(g * GW + q * 256, g * GW + (q + 1) * 256)
                    nc.tensor.matmul(ps[:, 5 + j % 2, 0:256], ct, hF[:, c - 1, w4], start=True, stop=True)
                    nc.tensor.matmul(ps[:, 5 + j % 2, 256:512], ct, hb(c)[:, w4], start=True, stop=True)
                pe.wait_ge(s_m, j + 1)
                for h in range(4):
                    x0 = g * GW + q * 256 + (h // 2) * P
                    last = nc.tensor.matmul(ps[:, 2 + j % 2, h * P:(h + 1) * P], M[:, j % 2, h * P:(h + 1) * P],
                                            X[:, c, x0:x0 + P], start=True, stop=True)
                last.then_inc(s_y, 1)

        @block.scalar
        def _(act):
            act.wait_ge(s_ex, 1)
            for n in range(2):
                nc.scalar.activation(EX[:, 3 * n:3 * n + 3, :, :].rearrange("p a b c -> p (a b c)"), ps[:, n, 0:480],
                                     ACT.Exp).then_inc(s_exa, 1)
            for x in range(NX):
                act.wait_ge(s_stp, x + 1)
                if x >= 2:
                    act.wait_ge(s_so[x % 2], 16 * (x // 2))
                nc.scalar.activation(SO[:, x % 2, :], ps[:, bank_of(x), :], ACT.Copy).then_inc(s_cst, 1)
            for j, (c, g, q) in enumerate(subs):
                act.wait_ge(s_seg, j + 1)
                if j >= 2:
                    act.wait_ge(s_m, j - 1)
                nc.scalar.activation(GX[:, j % 2, :], ps[:, j % 2, :], ACT.Exp).then_inc(s_g, 1)
                act.wait_ge(s_cb, 2 * (j // 2) + 2)
                for h in range(4):
                    dt = DT[:, c, g * HPG + 4 * q + h:g * HPG + 4 * q + h + 1]
                    nc.scalar.activation(TT[:, j % 2, h * P:(h + 1) * P], CB[:, (j // 2) % 2, 0, :], ACT.Copy,
                                         scale=dt).then_inc(s_a1, 1)

        @block.vector
        def _(dve):
            dve.wait_ge(s_exa, 2)
            for d in range(2):
                nc.vector.tensor_tensor(DD[:, d, :, :], DT[:, :, 32 * d:32 * d + 32], EX[:, 3 * d + 1, :, :],
                                        ALU.mult).then_inc(s_dd, 1)

            def carry(x):
                d, c, g = states[x]
                if d == 0:
                    src, dst = hF[:, c - 1, cols(g)], hF[:, c, cols(g)]
                else:
                    src, dst = hb(c)[:, cols(g)], hb(c - 1)[:, cols(g)]
                    dve.wait_ge(s_y, 8 * (4 - c))
                dec = EX[:, 3 * d + 2, c, g * HPG:(g + 1) * HPG].unsqueeze(2).broadcast_to([P, HPG, HD])
                n = x - NX
                nc.vector.tensor_tensor(byhead(HT_[:, x % 2, :], HPG), byhead(src, HPG), dec, ALU.mult).then_inc(s_dd, 1)
                dve.wait_ge(s_dd, 3 + n)
                dve.wait_ge(s_stp, x + 1)
                nc.vector.tensor_tensor(dst, HT_[:, x % 2, :], ps[:, bank_of(x), :], ALU.add).then_inc(s_st, 1)

            dve.wait_ge(s_in, 48)
            for x in range(NX, NF):
                if x >= NX + 4:
                    dve.wait_ge(s_st, x - NX - 3)
                carry(x)

            def masks(gi):
                dve.wait_ge(s_cbp, gi + 1)
                src = ps[:, 4, (gi % 2) * P:(gi % 2 + 1) * P]
                if gi >= 2:
                    dve.wait_ge(s_a1, 8 * (gi - 1))
                    dve.wait_ge(s_t, 8 * (gi - 1))
                nc.vector.tensor_tensor(CB[:, gi % 2, 0, :], src, le, ALU.mult).then_inc(s_cb, 1)
                nc.vector.tensor_tensor(CB[:, gi % 2, 1, :], src, ge, ALU.mult).then_inc(s_cb, 1)

            def take_y(j):
                c, g, q = subs[j]
                w4 = slice(g * GW + q * 256, g * GW + (q + 1) * 256)
                v = ps[:, 2 + j % 2, :].rearrange("p (a n) -> p a n", a=2)
                n = ev(j)
                dve.wait_ge(s_y, j + 1)
                dve.wait_ge(s_yk, j + 1)
                dst = V1[:, j % 2, :] if c else X[:, c, w4]
                if c:
                    for d in range(2):
                        nc.vector.tensor_tensor(byhead(OF[:, j % 2, d, :], 4), byhead(ps[:, 5 + j % 2, 256 * d:256 * d + 256], 4),
                                                EX[:, 3 * d, c, heads4(g, q)].unsqueeze(2).broadcast_to([P, 4, HD]),
                                                ALU.mult).then_inc(s_ev, 1)
                for e in range(2):
                    o = e * (P + HD)
                    nc.vector.tensor_tensor(dst.rearrange("p (a e n) -> p a e n", a=2, e=2)[:, :, e, :], v[:, :, o:o + HD],
                                            YK[:, j % 2, :].rearrange("p (a e n) -> p a e n", a=2, e=2)[:, :, e, :],
                                            ALU.add).then_inc(s_ev, 1)
                if c:
                    dve.wait_ge(s_ev, n + 4)
                    nc.vector.tensor_tensor(dst, dst, OF[:, j % 2, 0, :], ALU.add).then_inc(s_ev, 1)
                    dve.wait_ge(s_ev, n + 5)
                    nc.vector.tensor_tensor(X[:, c, w4], dst, OF[:, j % 2, 1, :], ALU.add).then_inc(s_ev, 1)

            masks(0)
            for j, (c, g, q) in enumerate(subs):
                if j % 2 and j + 1 < NS:
                    masks((j + 1) // 2)
                dve.wait_ge(s_a1, 4 * j + 4)
                dve.wait_ge(s_cb, 2 * (j // 2) + 2)
                for h in range(4):
                    dt = DT[:, c, 32 + g * HPG + 4 * q + h:32 + g * HPG + 4 * q + h + 1]
                    tt = TT[:, j % 2, h * P:(h + 1) * P]
                    nc.vector.scalar_tensor_tensor(out=tt, in0=CB[:, (j // 2) % 2, 1, :], scalar=dt, in1=tt,
                                                   op0=ALU.mult, op1=ALU.add).then_inc(s_t, 1)
                dve.wait_ge(s_t, 4 * j + 4)
                dve.wait_ge(s_g, j + 1)
                if j >= 2:
                    dve.wait_ge(s_y, j - 1)
                nc.vector.tensor_tensor(M[:, j % 2, :], TT[:, j % 2, :], GX[:, j % 2, :], ALU.mult).then_inc(s_m, 1)
                if j:
                    take_y(j - 1)
                if j in x_at:
                    x = x_at[j]
                    dve.wait_ge(s_st, x - NX - 3)
                    carry(x)
            take_y(NS - 1)


def stage_norm_y(kit, io, scr):
    nc, ps = kit.nc, kit.ps
    X = kit.at(O_X, NC, INNER)
    Z = kit.at(O_RAW, 2, INNER)
    hi, lo = kit.rnd(O_H, KI, T), kit.rnd(O_BC, KI, T)
    nw, ssq, rr = kit.at(O_TMP + 2560, KI), kit.at(O_TMP + 2580, NC * G), kit.at(O_TMP + 2600, NC * G)
    sc, cond = kit.at(O_TMP + 2624, 16), kit.at(O_TMP + 2640, 16)
    sq = kit.at(O_TMP + 2656, GW)
    row, brow = kit.at(O_TMP + 3168, 2, 512), kit.at(O_TMP + 4192, 512)
    WM = kit.at(O_HL, 2, 4096)
    ident = kit.const("ident")
    NM = 8
    (s_in, s_y, s_ms, s_r, s_sq, s_tr, s_hi, s_lo, s_mod, s_modr, s_b) = (
        kit.sem("n_" + x) for x in ("in", "y", "mean", "root", "squares", "turned", "hi", "lo", "mod", "mod_row", "bias"))
    s_z = [kit.sem(f"n_z{j}") for j in range(2)]
    s_w = [kit.sem(f"n_w{j}") for j in range(2)]
    s_mo = [kit.sem(f"n_mod_stored{j}") for j in range(2)]
    mods = [[0, 1], [2, 3], [4, 5], [6, 7], []]

    with nc.Block() as block:
        @block.sync
        def _(sp):
            sp.dma_start(nw, io["ssd_nw"]).then_inc(s_in, 16)
            sp.dma_start(cond, io["cond"]).then_inc(s_in, 16)
            for c in range(2):
                sp.dma_start(Z[:, c, :], scr["z"][c * P:(c + 1) * P, :]).then_inc(s_z[c], 16)
            for m in range(NM):
                if m >= 2:
                    sp.wait_ge(s_mod, m - 1)
                sp.dma_start(WM[:, m % 2, :], io["w_mod"][4 + m]).then_inc(s_w[m % 2], 16)
                if m % 2 == 0 and m // 2 + 2 < NC:
                    c = m // 2 + 2
                    sp.wait_ge(s_y, c - 1)
                    sp.dma_start(Z[:, c % 2, :], scr["z"][c * P:(c + 1) * P, :]).then_inc(s_z[c % 2], 16)

        @block.gpsimd
        def _(pool):
            for m in range(NM):
                if m:
                    pool.wait_ge(s_modr, m)
                pool.dma_start(brow[0:2, :], io["b_mod"][:, 2048 + 512 * m:2560 + 512 * m].partition_broadcast(2)).then_inc(s_b, 16)
                pool.wait_ge(s_modr, m + 1)
                pool.dma_start(scr["mod"][:, 512 * m:512 * (m + 1)], row[0:2, m % 2, :]).then_inc(s_mo[m % 2], 16)
            for j in range(2):
                pool.wait_ge(s_mo[j], 16 * NM // 2)

        @block.tensor
        def _(pe):
            pe.wait_ge(s_sq, 1)
            for c in range(NC):
                for m in mods[c]:
                    pe.wait_ge(s_w[m % 2], 16 * (m // 2 + 1))
                    if m >= 2:
                        pe.wait_ge(s_modr, m - 1)
                    for k in range(KD):
                        last = nc.tensor.matmul(ps[0:2, 4 + m % 2, :], sc.rearrange("p (k s) -> p k s", s=2)[:, k, :],
                                                WM[:, m % 2, k * 512:(k + 1) * 512], start=(k == 0), stop=(k == KD - 1))
                    last.then_inc(s_mod, 1)
                pe.wait_ge(s_r, NC * 0 + 4 * (c + 1))
                for g in range(G):
                    if c:
                        pe.wait_ge(s_lo, 4 * (G * (c - 1) + g + 1))
                    for q in range(4):
                        k = 4 * g + q
                        last = nc.tensor.transpose(ps[:, g, q * P:(q + 1) * P], X[:, c, k * P:(k + 1) * P], ident)
                    last.then_inc(s_tr, 1)

        @block.scalar
        def _(act):
            act.wait_ge(s_in, 32)
            nc.scalar.activation(sc, cond, ACT.Silu).then_inc(s_sq, 1)
            n = 1
            for c in range(NC):
                act.wait_ge(s_y, c + 1)
                for g in range(G):
                    if n > 1:
                        act.wait_ge(s_sq, n)
                    nc.scalar.activation(sq, X[:, c, g * GW:(g + 1) * GW], ACT.Square,
                                         accum_out=ssq[:, c * G + g:c * G + g + 1]).then_inc(s_sq, 1)
                    n += 1
                act.wait_ge(s_ms, 2 * c + 2)
                nc.scalar.activation(rr[:, c * G:(c + 1) * G], rr[:, c * G:(c + 1) * G], ACT.Sqrt).then_inc(s_sq, 1)
                n += 1
                for g in range(G):
                    act.wait_ge(s_tr, G * c + g + 1)
                    for q in range(4):
                        k = 4 * g + q
                        nc.scalar.activation(hi[:, k, c * P:(c + 1) * P], ps[:, g, q * P:(q + 1) * P],
                                             ACT.Copy, scale=nw[:, k:k + 1]).then_inc(s_hi, 1)

        @block.vector
        def _(dve):
            def gated(c):
                dve.wait_ge(s_z[c % 2], 16 * (c // 2 + 1))
                nc.vector.tensor_tensor(X[:, c, :], X[:, c, :], Z[:, c % 2, :], ALU.mult).then_inc(s_y, 1)

            def modulation_row(m):
                dve.wait_ge(s_mod, m + 1)
                dve.wait_ge(s_b, 16 * (m + 1))
                if m >= 2:
                    dve.wait_ge(s_mo[m % 2], 16 * (m // 2))
                nc.vector.tensor_tensor(row[0:2, m % 2, :], ps[0:2, 4 + m % 2, :], brow[0:2, :], ALU.add).then_inc(s_modr, 1)

            gated(0)
            for c in range(NC):
                dve.wait_ge(s_sq, 1 + 5 * c + 4)
                dve.wait_ge(s_y, c + 1)
                sl = slice(c * G, (c + 1) * G)
                nc.vector.tensor_scalar(ssq[:, sl], ssq[:, sl], 1.0 / GW, EPS, ALU.mult, ALU.add).then_inc(s_ms, 1)
                dve.wait_ge(s_ms, 2 * c + 1)
                nc.vector.reciprocal(rr[:, sl], ssq[:, sl]).then_inc(s_ms, 1)
                dve.wait_ge(s_sq, 1 + 5 * c + 5)
                for g in range(G):
                    v = X[:, c, g * GW:(g + 1) * GW]
                    nc.vector.tensor_scalar(v, v, rr[:, c * G + g:c * G + g + 1], None, ALU.mult).then_inc(s_r, 1)
                if c + 1 < NC:
                    gated(c + 1)
                for m in mods[c]:
                    modulation_row(m)
                for k in range(KI):
                    dve.wait_ge(s_hi, KI * c + 4 * (k // 4) + 4)
                    src, g, q = slice(c * P, (c + 1) * P), k // 4, k % 4
                    nc.vector.scalar_tensor_tensor(out=lo[:, k, src], in0=ps[:, g, q * P:(q + 1) * P],
                                                   scalar=nw[:, k:k + 1], in1=hi[:, k, src].bitcast(F32),
                                                   op0=ALU.mult, op1=ALU.subtract).then_inc(s_lo, 1)


def stage_branch_b(kit, io, scr):
    nc, ps = kit.nc, kit.ps
    y = [kit.rnd(o, KI, T) for o in (O_H, O_BC)]
    MG = kit.at(O_MG, KD, T)
    hi, lo = kit.rnd(O_X, KD, T), kit.rnd(O_X + 5120, KD, T)
    gate, v = kit.at(O_TMP + 2560, 2, T), kit.at(O_TMP + 3840, 2, T)
    w = Weights(kit, "b", lambda i: io["units"][40 + i])
    s_g = [kit.sem(f"b_gate{j}") for j in range(2)]
    s_v, s_hi, s_lo = kit.sem("b_merged"), kit.sem("b_hi"), kit.sem("b_lo")
    with nc.Block() as block:
        @block.sync
        def _(sp):
            for i in range(8):
                w.load(sp, i)
                if i >= 2:
                    sp.wait_ge(s_v, 2 * (i - 2) + 1)
                sp.dma_start(gate[:, i % 2, :], scr["gb"][i]).then_inc(s_g[i % 2], 16)

        @block.tensor
        def _(pe):
            for i in range(8):
                w.ready(pe, i)
                if i >= 2:
                    pe.wait_ge(s_v, 2 * (i - 2) + 1)
                feature_tile(nc, w.parts(i, KI), 0, y, lambda h: halves(kit, i % 2)[:, h, :], KI).then_inc(w.used, 1)

        @block.scalar
        def _(act):
            w.split_hi(act, 0)
            for i in range(8):
                if i + 1 < 8:
                    w.split_hi(act, i + 1)
                act.wait_ge(s_v, 2 * i + 2)
                nc.scalar.activation(hi[:, i, :], v[:, i % 2, :], ACT.Copy).then_inc(s_hi, 1)

        @block.vector
        def _(dve):
            w.split_lo(dve, 0)
            for i in range(8):
                if i + 1 < 8:
                    w.split_lo(dve, i + 1)
                dve.wait_ge(w.used, i + 1)
                dve.wait_ge(s_g[i % 2], 16 * (i // 2 + 1))
                nc.vector.tensor_tensor(two(v[:, i % 2, :]), halves(kit, i % 2), two(gate[:, i % 2, :]), ALU.mult).then_inc(s_v, 1)
                dve.wait_ge(s_v, 2 * i + 1)
                nc.vector.tensor_tensor(v[:, i % 2, :], v[:, i % 2, :], MG[:, i, :], ALU.add).then_inc(s_v, 1)
                dve.wait_ge(s_hi, i + 1)
                nc.vector.tensor_tensor(lo[:, i, :], v[:, i % 2, :], hi[:, i, :].bitcast(F32), ALU.subtract).then_inc(s_lo, 1)
                dve.wait_ge(s_lo, i + 1)


T_G2, T_FN, T_RT = O_TMP, O_TMP + 2048, O_TMP + 3072


class Routing:

    def __init__(self, kit):
        self.slot = [kit.at(T_RT + 8 * k, NC).bitcast(U32) for k in range(2)]
        self.weight = kit.at(T_RT + 16, 2, NC)
        self.table = kit.at(T_RT + 26, NMB + 1)[0:1].bitcast(I32)
        self.work = T_RT + 64


def stage_out(kit, io, scr):
    nc, ps = kit.nc, kit.ps
    x2, h2 = kit.at(O_H, NC, D), kit.at(O_H + 5120, NC, D)
    merged = [kit.rnd(o, KD, T) for o in (O_X, O_X + 5120)]
    G1, S2, A2, N2 = kit.at(O_BC, 2, D), kit.at(O_BC + 2048, 2, D), kit.at(O_BC + 4096, 2, D), kit.at(O_BC + 6144, D)
    G2, FN = kit.at(T_G2, 2, D), kit.at(T_FN, D)
    hT = kit.at(O_MG, 2, KD, P)
    rw = kit.at(O_MG + 2048, KD, NE)
    sq = kit.at(O_MG + 2176, D)
    prod = kit.at(O_MG + 3200, 2, UC)
    ssq, rr = kit.at(O_MG + 3712, NC), kit.at(O_MG + 3720, NC)
    score = kit.at(O_MG + 3728, NC, NE)
    ident = kit.const("ident")
    w = Weights(kit, "o", lambda i: io["units"][48 + i])
    (s_in, s_x, s_pe, s_x2, s_p, s_a2, s_sq, s_rt, s_ms, s_h2, s_tr, s_ht, s_rr, s_sc) = (
        kit.sem("o_" + v) for v in ("in", "x", "chunk", "x2", "product", "scale", "squares", "root", "mean", "h2",
                                    "turned", "ht", "router", "scores"))
    with nc.Block() as block:
        @block.sync
        def _(sp):
            sp.dma_start(x2, scr["xp"].rearrange("(c p) d -> p c d", p=P)).then_inc(s_x, 16)
            for i in range(2):
                w.load(sp, i)
            for q, dst in enumerate((G1, S2, A2, G2)):
                for st in range(2):
                    sp.dma_start(dst[:, st, :], scr["mod"][st:st + 1, q * D:(q + 1) * D].partition_broadcast(P)).then_inc(s_in, 16)
            sp.dma_start(N2, io["norm2"].partition_broadcast(P)).then_inc(s_in, 16)
            sp.dma_start(FN, io["fnorm"].partition_broadcast(P)).then_inc(s_in, 16)
            sp.dma_start(rw, io["router_w"].rearrange("p (k e) -> p k e", k=KD)).then_inc(s_in, 16)
            for i in range(2, 4):
                w.load(sp, i)

        @block.tensor
        def _(pe):
            for i in range(4):
                w.ready(pe, i)
                for c in range(NC):
                    if i:
                        pe.wait_ge(s_p, NC * (i - 1) + c + 1)
                    last = token_tile(nc, w.parts(i, KD), c, merged, ps[:, c, 0:UC])
                    if c < NC - 1:
                        last.then_inc(s_pe, 1)
                last.then_inc(w.used, 1)

            def route(c):
                for k in range(KD):
                    last = nc.tensor.matmul(ps[:, 7, c * NE:(c + 1) * NE], hT[:, c % 2, k, :], rw[:, k, :],
                                            start=(k == 0), stop=(k == KD - 1))
                last.then_inc(s_rr, 1)

            for c in range(NC):
                pe.wait_ge(s_h2, 2 * c + 2)
                if c:
                    pe.wait_ge(s_ht, c)
                else:
                    pe.wait_ge(s_in, 176)
                for k in range(KD):
                    last = nc.tensor.transpose(ps[:, 5 + k // 4, (k % 4) * P:(k % 4 + 1) * P], h2[:, c, k * P:(k + 1) * P], ident)
                last.then_inc(s_tr, 1)
                pe.wait_ge(s_ht, c + 1)
                route(c)

        @block.scalar
        def _(act):
            w.split_hi(act, 0)
            for i in range(3):
                w.split_hi(act, i + 1)
            for c in range(NC):
                act.wait_ge(s_x2, NC * 3 + c + 1)
                if c:
                    act.wait_ge(s_sq, c)
                nc.scalar.activation(sq, x2[:, c, :], ACT.Square, accum_out=ssq[:, c:c + 1]).then_inc(s_sq, 1)
                act.wait_ge(s_ms, 2 * c + 2)
                nc.scalar.activation(rr[:, c:c + 1], rr[:, c:c + 1], ACT.Sqrt).then_inc(s_rt, 1)
                act.wait_ge(s_tr, c + 1)
                if c >= 2:
                    act.wait_ge(s_rr, c - 1)
                nc.scalar.activation(hT[:, c % 2, :, :].rearrange("p k n -> p (k n)"),
                                     ps[:, 5:7, :].rearrange("p a b -> p (a b)"), ACT.Copy).then_inc(s_ht, 1)
            act.wait_ge(s_rr, NC)
            nc.scalar.activation(score.rearrange("p c e -> p (c e)"), ps[:, 7, 0:NC * NE], ACT.Sigmoid).then_inc(s_sc, 1)

        @block.vector
        def _(dve):
            w.split_lo(dve, 0)
            w.split_lo(dve, 1)
            dve.wait_ge(s_in, 176)
            dve.wait_ge(s_x, 16)
            for st in range(2):
                nc.vector.scalar_tensor_tensor(out=A2[:, st, :], in0=A2[:, st, :], scalar=1.0, in1=N2,
                                               op0=ALU.add, op1=ALU.mult).then_inc(s_a2, 1)
            for i in range(4):
                if i and i + 1 < 4:
                    w.split_lo(dve, i + 1)
                cols = slice(i * UC, (i + 1) * UC)
                for c in range(NC):
                    n = NC * i + c
                    if c < NC - 1:
                        dve.wait_ge(s_pe, (NC - 1) * i + c + 1)
                    else:
                        dve.wait_ge(w.used, i + 1)
                    nc.vector.tensor_tensor(prod[:, n % 2, :], ps[:, c, 0:UC], G1[:, min(c, 1), cols], ALU.mult).then_inc(s_p, 1)
                    dve.wait_ge(s_p, n + 1)
                    nc.vector.tensor_tensor(x2[:, c, cols], x2[:, c, cols], prod[:, n % 2, :], ALU.add).then_inc(s_x2, 1)
            for c in range(NC):
                st = min(c, 1)
                dve.wait_ge(s_sq, c + 1)
                nc.vector.tensor_scalar(ssq[:, c:c + 1], ssq[:, c:c + 1], 1.0 / D, EPS, ALU.mult, ALU.add).then_inc(s_ms, 1)
                dve.wait_ge(s_ms, 2 * c + 1)
                nc.vector.reciprocal(rr[:, c:c + 1], ssq[:, c:c + 1]).then_inc(s_ms, 1)
                dve.wait_ge(s_rt, c + 1)
                dve.wait_ge(s_a2, 2)
                nc.vector.scalar_tensor_tensor(out=h2[:, c, :], in0=x2[:, c, :], scalar=rr[:, c:c + 1], in1=A2[:, st, :],
                                               op0=ALU.mult, op1=ALU.mult).then_inc(s_h2, 1)
                dve.wait_ge(s_h2, 2 * c + 1)
                nc.vector.tensor_tensor(h2[:, c, :], h2[:, c, :], S2[:, st, :], ALU.add).then_inc(s_h2, 1)


def stage_route(kit, io, scr):
    nc, ps = kit.nc, kit.ps
    r = Routing(kit)
    h2 = kit.at(O_H + 5120, NC, D)
    score = kit.at(O_MG + 3728, NC, NE)
    at = [r.work]

    def take(*dims):
        n = 1
        for d in dims:
            n *= d
        at[0] += n
        return kit.at(at[0] - n, *dims)

    sel, selm, m1, m2, tmp, slot = (take(NC, NE) for _ in range(6))
    q20 = [take(NC * NG) for _ in range(7)]
    five, gmax = take(NC), take(NC)
    bias = take(NE)
    cnt, ext, pre, ca, cb = (take(NE) for _ in range(5))
    over = take(10, NE)
    tabf = take(NMB + 1)
    w12 = r.weight
    sbf = take(NC * NE // 2).bitcast(BF16).rearrange("p (c e) -> p c e", c=NC)
    ltb, oneb = take(P // 2).bitcast(BF16), take(P // 2).bitcast(BF16)
    assert at[0] <= O_MG
    s_in, s_v, s_pe, s_ready, s_mask = kit.sem("r_in"), kit.sem("r_steps"), kit.sem("r_ranks"), kit.sem("r_slots"), kit.sem("r_chosen")
    s_sc = kit.sem("r_scattered")
    pri16, pri4, e128, thr = (kit.const(n, k) for n, k in (("pri16", NE), ("pri4", NG), ("e128", NE), ("thr", 5)))
    col = kit.const("col", 26)
    bc = lambda v, n: v.unsqueeze(2).broadcast_to([P, v.shape[1], n])
    over_c = lambda v: v.unsqueeze(1).broadcast_to([P, NC, v.shape[1]])

    with nc.Block() as block:
        @block.sync
        def _(sp):
            sp.dma_start(bias, io["router_b"].partition_broadcast(P)).then_inc(s_in, 16)

        @block.vector
        def _(dve):
            ch = Chain(dve, s_v)
            tt = nc.vector.tensor_tensor

            def do(ins):
                ch.step(ins)
                ch.sync()

            def first_of(out, values, pri, width):
                do(nc.vector.tensor_reduce(five, values, AX.X, ALU.max))
                do(tt(out, values, bc(five, width), ALU.is_equal))
                do(tt(out, out, over_c(pri), ALU.mult))
                do(nc.vector.tensor_reduce(gmax, out, AX.X, ALU.max))
                do(tt(out, out, bc(gmax, width), ALU.is_equal))

            do(nc.vector.tensor_copy(ltb, kit.const("lt")))
            do(nc.vector.tensor_copy(oneb, kit.const("one")))
            dve.wait_ge(s_in, 16)
            do(tt(sel, score, over_c(bias), ALU.add))
            v = sel.rearrange("p c (g e) -> p (c g) e", e=4)
            hi1, hi2, lo1, lo2, best, gs, keep = q20
            for o, a, op in ((hi1, 0, ALU.max), (lo1, 0, ALU.min), (hi2, 2, ALU.max), (lo2, 2, ALU.min)):
                do(tt(o, v[:, :, a], v[:, :, a + 1], op))
            do(tt(gs, hi1, hi2, ALU.min))
            do(tt(lo1, lo1, lo2, ALU.max))
            do(tt(gs, gs, lo1, ALU.max))
            do(tt(hi1, hi1, hi2, ALU.max))
            do(tt(gs, hi1, gs, ALU.add))
            best3 = best.rearrange("p (c g) -> p c g", c=NC)
            first_of(best3, gs.rearrange("p (c g) -> p c g", c=NC), pri4, NG)
            do(nc.vector.tensor_scalar(keep, best, BIG, -BIG, ALU.mult, ALU.add))
            sm = selm.rearrange("p c (g e) -> p (c g) e", e=4)
            do(tt(sm, v, bc(best, 4), ALU.mult))
            do(tt(sm, sm, bc(keep, 4), ALU.add))
            first_of(m1, selm, pri16, NE)
            do(nc.vector.scalar_tensor_tensor(out=selm, in0=m1, scalar=-2.0 * BIG, in1=selm, op0=ALU.mult, op1=ALU.add))
            first_of(m2, selm, pri16, NE)
            do(tt(tmp, m1, m2, ALU.add))
            nc.vector.tensor_copy(sbf, tmp).then_inc(s_mask, 1)
            for k, m in enumerate((m1, m2)):
                do(tt(tmp, m, score, ALU.mult) if k else tt(slot, m, score, ALU.mult))
            do(nc.vector.tensor_reduce(w12[:, 0, :], slot, AX.X, ALU.add))
            do(nc.vector.tensor_reduce(w12[:, 1, :], tmp, AX.X, ALU.add))
            do(tt(five, w12[:, 0, :], w12[:, 1, :], ALU.add))
            do(nc.vector.reciprocal(five, five))
            do(tt(w12, w12, five.unsqueeze(1).broadcast_to([P, 2, NC]), ALU.mult))
            dve.wait_ge(s_pe, 1)
            do(nc.vector.tensor_copy(cnt, ps[:, 1, 0:NE]))
            do(nc.vector.tensor_scalar(ext, cnt, 128.0, None, ALU.is_gt))
            for m in range(2, NC):
                do(nc.vector.scalar_tensor_tensor(out=ext, in0=cnt, scalar=128.0 * m, in1=ext, op0=ALU.is_gt, op1=ALU.add))
            src, dst = ext, ca
            for sh in (1, 2, 4, 8):
                do(nc.vector.tensor_copy(dst[:, 0:sh], src[:, 0:sh]))
                do(tt(dst[:, sh:NE], src[:, sh:NE], src[:, 0:NE - sh], ALU.add))
                src, dst = dst, (cb if dst is ca else ca)
            cum = src
            do(tt(pre, cum, ext, ALU.subtract))
            do(nc.vector.tensor_scalar(pre, pre, 128.0, 16.0 * 128 - 128, ALU.mult, ALU.add))
            rank = ps[:, 0, 0:NC * NE].rearrange("p (c e) -> p c e", c=NC)
            do(nc.vector.tensor_copy(tmp, rank))
            do(tt(slot, tmp, over_c(pre), ALU.add))
            do(tt(pre, e128, pre, ALU.subtract))
            do(nc.vector.scalar_tensor_tensor(out=tmp, in0=tmp, scalar=128.0, in1=over_c(pre), op0=ALU.is_lt, op1=ALU.mult))
            do(tt(slot, slot, tmp, ALU.add))
            for k, m in enumerate((m1, m2)):
                do(tt(tmp, m, slot, ALU.mult))
                do(nc.vector.tensor_reduce(five, tmp, AX.X, ALU.add))
                do(nc.vector.tensor_copy(r.slot[k], five))
            one = lambda v: v[0:1]
            do(tt(one(over), one(col)[:, 0:10].unsqueeze(2).broadcast_to([1, 10, NE]),
                  one(cum).unsqueeze(1).broadcast_to([1, 10, NE]), ALU.is_ge))
            do(nc.vector.tensor_reduce(one(tabf)[:, NE:NMB], one(over), AX.X, ALU.add))
            do(nc.vector.tensor_scalar(one(tabf)[:, NE:NMB], one(tabf)[:, NE:NMB], NE - 1.0, None, ALU.min))
            do(nc.vector.tensor_copy(one(tabf)[:, 0:NE], one(col)[:, 0:NE]))
            do(nc.vector.tensor_scalar(one(five), one(thr), one(cum)[:, NE - 1:NE], None, ALU.is_lt))
            do(nc.vector.tensor_reduce(one(tabf)[:, NMB:NMB + 1], one(five), AX.X, ALU.add))
            do(nc.vector.tensor_scalar(one(tabf)[:, NMB:NMB + 1], one(tabf)[:, NMB:NMB + 1], NE / 2.0, None, ALU.add))
            nc.vector.tensor_copy(r.table, one(tabf)).then_inc(s_ready, 1)

        @block.tensor
        def _(pe):
            pe.wait_ge(s_mask, 1)
            for c in range(NC):
                for d in range(c):
                    nc.tensor.matmul(ps[:, 0, c * NE:(c + 1) * NE], oneb, sbf[:, d, :], start=(d == 0), stop=False)
                nc.tensor.matmul(ps[:, 0, c * NE:(c + 1) * NE], ltb, sbf[:, c, :], start=(c == 0), stop=True)
            for c in range(NC):
                last = nc.tensor.matmul(ps[:, 1, 0:NE], oneb, sbf[:, c, :], start=(c == 0), stop=(c == NC - 1))
            last.then_inc(s_pe, 1)

        @block.gpsimd
        def _(pool):
            pool.wait_ge(s_ready, 1)
            for c in range(NC):
                for k in range(2):
                    pool.indirect_dma_start(out=scr["xs"], out_offset=bass.IndirectOffsetOnAxis(ap=r.slot[k][:, c:c + 1], axis=0),
                                            in_=h2[:, c, :], in_offset=None).then_inc(s_sc, 16)
            pool.wait_ge(s_sc, 16 * 2 * NC)


def stage_experts(kit, io, scr):
    nc, ps = kit.nc, kit.ps
    r = Routing(kit)
    S = 4096
    slots = [O_X + S * j for j in range(4)] + [O_MG + S * j for j in range(4)]
    WG, WU, WD = ([kit.at(slots[3 * u + q], S) for u in range(2)] for q in range(3))
    act0 = slots[6]
    XB, YB = kit.at(act0, 2, D), kit.at(act0 + 2048, 2, D)
    HB = kit.at(slots[7], 2, KD, P)
    AB, AT_ = kit.at(slots[7] + 2048, 2, FE), kit.at(slots[7] + 3072, 2, 4, P)
    ident = kit.const("ident")
    pair = lambda name: [kit.sem(f"e_{name}{u}") for u in range(2)]
    ldx, ldg, ldu, ldd = pair("rows_loaded"), pair("gate_loaded"), pair("up_loaded"), pair("down_loaded")
    ti, hta, htd = pair("rows_turned"), pair("rows_taken_a"), pair("rows_taken_v")
    gu, sg, ab, ta, at = pair("hidden"), pair("silu"), pair("product"), pair("product_turned"), pair("product_taken")
    dn, ya, yd, yst = pair("down"), pair("y_taken_a"), pair("y_taken_v"), pair("y_stored")
    yfree = pair("y_free")
    xs = scr["xs"].rearrange("(b p) d -> b p d", p=P)
    ys = scr["ys"].rearrange("(b p) d -> b p d", p=P)
    row = lambda ap: ap.rearrange("a p d -> (a p) d")
    pairs = lambda eng: eng.value_load(r.table[0:1, NMB:NMB + 1], min_val=NE // 2, max_val=NMB // 2)

    with nc.Block() as block:
        @block.sync
        def _(sp):
            n = pairs(sp)
            sp.dma_start(XB[:, 0, :], xs[0]).then_inc(ldx[0], 16)
            with sp.Fori(0, n) as j:
                for u in range(2):
                    e = sp.value_load(r.table[0:1, bass.ds(j * 2 + u, 1)], min_val=0, max_val=NE - 1)
                    v = 1 - u
                    if u == 0:
                        sp.wait_ge(ti[1], j + 1)
                    else:
                        sp.wait_ge(ti[0], j + 2)
                    sp.dma_start(XB[:, v, :], row(xs[bass.ds(j * 2 + (u + 1), 1)])).then_inc(ldx[v], 16)
                    sp.wait_ge(gu[u], j + 1)
                    sp.dma_start(WG[u], row(io["wg"][bass.ds(e, 1)])).then_inc(ldg[u], 16)
                    sp.dma_start(WU[u], row(io["wu"][bass.ds(e, 1)])).then_inc(ldu[u], 16)
                    sp.wait_ge(dn[u], j + 1)
                    sp.dma_start(WD[u], row(io["wd"][bass.ds(e, 1)])).then_inc(ldd[u], 16)
            for u in range(2):
                pass

        @block.gpsimd
        def _(pool):
            for u in range(2):
                pool.sem_inc(yfree[u], 1)
            n = pairs(pool)
            with pool.Fori(0, n) as j:
                for u in range(2):
                    pool.wait_ge(ya[u], j + 2)
                    pool.wait_ge(yd[u], j + 2)
                    pool.dma_start(row(ys[bass.ds(j * 2 + u, 1)]), YB[:, u, :]).then_inc(yst[u], 16)
                    pool.wait_ge(yst[u], j * 16 + 16)
                    pool.sem_inc(yfree[u], 1)

        @block.tensor
        def _(pe):
            for s in (gu, dn, ta):
                for u in range(2):
                    pe.sem_inc(s[u], 1)
            pe.sem_inc(ti[1], 1)
            pe.sem_inc(ti[0], 1)
            n = pairs(pe)

            def turn_rows(u, loaded):
                pe.wait_ge(ldx[u], loaded)
                for k in range(KD):
                    last = nc.tensor.transpose(ps[:, 6 + k // 4, (k % 4) * P:(k % 4 + 1) * P], XB[:, u, k * P:(k + 1) * P], ident)
                last.then_inc(ti[u], 1)

            turn_rows(0, 16)
            with pe.Fori(0, n) as j:
                for u in range(2):
                    v = 1 - u
                    pe.wait_ge(hta[u], j + 2)
                    pe.wait_ge(htd[u], j + 2)
                    pe.wait_ge(ab[u], j + 1)
                    for W, ld, b in ((WG[u], ldg[u], 2 * u), (WU[u], ldu[u], 2 * u + 1)):
                        pe.wait_ge(ld, j * 16 + 16)
                        for k in range(KD):
                            last = nc.tensor.matmul(ps[:, b, :], HB[:, u, k, :], W[:, k * FE:(k + 1) * FE],
                                                    start=(k == 0), stop=(k == KD - 1))
                    last.then_inc(gu[u], 1)
                    pe.wait_ge(at[v], j + 1 if u == 0 else j + 2)
                    turn_rows(v, j * 16 + 16 if u == 0 else j * 16 + 32)
                    pe.wait_ge(hta[v], j + 2 if u == 0 else j + 3)
                    pe.wait_ge(ab[u], j + 2)
                    for k in range(4):
                        last = nc.tensor.transpose(ps[:, 6, k * P:(k + 1) * P], AB[:, u, k * P:(k + 1) * P], ident)
                    last.then_inc(ta[u], 1)
                    pe.wait_ge(ldd[u], j * 16 + 16)
                    pe.wait_ge(at[u], j + 2)
                    pe.wait_ge(ya[v], j + 1 if u == 0 else j + 2)
                    pe.wait_ge(yd[v], j + 1 if u == 0 else j + 2)
                    for h in range(2):
                        for k in range(4):
                            last = nc.tensor.matmul(ps[:, 4 + h, :], AT_[:, u, k, :],
                                                    WD[u][:, k * D + h * 512:k * D + (h + 1) * 512],
                                                    start=(k == 0), stop=(k == 3))
                    last.then_inc(dn[u], 1)

        @block.scalar
        def _(act):
            for s in (hta, at, ya):
                for u in range(2):
                    act.sem_inc(s[u], 1)
            n = pairs(act)

            def take_rows(u, turned, used):
                act.wait_ge(ti[u], turned)
                act.wait_ge(gu[u], used)
                nc.scalar.activation(HB[:, u, 0:4, :].rearrange("p k n -> p (k n)"), ps[:, 6, :], ACT.Copy).then_inc(hta[u], 1)

            take_rows(0, 2, 1)
            with act.Fori(0, n) as j:
                for u in range(2):
                    v = 1 - u
                    act.wait_ge(gu[u], j + 2)
                    act.wait_ge(ta[u], j + 1)
                    nc.scalar.activation(AB[:, u, :], ps[:, 2 * u, :], ACT.Silu).then_inc(sg[u], 1)
                    take_rows(v, j + 2 if u == 0 else j + 3, j + 1 if u == 0 else j + 2)
                    act.wait_ge(ta[u], j + 2)
                    act.wait_ge(dn[u], j + 1)
                    nc.scalar.activation(AT_[:, u, :, :].rearrange("p k n -> p (k n)"), ps[:, 6, :], ACT.Copy).then_inc(at[u], 1)
                    act.wait_ge(dn[u], j + 2)
                    act.wait_ge(yfree[u], j + 1)
                    nc.scalar.activation(YB[:, u, 0:512], ps[:, 4, :], ACT.Copy).then_inc(ya[u], 1)

        @block.vector
        def _(dve):
            for s in (htd, ab, yd):
                for u in range(2):
                    dve.sem_inc(s[u], 1)
            n = pairs(dve)

            def take_rows(u, turned, used):
                dve.wait_ge(ti[u], turned)
                dve.wait_ge(gu[u], used)
                nc.vector.tensor_copy(HB[:, u, 4:8, :].rearrange("p k n -> p (k n)"), ps[:, 7, :]).then_inc(htd[u], 1)

            take_rows(0, 2, 1)
            with dve.Fori(0, n) as j:
                for u in range(2):
                    v = 1 - u
                    dve.wait_ge(sg[u], j + 1)
                    nc.vector.tensor_tensor(AB[:, u, :], AB[:, u, :], ps[:, 2 * u + 1, :], ALU.mult).then_inc(ab[u], 1)
                    take_rows(v, j + 2 if u == 0 else j + 3, j + 1 if u == 0 else j + 2)
                    dve.wait_ge(dn[u], j + 2)
                    dve.wait_ge(yfree[u], j + 1)
                    nc.vector.tensor_copy(YB[:, u, 512:1024], ps[:, 5, :]).then_inc(yd[u], 1)


def stage_combine(kit, io, scr, out):
    nc = kit.nc
    r = Routing(kit)
    x2 = kit.at(O_H, NC, D)
    G2, FN = kit.at(T_G2, 2, D), kit.at(T_FN, D)
    Y = kit.at(O_X, 2 * NC, D)
    sq, ssq, rr = kit.at(O_MG, D), kit.at(O_MG + 1024, NC), kit.at(O_MG + 1032, NC)
    O = kit.at(O_MG + 1040, 2, D)
    s_y = [kit.sem(f"f_rows{c}") for c in range(NC)]
    s_v, s_sq, s_rt, s_o = kit.sem("f_steps"), kit.sem("f_squares"), kit.sem("f_root"), kit.sem("f_out")
    s_st = [kit.sem(f"f_stored{j}") for j in range(2)]
    NS = 7
    with nc.Block() as block:
        @block.gpsimd
        def _(pool):
            for c in range(NC):
                for k in range(2):
                    pool.indirect_dma_start(out=Y[:, 2 * c + k, :], out_offset=None, in_=scr["ys"],
                                            in_offset=bass.IndirectOffsetOnAxis(ap=r.slot[k][:, c:c + 1], axis=0)).then_inc(s_y[c], 16)

        @block.vector
        def _(dve):
            ch = Chain(dve, s_v)
            for c in range(NC):
                dve.wait_ge(s_y[c], 32)
                a, b = Y[:, 2 * c, :], Y[:, 2 * c + 1, :]
                ch.step(nc.vector.tensor_scalar(a, a, r.weight[:, 0, c:c + 1], None, ALU.mult))
                ch.sync()
                ch.step(nc.vector.scalar_tensor_tensor(out=a, in0=b, scalar=r.weight[:, 1, c:c + 1], in1=a,
                                                       op0=ALU.mult, op1=ALU.add))
                ch.sync()
                ch.step(nc.vector.tensor_tensor(a, a, G2[:, min(c, 1), :], ALU.mult))
                ch.sync()
                ch.step(nc.vector.tensor_tensor(x2[:, c, :], x2[:, c, :], a, ALU.add))
                dve.wait_ge(s_sq, c + 1)
                ch.step(nc.vector.tensor_scalar(ssq[:, c:c + 1], ssq[:, c:c + 1], 1.0 / D, EPS, ALU.mult, ALU.add))
                ch.sync()
                ch.step(nc.vector.reciprocal(rr[:, c:c + 1], ssq[:, c:c + 1]))
                dve.wait_ge(s_rt, c + 1)
                if c >= 2:
                    dve.wait_ge(s_st[c % 2], 16 * (c // 2))
                ch.step(nc.vector.scalar_tensor_tensor(out=O[:, c % 2, :], in0=x2[:, c, :], scalar=rr[:, c:c + 1], in1=FN,
                                                       op0=ALU.mult, op1=ALU.mult))

        @block.scalar
        def _(act):
            for c in range(NC):
                act.wait_ge(s_v, NS * c + 4)
                if c:
                    act.wait_ge(s_sq, c)
                nc.scalar.activation(sq, x2[:, c, :], ACT.Square, accum_out=ssq[:, c:c + 1]).then_inc(s_sq, 1)
                act.wait_ge(s_v, NS * c + 6)
                nc.scalar.activation(rr[:, c:c + 1], rr[:, c:c + 1], ACT.Sqrt).then_inc(s_rt, 1)

        @block.sync
        def _(sp):
            for c in range(NC):
                sp.wait_ge(s_v, NS * (c + 1))
                dst = out["y_prompt"] if c == 0 else out["y_sample"][(c - 1) * P:c * P, :]
                sp.dma_start(dst, O[:, c % 2, :]).then_inc(s_st[c % 2], 16)
            sp.wait_ge(s_st[0], 48)
            sp.wait_ge(s_st[1], 32)


def scratch(nc):
    dram = lambda name, shape: nc.dram_tensor(name, shape, F32, kind="Internal").ap()
    return dict(xp=dram("x_plus_pos", [T, D]), xs=dram("slot_rows", [(NMB + 1) * P, D]), ys=dram("expert_rows", [NMB * P, D]),
                z=dram("silu_z", [T, INNER]), gb=dram("gate_b", [KD, P, T]), mod=dram("modulation", [2, 4 * D]))


def run_stages(kit, io, scr, out, upto=99):
    ht = stage_modulate(kit, io, scr)
    if upto < 1:
        return
    ya = stage_gmlp(kit, io, scr, ht)
    if upto < 2:
        return
    stage_branch_a(kit, io, scr, ht, ya)
    if upto < 3:
        return
    stage_dt(kit, io)
    stage_conv(kit, io)
    if upto < 4:
        return
    stage_gates(kit, io, scr)
    if upto < 5:
        return
    stage_ssd(kit, io, out)
    if upto < 6:
        return
    stage_norm_y(kit, io, scr)
    kit.recycle()
    if upto < 7:
        return
    stage_branch_b(kit, io, scr)
    if upto < 8:
        return
    stage_out(kit, io, scr)
    stage_route(kit, io, scr)
    if upto < 9:
        return
    stage_experts(kit, io, scr)
    if upto < 10:
        return
    stage_combine(kit, io, scr, out)


def build(nc, io, out):
    with ExitStack() as ctx:
        run_stages(Kit(nc, ctx), io, scratch(nc), out)


def host_layout(i):
    import numpy as np
    a = {k: np.asarray(v) for k, v in i.items()}
    w_in = a["w_in"][0]
    cut = [0, 1024, 2048, 3072, 4096, 6144, 9216, 9280]
    ga, gb, u, v, z, xbc, dt = [w_in[:, cut[j]:cut[j + 1]] for j in range(7)]

    def units(w, cols):
        r, n = w.shape
        return w.reshape(r // P, P, n // cols, cols).transpose(2, 1, 0, 3).reshape(n // cols, P, -1)

    A = [units(ga, UC), units(a["w_branch_a"][0], UC)]
    stream = [units(v, UC), units(u, UC), np.stack(A, 1).reshape(8, P, UNIT), units(xbc, UC), units(z, UC),
              units(gb, UC), units(a["w_branch_b"][0], P), units(a["w_out"][0], UC)]
    o = {"units": np.concatenate(stream, 0)}
    o["w_dt"] = units(dt, 64)[0]
    o["w_mod"] = units(a["w_mod"][0], 512)
    o["b_mod"] = a["b_mod"][0][None]
    o["cond"] = np.stack([a["c_ctx"], a["c"][0]], 0).reshape(2, KD, P).transpose(2, 1, 0).reshape(P, 16)
    o["x"] = np.concatenate([a["x_prompt"][0], a["x_sample"][0]], 0)
    col = lambda w: w.reshape(-1, P).T
    o["norm1"] = col(a["norm1_w"][0])
    o["wsT"] = a["gmlp_ws"][0].transpose(2, 0, 1)
    o["gmlp_nw"] = col(a["gmlp_norm_w"][0])
    o["gmlp_bs"] = a["gmlp_bs"][0].reshape(1, -1)
    o["dt_bias"] = a["dt_bias"][0].reshape(64, 1)
    o["a_log"] = a["a_log"][0].reshape(1, 64)
    o["conv_w"] = a["conv_w"][0].reshape(TAPS, -1, P).transpose(2, 1, 0).reshape(P, -1)
    o["conv_b"] = col(a["conv_b"][0])
    o["state_t"] = a["state_ssd"][0, 0].reshape(2, INNER, P).transpose(0, 2, 1)
    o["d_skip"] = a["d_skip"].reshape(1, HEADS)
    o["ssd_nw"] = col(a["ssd_norm_w"][0])
    o["norm2"], o["fnorm"] = a["norm2_w"][0].reshape(1, D), a["final_norm_w"].reshape(1, D)
    o["router_w"], o["router_b"] = units(a["router_w"], NE)[0], a["router_bias"].reshape(1, NE)
    experts = lambda w: w.reshape(NE, w.shape[1] // P, P, w.shape[2]).transpose(0, 2, 1, 3).reshape(NE, P, -1)
    o["wg"], o["wu"], o["wd"] = experts(a["w_gate_e"][0]), experts(a["w_up_e"][0]), experts(a["w_down_e"][0])
    grid = 64
    omega = 1.0 / (10000.0 ** (np.arange(D // 4, dtype=np.float32) / np.float32(D // 4)))
    r = np.arange(LAT // grid, dtype=np.float32)[:, None] * omega
    cc = np.arange(grid, dtype=np.float32)[:, None] * omega
    r = np.concatenate([np.sin(r), np.cos(r)], -1)
    cc = np.concatenate([np.sin(cc), np.cos(cc)], -1)
    pos = np.concatenate([np.repeat(r, grid, 0), np.tile(cc, (LAT // grid, 1))], -1).astype(np.float32)
    o["pos"] = pos
    K = np.zeros((P, KOFF["end"]), np.float32)
    p, q = np.arange(P)[:, None], np.arange(P)[None]
    for name, m in (("ident", p == q), ("le", p <= q), ("ge", p >= q), ("gt", p > q), ("lt", p < q), ("one", p >= 0)):
        K[:, KOFF[name]:KOFF[name] + P] = m
    K[:, KOFF["e128"]:KOFF["e128"] + 16] = np.arange(16) * 128
    K[:, KOFF["pri16"]:KOFF["pri16"] + 16] = 16 - np.arange(16)
    K[:, KOFF["pri4"]:KOFF["pri4"] + 4] = 4 - np.arange(4)
    K[:, KOFF["thr"]:KOFF["thr"] + 5] = 2 * np.arange(5)
    K[:, KOFF["col"]:KOFF["col"] + 26] = np.arange(26)
    o["consts"] = K
    return {k: np.ascontiguousarray(v) for k, v in o.items()}


def kernel(**inputs):
    import numpy as np
    import concourse.bacc as bacc
    from concourse.bass_utils import run_bass_kernel_spmd

    nc = bacc.Bacc("TRN2", target_bir_lowering=False, num_devices=1)
    arrays = host_layout(inputs)
    io = {k: nc.dram_tensor("in_" + k, v.shape, mybir.dt.from_np(v.dtype), kind="ExternalInput").ap()
          for k, v in arrays.items()}
    shapes = dict(y_prompt=(P, D), y_sample=(LAT, D), state=(2, INNER, P))
    out = {k: nc.dram_tensor("out_" + k, s, F32, kind="ExternalOutput").ap() for k, s in shapes.items()}
    build(nc, io, out)
    r = run_bass_kernel_spmd(nc, [{"in_" + k: v for k, v in arrays.items()}], core_ids=[0]).results[0]
    return (np.asarray(r["out_y_prompt"]).reshape(1, P, D), np.asarray(r["out_y_sample"]).reshape(1, LAT, D),
            np.asarray(r["out_state"]).reshape(1, 1, 2, HEADS, HD, P))
```

```python
import concourse.bass as bass
from concourse import mybir
from contextlib import ExitStack

F32 = mybir.dt.float32
F32R = mybir.dt.float32r
BF16 = mybir.dt.bfloat16
I32 = mybir.dt.int32
U32 = mybir.dt.uint32
ALU = mybir.AluOpType
ACT = mybir.ActivationFunctionType
AX = mybir.AxisListType

P = 128
D = 1024
KD = D // P
NC = 5
T = NC * P
LAT = T - P
HALF = T // 2
G = 4
HPG = 8
HEADS = G * HPG
HD = 64
GW = HPG * HD
INNER = G * GW
KI = INNER // P
NE = 16
NG = 4
FE = 512
EPS = 1e-6
TAPS = 5
UNIT = 2048
UC = 256
NMB = 26
BIG = 1.0e30

O_H = 0
O_X = 10240
O_BC = 20480
O_TMP = 28160
O_MG = 33280
O_RAW = 38400
O_HL = 42496
O_K = 50688
ARENA = 52992
REGIONS = (O_H, O_X, O_BC, O_TMP, O_MG, O_RAW, O_HL, O_K)
KOFF = dict(ident=0, le=128, ge=256, gt=384, lt=512, one=640, e128=768, pri16=784, pri4=800, thr=804, col=812, end=840)


class Kit:

    def __init__(self, nc, ctx):
        self.nc, self.sems = nc, []
        self.arena = ctx.enter_context(nc.sbuf_tensor("arena", [P, ARENA], F32))
        self.base = nc.sbuf_base - 4 * ARENA
        self.tensors = {}
        self.ps = ctx.enter_context(nc.psum_tensor("banks", [P, 8, 512], F32))

    def sem(self, name):
        self.sems.append(self.nc.alloc_semaphore(name=name))
        return self.sems[-1]

    def recycle(self):
        self.nc.clear_and_free_semaphores(self.sems)
        self.nc.all_engine_barrier()
        self.sems = []

    def placed(self, name, off, n, dtype):
        if name not in self.tensors:
            self.tensors[name] = self.nc.alloc_sbuf_tensor_at(name, [P, n], dtype,
                                                              offset=self.base + 4 * off)
        return self.tensors[name]

    def at(self, off, *dims):
        n = 1
        for d in dims:
            n *= d
        first = max(o for o in REGIONS if o <= off)
        end = min(o for o in REGIONS + (ARENA,) if o >= off + n)
        t = self.placed(f"words_{first}_{end}", first, end - first, F32)
        return self.shaped(t[:, off - first:off - first + n], dims)

    def rnd(self, off, *dims):
        n = 1
        for d in dims:
            n *= d
        return self.shaped(self.placed(f"rounded_{off}_{n}", off, n, F32R)[:, :], dims)

    def shaped(self, v, dims):
        if len(dims) == 2:
            v = v.rearrange("p (a b) -> p a b", a=dims[0])
        if len(dims) == 3:
            v = v.rearrange("p (a b c) -> p a b c", a=dims[0], b=dims[1])
        return v

    def const(self, name, n=P):
        return self.at(O_K, KOFF["end"])[:, KOFF[name]:KOFF[name] + n]


class Chain:

    def __init__(self, eng, sem):
        self.eng, self.sem, self.n = eng, sem, 0

    def step(self, ins):
        ins.then_inc(self.sem, 1)
        self.n += 1

    def sync(self):
        self.eng.wait_ge(self.sem, self.n)


class Weights:

    def __init__(self, kit, stream, units):
        self.nc, self.units, self.count, self.first = kit.nc, units, units.shape[0], 0
        self.raw = kit.at(O_RAW, 2, UNIT)
        self.hi, self.lo = kit.rnd(O_HL, 2, UNIT), kit.rnd(O_HL + 2 * UNIT, 2, UNIT)
        self.raw_loaded = [kit.sem(f"{stream}_raw_loaded{s}") for s in range(2)]
        self.hi_ready = kit.sem(f"{stream}_hi_ready")
        self.lo_ready = kit.sem(f"{stream}_lo_ready")
        self.used = kit.sem(f"{stream}_unit_used")

    def section(self, n):
        w = Section(self, n)
        self.first += n
        return w


class Section(Weights):

    AHEAD = 2

    def __init__(self, stream, n):
        self.nc, self.units, self.count = stream.nc, stream.units, stream.count
        self.first, self.n = stream.first, n
        self.raw, self.hi, self.lo = stream.raw, stream.hi, stream.lo
        self.raw_loaded, self.hi_ready, self.lo_ready = stream.raw_loaded, stream.hi_ready, stream.lo_ready
        self.used = stream.used

    def to_load(self):
        return range(self.AHEAD if self.n else 0, min(self.n + self.AHEAD, self.count - self.first))

    def exists(self, i):
        return self.first + i < self.count

    def load(self, sp, i):
        i += self.first
        if i >= 2:
            sp.wait_ge(self.lo_ready, i - 1)
        sp.dma_start(self.raw[:, i % 2, :], self.units[i]).then_inc(self.raw_loaded[i % 2], 16)

    def split_hi(self, act, i):
        i += self.first
        act.wait_ge(self.raw_loaded[i % 2], 16 * (i // 2 + 1))
        if i >= 2:
            act.wait_ge(self.used, i - 1)
        self.nc.scalar.activation(self.hi[:, i % 2, :], self.raw[:, i % 2, :],
                                  ACT.Copy).then_inc(self.hi_ready, 1)

    def split_lo(self, dve, i):
        i += self.first
        dve.wait_ge(self.hi_ready, i + 1)
        if i >= 2:
            dve.wait_ge(self.used, i - 1)
        self.nc.vector.tensor_tensor(self.lo[:, i % 2, :], self.raw[:, i % 2, :],
                                     self.hi[:, i % 2, :].bitcast(F32), ALU.subtract).then_inc(self.lo_ready, 1)

    def parts(self, i, k):
        i += self.first
        return [x[:, i % 2, :].rearrange("p (k n) -> p k n", k=k)
                for x in (self.hi, self.lo)]

    def ready(self, pe, i):
        pe.wait_ge(self.hi_ready, self.first + i + 1)
        pe.wait_ge(self.lo_ready, self.first + i + 1)

    def done(self, i):
        return self.used, self.first + i + 1


def split3(nc, out, lhs, rhs, nk):
    for k in range(nk):
        nc.tensor.matmul(out, lhs[0](k), rhs[0](k), start=(k == 0), stop=False)
        nc.tensor.matmul(out, lhs[0](k), rhs[1](k), start=False, stop=False)
        last = nc.tensor.matmul(out, lhs[1](k), rhs[0](k), start=False, stop=(k == nk - 1))
    return last


def feature_tile(nc, w, t, moving, out, nk):
    for h in range(2):
        last = split3(nc, out(h), [lambda k, x=x: x[:, k, t * P:(t + 1) * P] for x in w],
                      [lambda k, x=x: x[:, k, h * HALF:(h + 1) * HALF] for x in moving], nk)
    return last


def token_tile(nc, w, c, stationary, out):
    return split3(nc, out, [lambda k, x=x: x[:, k, c * P:(c + 1) * P] for x in stationary],
                  [lambda k, x=x: x[:, k, :] for x in w], KD)


def halves(kit, pair):
    return kit.ps[:, 2 * pair:2 * pair + 2, 0:HALF]


def two(ap):
    return ap.rearrange("p (h n) -> p h n", h=2)


def stage_modulate(kit, stream, io, scr):
    nc, ps = kit.nc, kit.ps
    WM = [kit.at(o, 4096) for o in (O_H, O_H + 5120, O_MG, O_BC + 2304)]
    w = stream.section(0)
    RB = (4, 5, 7, 3)
    x = kit.at(O_X, NC, D)
    pos = kit.at(O_X + 5120, NC - 1, D)
    xn = kit.at(O_X + 5120, NC, D)
    cond = kit.at(O_TMP, 16)
    sc = kit.at(O_TMP + 16, 16)
    row = kit.at(O_TMP + 32, 2048)
    brow = kit.at(O_TMP + 2080, 2048)
    n1 = kit.at(O_TMP + 4128, KD)
    AS = kit.at(O_TMP + 4136, 2, KD, 2)
    ssq = kit.at(O_TMP + 4168, NC)
    rr = kit.at(O_TMP + 4173, NC)
    sq = kit.at(O_BC, D)
    full = kit.at(O_BC + 1024, 2, T)
    hi, lo = kit.rnd(O_H, KD, T), kit.rnd(O_H + 5120, KD, T)
    ident = kit.const("ident")
    s_small, s_x, s_w = kit.sem("m_small"), kit.sem("m_x"), [kit.sem(f"m_w{j}") for j in range(4)]
    s_c = kit.sem("m_consts")
    s_act, s_dve, s_row, s_cols = kit.sem("m_act"), kit.sem("m_dve"), kit.sem("m_row"), kit.sem("m_cols")
    s_xt, s_full, s_split, s_xp = kit.sem("m_xt"), kit.sem("m_full"), kit.sem("m_split"), kit.sem("m_xp")

    with nc.Block() as block:
        @block.sync
        def _(sp):
            sp.dma_start(kit.at(O_K, KOFF["end"]), io["consts"]).then_inc(s_c, 16)
            sp.dma_start(cond, io["cond"]).then_inc(s_small, 16)
            sp.dma_start(n1, io["norm1"]).then_inc(s_small, 16)
            sp.dma_start(brow[0:2, :], io["b_mod"][:, 0:2048].partition_broadcast(2)).then_inc(s_small, 16)
            sp.dma_start(WM[0], io["w_mod"][0]).then_inc(s_w[0], 16)
            sp.dma_start(x, io["x"].rearrange("(c p) d -> p c d", p=P)).then_inc(s_x, 16)
            sp.dma_start(pos, io["pos"].rearrange("(c p) d -> p c d", p=P)).then_inc(s_x, 16)
            for j in range(1, 4):
                sp.dma_start(WM[j], io["w_mod"][j]).then_inc(s_w[j], 16)
            for i in w.to_load():
                w.load(sp, i)
            sp.wait_ge(s_dve, 2)
            sp.dma_start(scr["xp"].rearrange("(c p) d -> p c d", p=P), x).then_inc(s_xp, 16)
            sp.wait_ge(s_xp, 16)

        @block.scalar
        def _(act):
            act.wait_ge(s_small, 48)
            nc.scalar.activation(sc, cond, ACT.Silu).then_inc(s_act, 1)
            act.wait_ge(s_dve, 2)
            for c in range(NC):
                if c:
                    act.wait_ge(s_act, c + 1)
                nc.scalar.activation(sq, x[:, c, :], ACT.Square, accum_out=ssq[:, c:c + 1]).then_inc(s_act, 1)
            act.wait_ge(s_dve, 4)
            nc.scalar.activation(rr, rr, ACT.Sqrt).then_inc(s_act, 1)
            w.split_hi(act, 0)
            for k in range(KD):
                act.wait_ge(s_xt, k + 1)
                act.wait_ge(s_cols, 2)
                if k >= 2:
                    act.wait_ge(s_split, 2 * (k - 1))
                for st, lo_, hi_ in ((0, 0, P), (1, P, T)):
                    b = 2 * (k % 2)
                    src = ps[:, b:b + 2, :].rearrange("p a b -> p (a b)")[:, lo_:hi_]
                    nc.scalar.activation(full[:, k % 2, lo_:hi_], src, ACT.Identity,
                                         scale=AS[:, 1, k, st:st + 1],
                                         bias=AS[:, 0, k, st:st + 1]).then_inc(s_full, 1)

        @block.vector
        def _(dve):
            ch = Chain(dve, s_dve)
            dve.wait_ge(s_x, 32)
            ch.step(nc.vector.tensor_tensor(x[:, 1:3, :], x[:, 1:3, :], pos[:, 0:2, :], ALU.add))
            ch.step(nc.vector.tensor_tensor(x[:, 3:5, :], x[:, 3:5, :], pos[:, 2:4, :], ALU.add))
            dve.wait_ge(s_act, 1 + NC)
            ch.step(nc.vector.tensor_scalar(ssq, ssq, 1.0 / D, EPS, ALU.mult, ALU.add))
            ch.sync()
            ch.step(nc.vector.reciprocal(rr, ssq))
            dve.wait_ge(s_act, 2 + NC)
            for c in range(NC):
                ch.step(nc.vector.tensor_scalar(xn[:, c, :], x[:, c, :], rr[:, c:c + 1], None, ALU.mult))
            for j in range(4):
                dve.wait_ge(s_row, j + 1)
                ch.step(nc.vector.tensor_tensor(row[0:2, j * 512:(j + 1) * 512], ps[0:2, RB[j], :],
                                                brow[0:2, j * 512:(j + 1) * 512], ALU.add))
            dve.wait_ge(s_row, 5)
            v = ps[:, 6, 0:32].rearrange("p (q k s) -> p q k s", q=2, k=KD)
            nc.vector.tensor_copy(AS[:, 0, :, :], v[:, 0, :, :]).then_inc(s_cols, 1)
            nc.vector.scalar_tensor_tensor(out=AS[:, 1, :, :], in0=v[:, 1, :, :], scalar=1.0,
                                           in1=n1.unsqueeze(2).broadcast_to([P, KD, 2]),
                                           op0=ALU.add, op1=ALU.mult).then_inc(s_cols, 1)
            w.split_lo(dve, 0)
            for k in range(KD):
                dve.wait_ge(s_full, 2 * k + 2)
                nc.vector.tensor_copy(hi[:, k, :], full[:, k % 2, :]).then_inc(s_split, 1)
                dve.wait_ge(s_split, 2 * k + 1)
                nc.vector.tensor_tensor(lo[:, k, :], full[:, k % 2, :], hi[:, k, :].bitcast(F32),
                                        ALU.subtract).then_inc(s_split, 1)

        @block.tensor
        def _(pe):
            pe.wait_ge(s_c, 16)
            pe.wait_ge(s_act, 1)
            for j in range(4):
                pe.wait_ge(s_w[j], 16)
                for k in range(KD):
                    last = nc.tensor.matmul(ps[0:2, RB[j], :], sc.rearrange("p (k s) -> p k s", s=2)[:, k, :],
                                            WM[j][:, k * 512:(k + 1) * 512], start=(k == 0), stop=(k == KD - 1))
                last.then_inc(s_row, 1)
            pe.wait_ge(s_dve, 4 + NC + 4)
            for j in range(16):
                last = nc.tensor.transpose(ps[:, 6, 2 * j:2 * j + 2], row[0:2, j * P:(j + 1) * P], ident[0:2, 0:2])
            last.then_inc(s_row, 1)
            for k in range(KD):
                if k >= 2:
                    pe.wait_ge(s_full, 2 * (k - 1))
                b = 2 * (k % 2)
                for c in range(NC):
                    o = ps[:, b, c * P:(c + 1) * P] if c < 4 else ps[:, b + 1, 0:P]
                    last = nc.tensor.transpose(o, xn[:, c, k * P:(k + 1) * P], ident)
                last.then_inc(s_xt, 1)
    return hi, lo


def stage_gmlp(kit, stream, io, scr, ht):
    nc, ps = kit.nc, kit.ps
    V = kit.at(O_X, NC, D)
    ya = kit.at(O_X + 5120, KD, T)
    ya_hi, ya_lo = kit.rnd(O_X + 5120, KD, T), kit.rnd(O_X + 10240, KD, T)
    full = kit.at(O_TMP, 2, T)
    wsT = kit.at(O_TMP + 1280, KD, P)
    bsb = kit.at(O_TMP + 2304, KD, P)
    nw = kit.at(O_TMP + 3328, KD)
    ssq = kit.at(O_TMP + 3336, NC)
    rr = kit.at(O_TMP + 3341, NC)
    sq = kit.at(O_TMP + 3400, D)
    gate = kit.at(O_MG, KD, T)
    nv, nu, ng = 4, 4, 4
    w = stream.section(nv + nu + ng)
    s_c = kit.sem("g_consts")
    s_gt, s_gate = kit.sem("g_gate_tile"), kit.sem("g_gate")
    s_v, s_vev = kit.sem("g_v"), kit.sem("g_v_taken")
    s_u, s_uev = kit.sem("g_u"), kit.sem("g_u_taken")
    s_sq, s_n = kit.sem("g_squares"), kit.sem("g_norm")
    s_mix, s_m, s_split = kit.sem("g_mixed"), kit.sem("g_product"), kit.sem("g_split")
    s_zero, s_zo = kit.sem("g_zero"), kit.sem("g_zeros_stored")

    with nc.Block() as block:
        @block.sync
        def _(sp):
            sp.dma_start(wsT, io["wsT"]).then_inc(s_c, 16)
            sp.dma_start(nw, io["gmlp_nw"]).then_inc(s_c, 16)
            sp.dma_start(bsb, io["gmlp_bs"].partition_broadcast(P)).then_inc(s_c, 16)
            for i in w.to_load():
                w.load(sp, i)

        @block.gpsimd
        def _(pool):
            zero = kit.at(O_TMP + 4600, 512)
            nc.gpsimd.memset(zero, 0.0).then_inc(s_zero, 1)
            pool.wait_ge(s_zero, 1)
            rows = [(scr["xs"], b) for b in range(NMB + 1)] + [(scr["ys"], b) for b in range(NE, NMB)]
            for dst, b in rows:
                pool.dma_start(dst[b * P:(b + 1) * P, :].rearrange("p (a d) -> p a d", a=2),
                               zero.unsqueeze(1).broadcast_to([P, 2, 512])).then_inc(s_zo, 16)
            pool.wait_ge(s_zo, 16 * len(rows))

        @block.tensor
        def _(pe):
            for i in range(4):
                w.ready(pe, i)
                for c in range(NC):
                    if i:
                        pe.wait_ge(s_vev, NC * (i - 1) + c + 1)
                    last = token_tile(nc, w.parts(i, KD), c, ht, ps[:, c, 0:UC])
                    if c < NC - 1:
                        last.then_inc(s_v, 1)
                last.then_inc(w.used, 1)
            pe.wait_ge(s_vev, NC * 4)
            for i in range(4, 8):
                w.ready(pe, i)
                for t in range(2):
                    if i > 4:
                        pe.wait_ge(s_uev, 2 * (i - 5) + t + 1)
                    last = feature_tile(nc, w.parts(i, KD), t, ht, lambda h: halves(kit, t)[:, h, :], KD)
                    if t == 0:
                        last.then_inc(s_u, 1)
                last.then_inc(w.used, 1)
            for g in range(KD):
                i, t = nv + nu + g // 2, g % 2
                if t == 0:
                    w.ready(pe, i)
                if g < 2:
                    pe.wait_ge(s_uev, 6 + g + 1)
                else:
                    pe.wait_ge(s_gate, g - 1)
                last = feature_tile(nc, w.parts(i, KD), t, ht, lambda h: halves(kit, t)[:, h, :], KD)
                last.then_inc(w.used if t else s_gt, 1)
                if g == 0:
                    pe.wait_ge(s_c, 48)
                    pe.wait_ge(s_n, 2 + NC)
                if g >= 2:
                    pe.wait_ge(s_m, 3 * (g - 2) + 1)
                b = 4 + 2 * (g % 2)
                for c in range(NC):
                    o = ps[:, b, c * P:(c + 1) * P] if c < 4 else ps[:, b + 1, 0:P]
                    last = nc.tensor.matmul(o, V[:, c, g * P:(g + 1) * P], wsT[:, g, :], start=True, stop=True)
                last.then_inc(s_mix, 1)

        @block.scalar
        def _(act):
            for i in range(4):
                w.split_hi(act, i + 1)
                for c in range(NC):
                    if c < NC - 1:
                        act.wait_ge(s_v, (NC - 1) * i + c + 1)
                    else:
                        act.wait_ge(*w.done(i))
                    nc.scalar.activation(V[:, c, i * UC:(i + 1) * UC], ps[:, c, 0:UC],
                                         ACT.Gelu_apprx_tanh).then_inc(s_vev, 1)
            act.wait_ge(s_vev, NC * 4)
            for i in range(4, 8):
                w.split_hi(act, i + 1)
                for t in range(2):
                    if t == 0:
                        act.wait_ge(s_u, i - 4 + 1)
                    else:
                        act.wait_ge(*w.done(i))
                    nc.scalar.activation(two(ya[:, 2 * (i - 4) + t, :]), halves(kit, t),
                                         ACT.Gelu_apprx_tanh).then_inc(s_uev, 1)
                if i == 4:
                    for c in range(NC):
                        if c:
                            act.wait_ge(s_sq, c)
                        nc.scalar.activation(sq, V[:, c, :], ACT.Square,
                                             accum_out=ssq[:, c:c + 1]).then_inc(s_sq, 1)
            act.wait_ge(s_n, 2)
            nc.scalar.activation(rr, rr, ACT.Sqrt).then_inc(s_sq, 1)
            for g in range(KD):
                i, t = nv + nu + g // 2, g % 2
                if t == 0:
                    w.split_hi(act, i + 1)
                act.wait_ge(*(w.done(i) if t else (s_gt, g // 2 + 1)))
                nc.scalar.activation(two(gate[:, g, :]), halves(kit, t), ACT.Sigmoid).then_inc(s_gate, 1)
                act.wait_ge(s_m, 3 * g + 3)
                nc.scalar.activation(ya_hi[:, g, :], full[:, g % 2, :], ACT.Copy).then_inc(s_split, 1)

        @block.vector
        def _(dve):
            for i in range(4):
                w.split_lo(dve, i + 1)
            w.split_lo(dve, 5)
            dve.wait_ge(s_sq, NC)
            nc.vector.tensor_scalar(ssq, ssq, 1.0 / D, EPS, ALU.mult, ALU.add).then_inc(s_n, 1)
            dve.wait_ge(s_n, 1)
            nc.vector.reciprocal(rr, ssq).then_inc(s_n, 1)
            w.split_lo(dve, 6)
            w.split_lo(dve, 7)
            w.split_lo(dve, 8)
            dve.wait_ge(s_sq, NC + 1)
            for c in range(NC):
                nc.vector.tensor_scalar(V[:, c, :], V[:, c, :], rr[:, c:c + 1], None, ALU.mult).then_inc(s_n, 1)
            dve.wait_ge(s_c, 48)
            dve.wait_ge(s_uev, 8)
            for g in range(KD):
                if g % 2 == 0:
                    w.split_lo(dve, nv + nu + g // 2 + 1)
                dve.wait_ge(s_mix, g + 1)
                b = 4 + 2 * (g % 2)
                mixed = ps[:, b:b + 2, :].rearrange("p a b -> p (a b)")[:, 0:T].rearrange("p (c t) -> p c t", c=NC)
                f = full[:, g % 2, :]
                nc.vector.scalar_tensor_tensor(out=f.rearrange("p (c t) -> p c t", c=NC), in0=mixed, scalar=nw[:, g:g + 1],
                                               in1=bsb[:, g, :].unsqueeze(1).broadcast_to([P, NC, P]),
                                               op0=ALU.mult, op1=ALU.add).then_inc(s_m, 1)
                dve.wait_ge(s_m, 3 * g + 1)
                nc.vector.tensor_tensor(f, f, ya[:, g, :], ALU.mult).then_inc(s_m, 2)
                dve.wait_ge(s_split, g + 1)
                nc.vector.tensor_tensor(ya_lo[:, g, :], f, ya_hi[:, g, :].bitcast(F32), ALU.subtract).then_inc(s_n, 1)
                dve.wait_ge(s_n, 2 + NC + g + 1)
    return ya_hi, ya_lo


def stage_branch_a(kit, stream, io, scr, ya):
    nc = kit.nc
    MG = kit.at(O_MG, KD, T)
    w = stream.section(4)
    s_t0, s_mg = kit.sem("a_tile0"), kit.sem("a_merged")
    with nc.Block() as block:
        @block.sync
        def _(sp):
            for i in w.to_load():
                w.load(sp, i)

        @block.tensor
        def _(pe):
            for i in range(4):
                w.ready(pe, i)
                for t in range(2):
                    if i:
                        pe.wait_ge(s_mg, 2 * (i - 1) + t + 1)
                    last = feature_tile(nc, w.parts(i, KD), t, ya, lambda h: halves(kit, t)[:, h, :], KD)
                    last.then_inc(w.used if t else s_t0, 1)

        @block.scalar
        def _(act):
            for i in range(4):
                w.split_hi(act, i + 1)

        @block.vector
        def _(dve):
            for i in range(4):
                w.split_lo(dve, i + 1)
                for t in range(2):
                    dve.wait_ge(*(w.done(i) if t else (s_t0, i + 1)))
                    tile = MG[:, 2 * i + t, :]
                    nc.vector.tensor_tensor(two(tile), halves(kit, t), two(tile), ALU.mult).then_inc(s_mg, 1)


def stage_conv(kit, stream, io):
    nc, ps = kit.nc, kit.ps
    nt = (INNER + 2 * G * P) // P
    n, W0 = nt // 2, 2 + T + 4
    pre, acc, post = kit.at(O_TMP, 2, W0), kit.at(O_TMP + 2 * W0, 2, W0 - 4), kit.at(O_TMP + 4 * W0 - 8, 2, T)
    cw, cb = kit.at(O_TMP + 4 * W0 + 1280, nt, TAPS), kit.at(O_TMP + 4 * W0 + 1400, nt)
    X, Bt = kit.at(O_X, NC, INNER), kit.at(O_BC + 5120, NC, G * P)
    BCT = kit.at(O_BC, 2 * G, T)
    ht = [kit.rnd(o, KD, T) for o in (O_H, O_H + 5120)]
    ident = kit.const("ident")
    w = stream.section(n)
    s_in, s_pad, s_t0 = kit.sem("c_in"), kit.sem("c_pad"), kit.sem("c_tile0")
    s_pre, s_cv, s_silu, s_tr, s_x = (kit.sem("c_" + x) for x in ("pre", "conv", "silu", "turned", "x"))
    turned = lambda tile: tile < 20
    dest = lambda tile: post[:, tile % 2, :] if tile < 16 else BCT[:, tile - 16, :]
    raw, whi, wlo = kit.at(O_BC, 512), kit.rnd(O_BC + 512, 512), kit.rnd(O_BC + 1024, 512)
    bias = kit.at(O_BC + 1536, 1)[0:64]
    alog = kit.at(O_BC + 1600, 64)
    dtT = kit.at(O_BC + 1700, T)[0:64]
    dx, e, r, sden, s, s2, q = (kit.at(O_BC + 2400 + 320 * j, 320) for j in range(7))
    DT, A = kit.at(O_TMP + 4480, NC, 64), kit.at(O_TMP + 4800, NC, 64)
    d_in, d_hl, d_pe, d_act, d_dve = (kit.sem("d_" + x) for x in ("in", "split", "pe", "act", "dve"))
    DT_STEPS = 16
    with nc.Block() as block:
        @block.sync
        def _(sp):
            sp.dma_start(raw, io["w_dt"]).then_inc(d_in, 16)
            sp.dma_start(bias, io["dt_bias"]).then_inc(d_in, 16)
            sp.dma_start(alog, io["a_log"].partition_broadcast(P)).then_inc(d_in, 16)
            sp.dma_start(cw, io["conv_w"].rearrange("p (t k) -> p t k", k=TAPS)).then_inc(s_in, 16)
            sp.dma_start(cb, io["conv_b"]).then_inc(s_in, 16)
            for i in w.to_load():
                w.load(sp, i)

        @block.tensor
        def _(pe):
            def turn(i):
                for t in range(2):
                    tile = 2 * i + t
                    if not turned(tile):
                        continue
                    pe.wait_ge(s_silu, 2 * tile + 2)
                    if tile >= 2:
                        pe.wait_ge(s_x, tile - 1)
                    for c in range(NC):
                        o = ps[:, 4 + 2 * t + c // 4, (c % 4) * P:(c % 4 + 1) * P]
                        last = nc.tensor.transpose(o, dest(tile)[:, c * P:(c + 1) * P], ident)
                    last.then_inc(s_tr, 1)

            pe.wait_ge(d_hl, 2)
            wd = [v.rearrange("p (k n) -> p k n", k=KD) for v in (whi, wlo)]
            for h in range(2):
                last = split3(nc, ps[0:64, h, 0:HALF], [lambda k, v=v: v[:, k, :] for v in wd],
                              [lambda k, v=v: v[:, k, h * HALF:(h + 1) * HALF] for v in ht], KD)
            last.then_inc(d_pe, 1)
            pe.wait_ge(d_act, 1)
            for c in range(NC):
                last = nc.tensor.transpose(ps[:, 2, c * 64:(c + 1) * 64], dtT[:, c * P:(c + 1) * P], ident[0:64, 0:64])
            last.then_inc(d_pe, 1)
            for i in range(n):
                w.ready(pe, i)
                for t in range(2):
                    if i:
                        pe.wait_ge(s_pre, 3 * (2 * i + t - 1))
                    elif t:
                        pe.wait_ge(d_act, 3)
                    last = feature_tile(nc, w.parts(i, KD), t, ht, lambda h: halves(kit, t)[:, h, :], KD)
                    if t == 0:
                        last.then_inc(s_t0, 1)
                last.then_inc(w.used, 1)
                if i:
                    turn(i - 1)
            turn(n - 1)

        @block.scalar
        def _(act):
            act.wait_ge(d_in, 48)
            nc.scalar.activation(whi, raw, ACT.Copy).then_inc(d_hl, 1)
            act.wait_ge(d_pe, 1)
            nc.scalar.activation(dtT.rearrange("p (h n) -> p h n", h=2), ps[0:64, 0:2, 0:HALF], ACT.Identity,
                                 bias=bias).then_inc(d_act, 1)
            act.wait_ge(d_pe, 2)
            nc.scalar.activation(dx, ps[:, 2, 0:320], ACT.Copy).then_inc(d_act, 1)
            nc.scalar.activation(e, ps[:, 2, 0:320], ACT.Abs).then_inc(d_act, 1)
            act.wait_ge(d_act, 3)
            nc.scalar.activation(e, e, ACT.Exp, scale=-1.0).then_inc(d_act, 1)
            nc.scalar.activation(alog, alog, ACT.Exp).then_inc(d_act, 1)
            act.wait_ge(s_in, 32)
            act.wait_ge(s_pad, 3)

            def take_turned(i):
                for t in range(2):
                    tile = 2 * i + t
                    if not turned(tile):
                        continue
                    act.wait_ge(s_tr, tile + 1)
                    src = ps[:, 4 + 2 * t:6 + 2 * t, :].rearrange("p a b -> p (a b)")[:, 0:T].rearrange("p (c n) -> p c n", c=NC)
                    d = X[:, :, tile * P:(tile + 1) * P] if tile < 16 else Bt[:, :, (tile - 16) * P:(tile - 15) * P]
                    nc.scalar.activation(d, src, ACT.Copy).then_inc(s_x, 1)

            for i in range(n):
                if w.exists(i + 1):
                    w.split_hi(act, i + 1)
                for t in range(2):
                    act.wait_ge(*((s_t0, i + 1) if t == 0 else w.done(i)))
                    if i:
                        act.wait_ge(s_cv, TAPS * (2 * i + t - 1))
                    for a, b, o in ((0, P, 2), (P, HALF, 4)):
                        nc.scalar.activation(pre[:, t, a + o:b + o], ps[:, 2 * t, a:b], ACT.Copy).then_inc(s_pre, 1)
                    nc.scalar.activation(pre[:, t, HALF + 4:T + 4], ps[:, 2 * t + 1, 0:HALF], ACT.Copy).then_inc(s_pre, 1)
                if i:
                    take_turned(i - 1)
                for t in range(2):
                    tile = 2 * i + t
                    if tile == 16:
                        act.wait_ge(d_dve, DT_STEPS)
                    act.wait_ge(s_cv, TAPS * (tile + 1))
                    for a, b, o in ((0, P, 0), (P, T, 2)):
                        nc.scalar.activation(dest(tile)[:, a:b], acc[:, t, a + o:b + o], ACT.Silu,
                                             bias=cb[:, tile:tile + 1]).then_inc(s_silu, 1)
            take_turned(n - 1)

        @block.vector
        def _(dve):
            ch = Chain(dve, d_dve)
            dve.wait_ge(d_hl, 1)
            nc.vector.tensor_tensor(wlo, raw, whi.bitcast(F32), ALU.subtract).then_inc(d_hl, 1)
            dve.wait_ge(d_act, 5)
            ch.step(nc.vector.tensor_scalar(r, dx, 0.0, None, ALU.max))
            ch.step(nc.vector.tensor_scalar(sden, e, 2.0, None, ALU.add))
            ch.sync()
            ch.step(nc.vector.reciprocal(sden, sden))
            ch.sync()
            ch.step(nc.vector.tensor_tensor(s, e, sden, ALU.mult))
            ch.sync()
            ch.step(nc.vector.tensor_tensor(s2, s, s, ALU.mult))
            ch.sync()
            ch.step(nc.vector.tensor_scalar(q, s2, 1.0 / 17, None, ALU.mult))
            for odd in range(15, 1, -2):
                ch.sync()
                ch.step(nc.vector.scalar_tensor_tensor(out=q, in0=q, scalar=1.0 / odd, in1=s2, op0=ALU.add, op1=ALU.mult))
            ch.sync()
            ch.step(nc.vector.scalar_tensor_tensor(out=q, in0=q, scalar=1.0, in1=s, op0=ALU.add, op1=ALU.mult))
            ch.sync()
            dt = DT.rearrange("p c h -> p (c h)")
            ch.step(nc.vector.scalar_tensor_tensor(out=dt, in0=q, scalar=2.0, in1=r, op0=ALU.mult, op1=ALU.add))
            ch.sync()
            ch.step(nc.vector.scalar_tensor_tensor(out=A, in0=DT, scalar=-1.0,
                                                   in1=alog.unsqueeze(1).broadcast_to([P, NC, 64]),
                                                   op0=ALU.mult, op1=ALU.mult))
            assert ch.n == DT_STEPS
            for a, b in ((0, 2), (P + 2, P + 4), (W0 - 2, W0)):
                nc.vector.memset(pre[:, :, a:b], 0.0).then_inc(s_pad, 1)
            dve.wait_ge(s_in, 32)
            dve.wait_ge(s_pad, 3)
            for i in range(n):
                if w.exists(i + 1):
                    w.split_lo(dve, i + 1)
                for t in range(2):
                    tile = 2 * i + t
                    dve.wait_ge(s_pre, 3 * (tile + 1))
                    if i:
                        dve.wait_ge(s_silu, 2 * (tile - 1))
                    for k in range(TAPS):
                        src, tap = pre[:, t, k:k + W0 - 4], cw[:, tile, k:k + 1]
                        if k == 0:
                            nc.vector.tensor_scalar(acc[:, t, :], src, tap, None, ALU.mult).then_inc(s_cv, 1)
                        else:
                            dve.wait_ge(s_cv, TAPS * tile + k)
                            nc.vector.scalar_tensor_tensor(out=acc[:, t, :], in0=src, scalar=tap, in1=acc[:, t, :],
                                                           op0=ALU.mult, op1=ALU.add).then_inc(s_cv, 1)


def stage_gates(kit, stream, io, scr):
    nc, ps = kit.nc, kit.ps
    zs = kit.at(O_TMP, NC, UC)
    gs = kit.at(O_TMP + NC * UC, 2, T)
    ht = [kit.rnd(o, KD, T) for o in (O_H, O_H + 5120)]
    s_pe, s_silu, s_t0, s_sig = kit.sem("z_chunk"), kit.sem("z_silu"), kit.sem("z_tile0"), kit.sem("z_sigmoid")
    s_out = [kit.sem(f"z_stored{c}") for c in range(NC)]
    s_gout = [kit.sem(f"z_gate_stored{t}") for t in range(2)]
    nz, ng = 8, 4
    w = stream.section(nz + ng)
    with nc.Block() as block:
        @block.sync
        def _(sp):
            for i in w.to_load():
                w.load(sp, i)

        @block.tensor
        def _(pe):
            for i in range(nz):
                w.ready(pe, i)
                for c in range(NC):
                    if i:
                        pe.wait_ge(s_silu, NC * (i - 1) + c + 1)
                    last = token_tile(nc, w.parts(i, KD), c, ht, ps[:, c, 0:UC])
                    if c < NC - 1:
                        last.then_inc(s_pe, 1)
                last.then_inc(w.used, 1)
            pe.wait_ge(s_silu, NC * nz)
            for i in range(nz, nz + ng):
                w.ready(pe, i)
                for t in range(2):
                    if i > nz:
                        pe.wait_ge(s_sig, 2 * (i - nz - 1) + t + 1)
                    last = feature_tile(nc, w.parts(i, KD), t, ht, lambda h: halves(kit, t)[:, h, :], KD)
                    if t == 0:
                        last.then_inc(s_t0, 1)
                last.then_inc(w.used, 1)

        @block.scalar
        def _(act):
            for i in range(nz):
                w.split_hi(act, i + 1)
                for c in range(NC):
                    act.wait_ge(*((s_pe, (NC - 1) * i + c + 1) if c < NC - 1 else w.done(i)))
                    if i:
                        act.wait_ge(s_out[c], 16 * i)
                    nc.scalar.activation(zs[:, c, :], ps[:, c, 0:UC], ACT.Silu).then_inc(s_silu, 1)
            for i in range(nz, nz + ng):
                if w.exists(i + 1):
                    w.split_hi(act, i + 1)
                for t in range(2):
                    act.wait_ge(*((s_t0, i + 1 - nz) if t == 0 else w.done(i)))
                    if i > nz:
                        act.wait_ge(s_gout[t], 16 * (i - nz))
                    nc.scalar.activation(two(gs[:, t, :]), halves(kit, t), ACT.Sigmoid).then_inc(s_sig, 1)

        @block.vector
        def _(dve):
            for i in range(1, nz + ng):
                w.split_lo(dve, i)

        @block.gpsimd
        def _(pool):
            for i in range(nz):
                for c in range(NC):
                    pool.wait_ge(s_silu, NC * i + c + 1)
                    pool.dma_start(scr["z"][c * P:(c + 1) * P, i * UC:(i + 1) * UC], zs[:, c, :]).then_inc(s_out[c], 16)
            for i in range(ng):
                for t in range(2):
                    pool.wait_ge(s_sig, 2 * i + t + 1)
                    pool.dma_start(scr["gb"][2 * i + t], gs[:, t, :]).then_inc(s_gout[t], 16)
            for c in range(NC):
                pool.wait_ge(s_out[c], 16 * nz)
            for t in range(2):
                pool.wait_ge(s_gout[t], 16 * ng)


def stage_ssd(kit, io, out):
    nc, ps = kit.nc, kit.ps
    hF, hB0 = kit.at(O_H, 4, INNER), kit.at(O_H + 4 * INNER, INNER)
    hB1 = kit.at(O_HL, INNER)
    R = kit.at(O_HL + 2048, 4, 512)
    GX, TT, M, XD = (kit.at(O_HL + 4096 + 1024 * j, 2, 512) for j in range(4))
    EX = kit.at(O_TMP, 6, NC, 32)
    DD = kit.at(O_TMP + 960, 2, NC, 32)
    CB = kit.at(O_TMP + 1280, 2, 2, P)
    OF = kit.at(O_TMP + 1792, 2, 2, 256)
    YK = kit.at(O_TMP + 2816, 2, 256)
    DSK = kit.at(O_TMP + 3328, 32)
    SO = kit.at(O_TMP + 3360, 2, 512)
    HT_ = kit.at(O_RAW, 2, 512)
    V1 = kit.at(O_RAW + 1024, 2, 256)
    DT, A = kit.at(O_TMP + 4480, NC, 64), kit.at(O_TMP + 4800, NC, 64)
    X, Bt = kit.at(O_X, NC, INNER), kit.at(O_BC + 5120, NC, G * P)
    BT, CT = kit.at(O_BC, G, T), kit.at(O_BC + 2560, G, T)
    sums = [(kit.const(m), d) for m, d in (("le", 0), ("gt", 0), ("one", 0), ("ge", 1), ("lt", 1), ("one", 1))]
    le, ge, gt, lt = (kit.const(m) for m in ("le", "ge", "gt", "lt"))

    names = ("in", "ex", "exa", "dd", "r", "seg", "g", "a1", "cbp", "cb", "t", "m", "y", "yk", "ev", "xd", "stp",
             "st", "cst")
    (s_in, s_ex, s_exa, s_dd, s_r, s_seg, s_g, s_a1, s_cbp, s_cb, s_t, s_m, s_y, s_yk, s_ev, s_xd, s_stp, s_st,
     s_cst) = (kit.sem("s_" + x) for x in names)
    s_so = [kit.sem(f"s_state_stored{j}") for j in range(2)]

    chunks = [4, 3, 2, 1, 0]
    subs = [(c, g, q) for c in chunks for g in range(G) for q in range(2)]
    NS, NL = len(subs), 32
    ev = lambda j: 6 * j if j <= NL else 6 * NL + 2 * (j - NL)
    ctx_states = [(d, 0, g) for d in range(2) for g in range(G)]
    fwd = [(0, c, g) for c in (1, 2, 3) for g in range(G)]
    bwd = [(1, c, g) for c in (4, 3, 2) for g in range(G)]
    states = ctx_states + fwd + bwd
    NX, NF = len(ctx_states), len(ctx_states) + len(fwd)
    bank_of = lambda x: 7 if x >= NF or x % 2 else 6
    hb = lambda c: (hB0, hB1)[(4 - c) % 2]
    x_at = {}
    for x, (d, c, g) in enumerate(bwd):
        x_at[subs.index((c, g, 0))] = NF + x
    cols = lambda g: slice(g * GW, (g + 1) * GW)
    heads4 = lambda g, q: slice(g * HPG + 4 * q, g * HPG + 4 * q + 4)
    byhead = lambda v, n: v.rearrange("p (h n) -> p h n", h=n)

    with nc.Block() as block:
        @block.sync
        def _(sp):
            sp.dma_start(hF[:, 0, :], io["state_t"][0]).then_inc(s_in, 16)
            sp.dma_start(hB0, io["state_t"][1]).then_inc(s_in, 16)
            sp.dma_start(DSK, io["d_skip"].partition_broadcast(P)).then_inc(s_in, 16)
            for x, (d, c, g) in enumerate(ctx_states):
                sp.wait_ge(s_cst, x + 1)
                sp.dma_start(out["state"][d, cols(g), :].rearrange("(q p) n -> p q n", p=P),
                             SO[:, x % 2, :].rearrange("p (q n) -> p q n", q=4)).then_inc(s_so[x % 2], 16)
            for j in range(2):
                sp.wait_ge(s_so[j], 16 * NX // 2)

        @block.gpsimd
        def _(pool):
            def decays(j):
                c, g, q = subs[j]
                if j >= 2:
                    pool.wait_ge(s_seg, j - 1)
                for d, mask in ((0, le), (1, ge)):
                    hs = heads4(g, q)
                    av = A[:, c, 32 * d + hs.start:32 * d + hs.stop]
                    nc.gpsimd.tensor_tensor(byhead(R[:, 2 * d + j % 2, :], 4), av.unsqueeze(2).broadcast_to([P, 4, P]),
                                            mask.unsqueeze(1).broadcast_to([P, 4, P]), ALU.mult).then_inc(s_r, 1)

            def weigh(x):
                d, c, g = states[x]
                if x >= 2:
                    pool.wait_ge(s_stp, x - 1)
                nc.gpsimd.tensor_tensor(byhead(XD[:, x % 2, :], HPG), byhead(X[:, c, cols(g)], HPG),
                                        DD[:, d, c, g * HPG:(g + 1) * HPG].unsqueeze(2).broadcast_to([P, HPG, HD]),
                                        ALU.mult).then_inc(s_xd, 1)

            pool.wait_ge(s_dd, 2)
            for x in range(NF):
                weigh(x)
            decays(0)
            decays(1)
            pool.wait_ge(s_in, 48)
            for j, (c, g, q) in enumerate(subs):
                if j + 2 < NS:
                    decays(j + 2)
                if j in x_at:
                    weigh(x_at[j])
                if j >= 2:
                    pool.wait_ge(s_ev, ev(j - 1))
                nc.gpsimd.tensor_tensor(byhead(YK[:, j % 2, :], 4), byhead(X[:, c, g * GW + q * 256:g * GW + (q + 1) * 256], 4),
                                        DSK[:, heads4(g, q)].unsqueeze(2).broadcast_to([P, 4, HD]),
                                        ALU.mult).then_inc(s_yk, 1)

        @block.tensor
        def _(pe):
            def state(x):
                d, c, g = states[x]
                pe.wait_ge(s_xd, x + 1)
                if x >= NF:
                    pe.wait_ge(s_st, x - NX)
                elif x >= NX + 2:
                    pe.wait_ge(s_st, x - NX - 1)
                elif x >= 2:
                    pe.wait_ge(s_cst, x - 1)
                b, bt = bank_of(x), Bt[:, c, g * P:(g + 1) * P]
                if x < NX:
                    for q in range(4):
                        last = nc.tensor.matmul(ps[:, b, q * P:(q + 1) * P], XD[:, x % 2, q * P:(q + 1) * P], bt,
                                                start=True, stop=True)
                else:
                    last = nc.tensor.matmul(ps[:, b, :], bt, XD[:, x % 2, :], start=True, stop=True)
                last.then_inc(s_stp, 1)

            def prepare(j):
                c, g, q = subs[j]
                pe.wait_ge(s_r, 2 * j + 2)
                if j >= 2:
                    pe.wait_ge(s_g, j - 1)
                nc.tensor.matmul(ps[:, j % 2, :], gt, R[:, j % 2, :], start=True, stop=False)
                nc.tensor.matmul(ps[:, j % 2, :], lt, R[:, 2 + j % 2, :], start=False, stop=True).then_inc(s_seg, 1)
                if q == 0:
                    gi = j // 2
                    if gi >= 2:
                        pe.wait_ge(s_cb, 2 * (gi - 1))
                    nc.tensor.matmul(ps[:, 4, (gi % 2) * P:(gi % 2 + 1) * P], BT[:, g, c * P:(c + 1) * P],
                                     CT[:, g, c * P:(c + 1) * P], start=True, stop=True).then_inc(s_cbp, 1)

            for n, (mask, d) in enumerate(sums):
                o = ps[:, n // 3, (n % 3) * 160:(n % 3 + 1) * 160]
                last = nc.tensor.matmul(o, mask, A[:, :, 32 * d:32 * d + 32], start=True, stop=True)
            last.then_inc(s_ex, 1)
            for x in range(NF):
                state(x)
            pe.wait_ge(s_exa, 2)
            prepare(0)
            for j, (c, g, q) in enumerate(subs):
                if j + 1 < NS:
                    prepare(j + 1)
                if j in x_at:
                    state(x_at[j])
                if j >= 2:
                    pe.wait_ge(s_ev, ev(j - 1))
                elif j == 0:
                    pe.wait_ge(s_in, 48)
                    pe.wait_ge(s_st, NF - NX)
                if c:
                    pe.wait_ge(s_st, NF - NX + 4 * (4 - c))
                    ct = CT[:, g, c * P:(c + 1) * P]
                    w4 = slice(g * GW + q * 256, g * GW + (q + 1) * 256)
                    nc.tensor.matmul(ps[:, 5 + j % 2, 0:256], ct, hF[:, c - 1, w4], start=True, stop=True)
                    nc.tensor.matmul(ps[:, 5 + j % 2, 256:512], ct, hb(c)[:, w4], start=True, stop=True)
                pe.wait_ge(s_m, j + 1)
                for h in range(4):
                    x0 = g * GW + q * 256 + (h // 2) * P
                    last = nc.tensor.matmul(ps[:, 2 + j % 2, h * P:(h + 1) * P], M[:, j % 2, h * P:(h + 1) * P],
                                            X[:, c, x0:x0 + P], start=True, stop=True)
                last.then_inc(s_y, 1)

        @block.scalar
        def _(act):
            act.wait_ge(s_ex, 1)
            for n in range(2):
                nc.scalar.activation(EX[:, 3 * n:3 * n + 3, :, :].rearrange("p a b c -> p (a b c)"), ps[:, n, 0:480],
                                     ACT.Exp).then_inc(s_exa, 1)
            for x in range(NX):
                act.wait_ge(s_stp, x + 1)
                if x >= 2:
                    act.wait_ge(s_so[x % 2], 16 * (x // 2))
                nc.scalar.activation(SO[:, x % 2, :], ps[:, bank_of(x), :], ACT.Copy).then_inc(s_cst, 1)
            for j, (c, g, q) in enumerate(subs):
                act.wait_ge(s_seg, j + 1)
                if j >= 2:
                    act.wait_ge(s_m, j - 1)
                nc.scalar.activation(GX[:, j % 2, :], ps[:, j % 2, :], ACT.Exp).then_inc(s_g, 1)
                act.wait_ge(s_cb, 2 * (j // 2) + 2)
                for h in range(4):
                    dt = DT[:, c, g * HPG + 4 * q + h:g * HPG + 4 * q + h + 1]
                    nc.scalar.activation(TT[:, j % 2, h * P:(h + 1) * P], CB[:, (j // 2) % 2, 0, :], ACT.Copy,
                                         scale=dt).then_inc(s_a1, 1)

        @block.vector
        def _(dve):
            dve.wait_ge(s_exa, 2)
            for d in range(2):
                nc.vector.tensor_tensor(DD[:, d, :, :], DT[:, :, 32 * d:32 * d + 32], EX[:, 3 * d + 1, :, :],
                                        ALU.mult).then_inc(s_dd, 1)

            def carry(x):
                d, c, g = states[x]
                if d == 0:
                    src, dst = hF[:, c - 1, cols(g)], hF[:, c, cols(g)]
                else:
                    src, dst = hb(c)[:, cols(g)], hb(c - 1)[:, cols(g)]
                    dve.wait_ge(s_y, 8 * (4 - c))
                dec = EX[:, 3 * d + 2, c, g * HPG:(g + 1) * HPG].unsqueeze(2).broadcast_to([P, HPG, HD])
                n = x - NX
                nc.vector.tensor_tensor(byhead(HT_[:, x % 2, :], HPG), byhead(src, HPG), dec, ALU.mult).then_inc(s_dd, 1)
                dve.wait_ge(s_dd, 3 + n)
                dve.wait_ge(s_stp, x + 1)
                nc.vector.tensor_tensor(dst, HT_[:, x % 2, :], ps[:, bank_of(x), :], ALU.add).then_inc(s_st, 1)

            dve.wait_ge(s_in, 48)
            for x in range(NX, NF):
                if x >= NX + 4:
                    dve.wait_ge(s_st, x - NX - 3)
                carry(x)

            def masks(gi):
                dve.wait_ge(s_cbp, gi + 1)
                src = ps[:, 4, (gi % 2) * P:(gi % 2 + 1) * P]
                if gi >= 2:
                    dve.wait_ge(s_a1, 8 * (gi - 1))
                    dve.wait_ge(s_t, 8 * (gi - 1))
                nc.vector.tensor_tensor(CB[:, gi % 2, 0, :], src, le, ALU.mult).then_inc(s_cb, 1)
                nc.vector.tensor_tensor(CB[:, gi % 2, 1, :], src, ge, ALU.mult).then_inc(s_cb, 1)

            def take_y(j):
                c, g, q = subs[j]
                w4 = slice(g * GW + q * 256, g * GW + (q + 1) * 256)
                v = ps[:, 2 + j % 2, :].rearrange("p (a n) -> p a n", a=2)
                n = ev(j)
                dve.wait_ge(s_y, j + 1)
                dve.wait_ge(s_yk, j + 1)
                dst = V1[:, j % 2, :] if c else X[:, c, w4]
                if c:
                    for d in range(2):
                        nc.vector.tensor_tensor(byhead(OF[:, j % 2, d, :], 4), byhead(ps[:, 5 + j % 2, 256 * d:256 * d + 256], 4),
                                                EX[:, 3 * d, c, heads4(g, q)].unsqueeze(2).broadcast_to([P, 4, HD]),
                                                ALU.mult).then_inc(s_ev, 1)
                for e in range(2):
                    o = e * (P + HD)
                    nc.vector.tensor_tensor(dst.rearrange("p (a e n) -> p a e n", a=2, e=2)[:, :, e, :], v[:, :, o:o + HD],
                                            YK[:, j % 2, :].rearrange("p (a e n) -> p a e n", a=2, e=2)[:, :, e, :],
                                            ALU.add).then_inc(s_ev, 1)
                if c:
                    dve.wait_ge(s_ev, n + 4)
                    nc.vector.tensor_tensor(dst, dst, OF[:, j % 2, 0, :], ALU.add).then_inc(s_ev, 1)
                    dve.wait_ge(s_ev, n + 5)
                    nc.vector.tensor_tensor(X[:, c, w4], dst, OF[:, j % 2, 1, :], ALU.add).then_inc(s_ev, 1)

            masks(0)
            for j, (c, g, q) in enumerate(subs):
                if j % 2 and j + 1 < NS:
                    masks((j + 1) // 2)
                dve.wait_ge(s_a1, 4 * j + 4)
                dve.wait_ge(s_cb, 2 * (j // 2) + 2)
                for h in range(4):
                    dt = DT[:, c, 32 + g * HPG + 4 * q + h:32 + g * HPG + 4 * q + h + 1]
                    tt = TT[:, j % 2, h * P:(h + 1) * P]
                    nc.vector.scalar_tensor_tensor(out=tt, in0=CB[:, (j // 2) % 2, 1, :], scalar=dt, in1=tt,
                                                   op0=ALU.mult, op1=ALU.add).then_inc(s_t, 1)
                dve.wait_ge(s_t, 4 * j + 4)
                dve.wait_ge(s_g, j + 1)
                if j >= 2:
                    dve.wait_ge(s_y, j - 1)
                nc.vector.tensor_tensor(M[:, j % 2, :], TT[:, j % 2, :], GX[:, j % 2, :], ALU.mult).then_inc(s_m, 1)
                if j:
                    take_y(j - 1)
                if j in x_at:
                    x = x_at[j]
                    dve.wait_ge(s_st, x - NX - 3)
                    carry(x)
            take_y(NS - 1)


def stage_norm_y(kit, stream, io, scr):
    nc, ps = kit.nc, kit.ps
    X = kit.at(O_X, NC, INNER)
    Z = kit.at(O_RAW, 2, INNER)
    hi, lo = kit.rnd(O_H, KI, T), kit.rnd(O_BC, KI, T)
    nw, ssq, rr = kit.at(O_TMP + 2560, KI), kit.at(O_TMP + 2580, NC * G), kit.at(O_TMP + 2600, NC * G)
    sc, cond = kit.at(O_TMP + 2624, 16), kit.at(O_TMP + 2640, 16)
    sq = kit.at(O_TMP + 2656, GW)
    row, brow = kit.at(O_TMP + 3168, 2, 512), kit.at(O_TMP + 4192, 512)
    WM = kit.at(O_HL, 2, 4096)
    ident = kit.const("ident")
    NM = 8
    (s_in, s_y, s_ms, s_r, s_sq, s_tr, s_hi, s_lo, s_mod, s_modr, s_b) = (
        kit.sem("n_" + x) for x in ("in", "y", "mean", "root", "squares", "turned", "hi", "lo", "mod", "mod_row", "bias"))
    s_z = [kit.sem(f"n_z{j}") for j in range(2)]
    s_w = [kit.sem(f"n_w{j}") for j in range(2)]
    s_mo = [kit.sem(f"n_mod_stored{j}") for j in range(2)]
    mods = [[0, 1], [2, 3], [4, 5], [6, 7], []]
    w = stream.section(0)

    with nc.Block() as block:
        @block.sync
        def _(sp):
            sp.dma_start(nw, io["ssd_nw"]).then_inc(s_in, 16)
            sp.dma_start(cond, io["cond"]).then_inc(s_in, 16)
            for c in range(2):
                sp.dma_start(Z[:, c, :], scr["z"][c * P:(c + 1) * P, :]).then_inc(s_z[c], 16)
            for m in range(NM):
                if m >= 2:
                    sp.wait_ge(s_mod, m - 1)
                sp.dma_start(WM[:, m % 2, :], io["w_mod"][4 + m]).then_inc(s_w[m % 2], 16)
                if m % 2 == 0 and m // 2 + 2 < NC:
                    c = m // 2 + 2
                    sp.wait_ge(s_y, c - 1)
                    sp.dma_start(Z[:, c % 2, :], scr["z"][c * P:(c + 1) * P, :]).then_inc(s_z[c % 2], 16)
            sp.wait_ge(s_y, NC)
            for i in w.to_load():
                w.load(sp, i)

        @block.gpsimd
        def _(pool):
            for m in range(NM):
                if m:
                    pool.wait_ge(s_modr, m)
                pool.dma_start(brow[0:2, :], io["b_mod"][:, 2048 + 512 * m:2560 + 512 * m].partition_broadcast(2)).then_inc(s_b, 16)
                pool.wait_ge(s_modr, m + 1)
                pool.dma_start(scr["mod"][:, 512 * m:512 * (m + 1)], row[0:2, m % 2, :]).then_inc(s_mo[m % 2], 16)
            for j in range(2):
                pool.wait_ge(s_mo[j], 16 * NM // 2)

        @block.tensor
        def _(pe):
            pe.wait_ge(s_sq, 1)
            for c in range(NC):
                for m in mods[c]:
                    pe.wait_ge(s_w[m % 2], 16 * (m // 2 + 1))
                    if m >= 2:
                        pe.wait_ge(s_modr, m - 1)
                    for k in range(KD):
                        last = nc.tensor.matmul(ps[0:2, 4 + m % 2, :], sc.rearrange("p (k s) -> p k s", s=2)[:, k, :],
                                                WM[:, m % 2, k * 512:(k + 1) * 512], start=(k == 0), stop=(k == KD - 1))
                    last.then_inc(s_mod, 1)
                pe.wait_ge(s_r, 4 * (c + 1))
                for g in range(G):
                    if c:
                        pe.wait_ge(s_lo, 4 * (G * (c - 1) + g + 1))
                    for q in range(4):
                        k = 4 * g + q
                        last = nc.tensor.transpose(ps[:, g, q * P:(q + 1) * P], X[:, c, k * P:(k + 1) * P], ident)
                    last.then_inc(s_tr, 1)

        @block.scalar
        def _(act):
            act.wait_ge(s_in, 32)
            nc.scalar.activation(sc, cond, ACT.Silu).then_inc(s_sq, 1)
            n = 1
            for c in range(NC):
                act.wait_ge(s_y, c + 1)
                for g in range(G):
                    if n > 1:
                        act.wait_ge(s_sq, n)
                    nc.scalar.activation(sq, X[:, c, g * GW:(g + 1) * GW], ACT.Square,
                                         accum_out=ssq[:, c * G + g:c * G + g + 1]).then_inc(s_sq, 1)
                    n += 1
                act.wait_ge(s_ms, 2 * c + 2)
                nc.scalar.activation(rr[:, c * G:(c + 1) * G], rr[:, c * G:(c + 1) * G], ACT.Sqrt).then_inc(s_sq, 1)
                n += 1
                for g in range(G):
                    act.wait_ge(s_tr, G * c + g + 1)
                    for q in range(4):
                        k = 4 * g + q
                        nc.scalar.activation(hi[:, k, c * P:(c + 1) * P], ps[:, g, q * P:(q + 1) * P],
                                             ACT.Copy, scale=nw[:, k:k + 1]).then_inc(s_hi, 1)
            act.wait_ge(s_mod, NM)
            w.split_hi(act, 0)

        @block.vector
        def _(dve):
            def gated(c):
                dve.wait_ge(s_z[c % 2], 16 * (c // 2 + 1))
                nc.vector.tensor_tensor(X[:, c, :], X[:, c, :], Z[:, c % 2, :], ALU.mult).then_inc(s_y, 1)

            def modulation_row(m):
                dve.wait_ge(s_mod, m + 1)
                dve.wait_ge(s_b, 16 * (m + 1))
                if m >= 2:
                    dve.wait_ge(s_mo[m % 2], 16 * (m // 2))
                nc.vector.tensor_tensor(row[0:2, m % 2, :], ps[0:2, 4 + m % 2, :], brow[0:2, :], ALU.add).then_inc(s_modr, 1)

            gated(0)
            for c in range(NC):
                dve.wait_ge(s_sq, 1 + 5 * c + 4)
                dve.wait_ge(s_y, c + 1)
                sl = slice(c * G, (c + 1) * G)
                nc.vector.tensor_scalar(ssq[:, sl], ssq[:, sl], 1.0 / GW, EPS, ALU.mult, ALU.add).then_inc(s_ms, 1)
                dve.wait_ge(s_ms, 2 * c + 1)
                nc.vector.reciprocal(rr[:, sl], ssq[:, sl]).then_inc(s_ms, 1)
                dve.wait_ge(s_sq, 1 + 5 * c + 5)
                for g in range(G):
                    v = X[:, c, g * GW:(g + 1) * GW]
                    nc.vector.tensor_scalar(v, v, rr[:, c * G + g:c * G + g + 1], None, ALU.mult).then_inc(s_r, 1)
                if c + 1 < NC:
                    gated(c + 1)
                for m in mods[c]:
                    modulation_row(m)
                for k in range(KI):
                    dve.wait_ge(s_hi, KI * c + 4 * (k // 4) + 4)
                    src, g, q = slice(c * P, (c + 1) * P), k // 4, k % 4
                    nc.vector.scalar_tensor_tensor(out=lo[:, k, src], in0=ps[:, g, q * P:(q + 1) * P],
                                                   scalar=nw[:, k:k + 1], in1=hi[:, k, src].bitcast(F32),
                                                   op0=ALU.mult, op1=ALU.subtract).then_inc(s_lo, 1)
            w.split_lo(dve, 0)


def stage_branch_b(kit, stream, io, scr):
    nc, ps = kit.nc, kit.ps
    y = [kit.rnd(o, KI, T) for o in (O_H, O_BC)]
    MG = kit.at(O_MG, KD, T)
    hi, lo = kit.rnd(O_X, KD, T), kit.rnd(O_X + 5120, KD, T)
    gate, v = kit.at(O_TMP + 2560, 2, T), kit.at(O_TMP + 3840, 2, T)
    w = stream.section(8)
    s_g = [kit.sem(f"b_gate{j}") for j in range(2)]
    s_v, s_hi, s_lo = kit.sem("b_merged"), kit.sem("b_hi"), kit.sem("b_lo")
    with nc.Block() as block:
        @block.sync
        def _(sp):
            for i in range(8):
                if i >= 2:
                    sp.wait_ge(s_v, 2 * (i - 2) + 1)
                sp.dma_start(gate[:, i % 2, :], scr["gb"][i]).then_inc(s_g[i % 2], 16)
                w.load(sp, i + 2)

        @block.tensor
        def _(pe):
            for i in range(8):
                w.ready(pe, i)
                if i >= 2:
                    pe.wait_ge(s_v, 2 * (i - 2) + 1)
                feature_tile(nc, w.parts(i, KI), 0, y, lambda h: halves(kit, i % 2)[:, h, :], KI).then_inc(w.used, 1)

        @block.scalar
        def _(act):
            for i in range(8):
                if w.exists(i + 1):
                    w.split_hi(act, i + 1)
                act.wait_ge(s_v, 2 * i + 2)
                nc.scalar.activation(hi[:, i, :], v[:, i % 2, :], ACT.Copy).then_inc(s_hi, 1)

        @block.vector
        def _(dve):
            for i in range(8):
                if w.exists(i + 1):
                    w.split_lo(dve, i + 1)
                dve.wait_ge(*w.done(i))
                dve.wait_ge(s_g[i % 2], 16 * (i // 2 + 1))
                nc.vector.tensor_tensor(two(v[:, i % 2, :]), halves(kit, i % 2), two(gate[:, i % 2, :]), ALU.mult).then_inc(s_v, 1)
                dve.wait_ge(s_v, 2 * i + 1)
                nc.vector.tensor_tensor(v[:, i % 2, :], v[:, i % 2, :], MG[:, i, :], ALU.add).then_inc(s_v, 1)
                dve.wait_ge(s_hi, i + 1)
                nc.vector.tensor_tensor(lo[:, i, :], v[:, i % 2, :], hi[:, i, :].bitcast(F32), ALU.subtract).then_inc(s_lo, 1)
                dve.wait_ge(s_lo, i + 1)


T_G2, T_FN, T_RT = O_TMP, O_TMP + 2048, O_TMP + 3072


class Routing:

    def __init__(self, kit):
        self.slot = [kit.at(T_RT + 8 * k, NC).bitcast(U32) for k in range(2)]
        self.weight = kit.at(T_RT + 16, 2, NC)
        self.table = kit.at(T_RT + 26, NMB + 1)[0:1].bitcast(I32)
        self.bias = kit.at(T_RT + 64, NE)
        self.work = T_RT + 64 + NE


def stage_out(kit, stream, io, scr, ex):
    nc, ps = kit.nc, kit.ps
    x2, h2 = kit.at(O_H, NC, D), kit.at(O_H + 5120, NC, D)
    merged = [kit.rnd(o, KD, T) for o in (O_X, O_X + 5120)]
    G1, S2, A2, N2 = kit.at(O_BC, 2, D), kit.at(O_BC + 2048, 2, D), kit.at(O_BC + 4096, 2, D), kit.at(O_BC + 6144, D)
    G2, FN = kit.at(T_G2, 2, D), kit.at(T_FN, D)
    hT = kit.at(O_MG, 2, KD, P)
    rw = kit.at(O_MG + 2048, KD, NE)
    sq = kit.at(O_MG + 2176, D)
    prod = kit.at(O_MG + 3200, 2, UC)
    ssq, rr = kit.at(O_MG + 3712, NC), kit.at(O_MG + 3720, NC)
    score = kit.at(O_MG + 3728, NC, NE)
    ident = kit.const("ident")
    w = stream.section(4)
    (s_in, s_x, s_pe, s_x2, s_p, s_a2, s_sq, s_rt, s_ms, s_h2, s_tr, s_ht, s_rr, s_sc) = (
        kit.sem("o_" + v) for v in ("in", "x", "chunk", "x2", "product", "scale", "squares", "root", "mean", "h2",
                                    "turned", "ht", "router", "scores"))
    with nc.Block() as block:
        @block.sync
        def _(sp):
            sp.dma_start(x2, scr["xp"].rearrange("(c p) d -> p c d", p=P)).then_inc(s_x, 16)
            for q, dst in enumerate((G1, S2, A2, G2)):
                for st in range(2):
                    sp.dma_start(dst[:, st, :], scr["mod"][st:st + 1, q * D:(q + 1) * D].partition_broadcast(P)).then_inc(s_in, 16)
            sp.dma_start(N2, io["norm2"].partition_broadcast(P)).then_inc(s_in, 16)
            sp.dma_start(FN, io["fnorm"].partition_broadcast(P)).then_inc(s_in, 16)
            sp.dma_start(Routing(kit).bias, io["router_b"].partition_broadcast(P)).then_inc(s_in, 16)
            sp.dma_start(rw, io["router_w"].rearrange("p (k e) -> p k e", k=KD)).then_inc(s_in, 16)
            for i in w.to_load():
                w.load(sp, i)
            sp.wait_ge(*w.done(3))
            for q in range(6):
                ex.load(sp, io, 0, q)

        @block.tensor
        def _(pe):
            def project(i, c):
                if i:
                    pe.wait_ge(s_p, NC * (i - 1) + c + 1)
                last = token_tile(nc, w.parts(i, KD), c, merged, ps[:, c, 0:UC])
                last.then_inc(s_pe if c < NC - 1 else w.used, 1)

            def turn(c):
                pe.wait_ge(s_h2, 2 * c + 2)
                if c:
                    pe.wait_ge(s_ht, c)
                for k in range(KD):
                    last = nc.tensor.transpose(ps[:, 5 + k // 4, (k % 4) * P:(k % 4 + 1) * P], h2[:, c, k * P:(k + 1) * P], ident)
                last.then_inc(s_tr, 1)

            def route(c):
                pe.wait_ge(s_ht, c + 1)
                for k in range(KD):
                    last = nc.tensor.matmul(ps[:, 7, c * NE:(c + 1) * NE], hT[:, c % 2, k, :], rw[:, k, :],
                                            start=(k == 0), stop=(k == KD - 1))
                last.then_inc(s_rr, 1)

            for i in range(3):
                w.ready(pe, i)
                for c in range(NC):
                    project(i, c)
            w.ready(pe, 3)
            pe.wait_ge(s_in, 192)
            for c in range(NC):
                project(3, c)
                if c >= 2:
                    turn(c - 2)
                if c >= 3:
                    route(c - 3)
            turn(3)
            route(2)
            turn(4)
            route(3)
            route(4)

        @block.scalar
        def _(act):
            for i in range(3):
                w.split_hi(act, i + 1)

            def take_turned(c):
                act.wait_ge(s_tr, c + 1)
                if c >= 2:
                    act.wait_ge(s_rr, c - 1)
                nc.scalar.activation(hT[:, c % 2, :, :].rearrange("p k n -> p (k n)"),
                                     ps[:, 5:7, :].rearrange("p a b -> p (a b)"), ACT.Copy).then_inc(s_ht, 1)

            for c in range(NC):
                act.wait_ge(s_x2, NC * 3 + c + 1)
                if c:
                    act.wait_ge(s_sq, c)
                nc.scalar.activation(sq, x2[:, c, :], ACT.Square, accum_out=ssq[:, c:c + 1]).then_inc(s_sq, 1)
                act.wait_ge(s_ms, 2 * c + 2)
                nc.scalar.activation(rr[:, c:c + 1], rr[:, c:c + 1], ACT.Sqrt).then_inc(s_rt, 1)
                if c >= 2:
                    take_turned(c - 2)
            take_turned(3)
            take_turned(4)
            act.wait_ge(s_rr, NC)
            nc.scalar.activation(score.rearrange("p c e -> p (c e)"), ps[:, 7, 0:NC * NE], ACT.Sigmoid).then_inc(s_sc, 1)

        @block.vector
        def _(dve):
            w.split_lo(dve, 1)
            dve.wait_ge(s_in, 192)
            dve.wait_ge(s_x, 16)
            for st in range(2):
                nc.vector.scalar_tensor_tensor(out=A2[:, st, :], in0=A2[:, st, :], scalar=1.0, in1=N2,
                                               op0=ALU.add, op1=ALU.mult).then_inc(s_a2, 1)

            def norm(c):
                st = min(c, 1)
                dve.wait_ge(s_sq, c + 1)
                nc.vector.tensor_scalar(ssq[:, c:c + 1], ssq[:, c:c + 1], 1.0 / D, EPS, ALU.mult, ALU.add).then_inc(s_ms, 1)
                dve.wait_ge(s_ms, 2 * c + 1)
                nc.vector.reciprocal(rr[:, c:c + 1], ssq[:, c:c + 1]).then_inc(s_ms, 1)
                dve.wait_ge(s_rt, c + 1)
                dve.wait_ge(s_a2, 2)
                nc.vector.scalar_tensor_tensor(out=h2[:, c, :], in0=x2[:, c, :], scalar=rr[:, c:c + 1], in1=A2[:, st, :],
                                               op0=ALU.mult, op1=ALU.mult).then_inc(s_h2, 1)
                dve.wait_ge(s_h2, 2 * c + 1)
                nc.vector.tensor_tensor(h2[:, c, :], h2[:, c, :], S2[:, st, :], ALU.add).then_inc(s_h2, 1)

            for i in range(4):
                if i and i + 1 < 4:
                    w.split_lo(dve, i + 1)
                cols = slice(i * UC, (i + 1) * UC)
                for c in range(NC):
                    n = NC * i + c
                    if c < NC - 1:
                        dve.wait_ge(s_pe, (NC - 1) * i + c + 1)
                    else:
                        dve.wait_ge(*w.done(i))
                    nc.vector.tensor_tensor(prod[:, n % 2, :], ps[:, c, 0:UC], G1[:, min(c, 1), cols], ALU.mult).then_inc(s_p, 1)
                    dve.wait_ge(s_p, n + 1)
                    nc.vector.tensor_tensor(x2[:, c, cols], x2[:, c, cols], prod[:, n % 2, :], ALU.add).then_inc(s_x2, 1)
                    if i == 3 and c:
                        norm(c - 1)
            norm(NC - 1)


def stage_route(kit, io, scr, ex):
    nc, ps = kit.nc, kit.ps
    r = Routing(kit)
    h2 = kit.at(O_H + 5120, NC, D)
    score = kit.at(O_MG + 3728, NC, NE)
    at = [r.work]

    def take(*dims):
        n = 1
        for d in dims:
            n *= d
        at[0] += n
        return kit.at(at[0] - n, *dims)

    sel, selm, m1, m2, tmp, slot = (take(NC, NE) for _ in range(6))
    q20 = [take(NC * NG) for _ in range(7)]
    five, gmax = take(NC), take(NC)
    cnt, ext, pre, ca, cb = (take(NE) for _ in range(5))
    over = take(10, NE)
    tabf = take(NMB + 1)
    w12 = r.weight
    sbf = take(NC * NE // 2).bitcast(BF16).rearrange("p (c e) -> p c e", c=NC)
    ltb, oneb = take(P // 2).bitcast(BF16), take(P // 2).bitcast(BF16)
    assert at[0] <= O_MG
    s_v, s_pe, s_ready, s_mask = kit.sem("r_steps"), kit.sem("r_ranks"), kit.sem("r_slots"), kit.sem("r_chosen")
    s_sc = kit.sem("r_scattered")
    pri16, pri4, e128, thr = (kit.const(n, k) for n, k in (("pri16", NE), ("pri4", NG), ("e128", NE), ("thr", 5)))
    col = kit.const("col", 26)
    bc = lambda v, n: v.unsqueeze(2).broadcast_to([P, v.shape[1], n])
    over_c = lambda v: v.unsqueeze(1).broadcast_to([P, NC, v.shape[1]])

    ex.parts()
    zero = Pair(None, 0)
    with nc.Block() as block:
        @block.sync
        def _(sp):
            for q in range(3):
                sp.wait_ge(ex.lo_ready, q + 1)
                ex.load(sp, io, 1, q)

        @block.scalar
        def _(act):
            for q in range(3):
                ex.split_hi(act, 0, zero, q)

        @block.vector
        def _(dve):
            ch = Chain(dve, s_v)
            tt = nc.vector.tensor_tensor

            def do(ins):
                ch.step(ins)
                ch.sync()

            def first_of(out, values, pri, width):
                do(nc.vector.tensor_reduce(five, values, AX.X, ALU.max))
                do(tt(out, values, bc(five, width), ALU.is_equal))
                do(tt(out, out, over_c(pri), ALU.mult))
                do(nc.vector.tensor_reduce(gmax, out, AX.X, ALU.max))
                do(tt(out, out, bc(gmax, width), ALU.is_equal))

            do(nc.vector.tensor_copy(ltb, kit.const("lt")))
            do(nc.vector.tensor_copy(oneb, kit.const("one")))
            do(tt(sel, score, over_c(r.bias), ALU.add))
            v = sel.rearrange("p c (g e) -> p (c g) e", e=4)
            hi1, hi2, lo1, lo2, best, gs, keep = q20
            for o, a, op in ((hi1, 0, ALU.max), (lo1, 0, ALU.min), (hi2, 2, ALU.max), (lo2, 2, ALU.min)):
                do(tt(o, v[:, :, a], v[:, :, a + 1], op))
            do(tt(gs, hi1, hi2, ALU.min))
            do(tt(lo1, lo1, lo2, ALU.max))
            do(tt(gs, gs, lo1, ALU.max))
            do(tt(hi1, hi1, hi2, ALU.max))
            do(tt(gs, hi1, gs, ALU.add))
            best3 = best.rearrange("p (c g) -> p c g", c=NC)
            first_of(best3, gs.rearrange("p (c g) -> p c g", c=NC), pri4, NG)
            do(nc.vector.tensor_scalar(keep, best, BIG, -BIG, ALU.mult, ALU.add))
            sm = selm.rearrange("p c (g e) -> p (c g) e", e=4)
            do(tt(sm, v, bc(best, 4), ALU.mult))
            do(tt(sm, sm, bc(keep, 4), ALU.add))
            first_of(m1, selm, pri16, NE)
            do(nc.vector.scalar_tensor_tensor(out=selm, in0=m1, scalar=-2.0 * BIG, in1=selm, op0=ALU.mult, op1=ALU.add))
            first_of(m2, selm, pri16, NE)
            do(tt(tmp, m1, m2, ALU.add))
            nc.vector.tensor_copy(sbf, tmp).then_inc(s_mask, 1)
            for k, m in enumerate((m1, m2)):
                do(tt(tmp, m, score, ALU.mult) if k else tt(slot, m, score, ALU.mult))
            do(nc.vector.tensor_reduce(w12[:, 0, :], slot, AX.X, ALU.add))
            do(nc.vector.tensor_reduce(w12[:, 1, :], tmp, AX.X, ALU.add))
            do(tt(five, w12[:, 0, :], w12[:, 1, :], ALU.add))
            do(nc.vector.reciprocal(five, five))
            do(tt(w12, w12, five.unsqueeze(1).broadcast_to([P, 2, NC]), ALU.mult))
            dve.wait_ge(s_pe, 1)
            do(nc.vector.tensor_copy(cnt, ps[:, 1, 0:NE]))
            do(nc.vector.tensor_scalar(ext, cnt, 128.0, None, ALU.is_gt))
            for m in range(2, NC):
                do(nc.vector.scalar_tensor_tensor(out=ext, in0=cnt, scalar=128.0 * m, in1=ext, op0=ALU.is_gt, op1=ALU.add))
            src, dst = ext, ca
            for sh in (1, 2, 4, 8):
                do(nc.vector.tensor_copy(dst[:, 0:sh], src[:, 0:sh]))
                do(tt(dst[:, sh:NE], src[:, sh:NE], src[:, 0:NE - sh], ALU.add))
                src, dst = dst, (cb if dst is ca else ca)
            cum = src
            do(tt(pre, cum, ext, ALU.subtract))
            do(nc.vector.tensor_scalar(pre, pre, 128.0, 16.0 * 128 - 128, ALU.mult, ALU.add))
            rank = ps[:, 0, 0:NC * NE].rearrange("p (c e) -> p c e", c=NC)
            do(nc.vector.tensor_copy(tmp, rank))
            do(tt(slot, tmp, over_c(pre), ALU.add))
            do(tt(pre, e128, pre, ALU.subtract))
            do(nc.vector.scalar_tensor_tensor(out=tmp, in0=tmp, scalar=128.0, in1=over_c(pre), op0=ALU.is_lt, op1=ALU.mult))
            do(tt(slot, slot, tmp, ALU.add))
            for k, m in enumerate((m1, m2)):
                do(tt(tmp, m, slot, ALU.mult))
                do(nc.vector.tensor_reduce(five, tmp, AX.X, ALU.add))
                do(nc.vector.tensor_copy(r.slot[k], five))
            one = lambda v: v[0:1]
            do(tt(one(over), one(col)[:, 0:10].unsqueeze(2).broadcast_to([1, 10, NE]),
                  one(cum).unsqueeze(1).broadcast_to([1, 10, NE]), ALU.is_ge))
            do(nc.vector.tensor_reduce(one(tabf)[:, NE:NMB], one(over), AX.X, ALU.add))
            do(nc.vector.tensor_scalar(one(tabf)[:, NE:NMB], one(tabf)[:, NE:NMB], NE - 1.0, None, ALU.min))
            do(nc.vector.tensor_copy(one(tabf)[:, 0:NE], one(col)[:, 0:NE]))
            do(nc.vector.tensor_scalar(one(five), one(thr), one(cum)[:, NE - 1:NE], None, ALU.is_lt))
            do(nc.vector.tensor_reduce(one(tabf)[:, NMB:NMB + 1], one(five), AX.X, ALU.add))
            do(nc.vector.tensor_scalar(one(tabf)[:, NMB:NMB + 1], one(tabf)[:, NMB:NMB + 1], NE / 2.0 - 2.0, None, ALU.add))
            nc.vector.tensor_copy(r.table, one(tabf)).then_inc(s_ready, 1)

        @block.tensor
        def _(pe):
            pe.wait_ge(s_mask, 1)
            for c in range(NC):
                for d in range(c):
                    nc.tensor.matmul(ps[:, 0, c * NE:(c + 1) * NE], oneb, sbf[:, d, :], start=(d == 0), stop=False)
                nc.tensor.matmul(ps[:, 0, c * NE:(c + 1) * NE], ltb, sbf[:, c, :], start=(c == 0), stop=True)
            for c in range(NC):
                last = nc.tensor.matmul(ps[:, 1, 0:NE], oneb, sbf[:, c, :], start=(c == 0), stop=(c == NC - 1))
            last.then_inc(s_pe, 1)

        @block.gpsimd
        def _(pool):
            for q in range(3):
                ex.split_lo(pool, 0, zero, q, ops=nc.gpsimd)
            pool.wait_ge(s_ready, 1)
            for c in range(NC):
                for k in range(2):
                    pool.indirect_dma_start(out=scr["xs"], out_offset=bass.IndirectOffsetOnAxis(ap=r.slot[k][:, c:c + 1], axis=0),
                                            in_=h2[:, c, :], in_offset=None).then_inc(s_sc, 16)
            pool.wait_ge(s_sc, 16 * 2 * NC)


class Pair:

    def __init__(self, register, constant):
        self.register, self.constant = register, constant

    def times(self, a, b):
        b += a * self.constant
        return b if self.register is None else self.register * a + b

    def plus(self, n):
        return Pair(self.register, self.constant + n)


def is_block(u, j, b):
    return j.register is None and 2 * j.constant + u == b


class Experts:

    def __init__(self, kit):
        self.kit, self.nc = kit, kit.nc
        self.raw = [kit.at(O_RAW + UNIT * q, UNIT) for q in range(6)]
        self.rows = O_X + 6 * UNIT
        self.loaded = [kit.sem(f"e_unit_loaded{q}") for q in range(6)]
        self.hi_ready, self.lo_ready, self.used = (kit.sem("e_" + n) for n in ("hi_ready", "lo_ready", "unit_used"))

    def parts(self):
        self.hi, self.lo = self.kit.rnd(O_X, 3, UNIT), self.kit.rnd(O_X + 3 * UNIT, 3, UNIT)

    def source(self, io, e, q):
        w = io[("wg", "wu", "wd")[q // 2]]
        src = w[e] if isinstance(e, int) else w[bass.ds(e, 1)].rearrange("a p d -> (a p) d")
        return src[:, (q % 2) * UNIT:(q % 2 + 1) * UNIT]

    def load(self, eng, io, e, q):
        eng.dma_start(self.raw[q], self.source(io, e, q)).then_inc(self.loaded[q], 16)

    def index(self, u, j, q, more=0):
        return q + more if is_block(u, j, 0) else j.times(12, 6 * u + q - 2 + more)

    def through(self, u, j, q):
        return self.index(u, j, q, 1)

    def slot_free(self, u, j, q):
        if q < 3 and (is_block(u, j, 0) or is_block(u, j, 1)):
            return (4, 2, 3)[q] if u else None
        return self.index(u, j, q, -2)

    def split_hi(self, act, u, j, q, free=None):
        if free is None:
            free = self.slot_free(u, j, q)
        act.wait_ge(self.loaded[q], j.times(32, 16 * (u + 1 if q < 4 else u)))
        if free is not None:
            act.wait_ge(self.used, free)
        self.nc.scalar.activation(self.hi[:, q % 3, :], self.raw[q], ACT.Copy).then_inc(self.hi_ready, 1)

    def split_lo(self, dve, u, j, q, free=None, hi_ready=None, ops=None):
        if free is None:
            free = self.slot_free(u, j, q)
            hi_ready = self.index(u, j, q, 1)
        dve.wait_ge(self.hi_ready, hi_ready)
        if free is not None:
            dve.wait_ge(self.used, free)
        (ops or self.nc.vector).tensor_tensor(self.lo[:, q % 3, :], self.raw[q], self.hi[:, q % 3, :].bitcast(F32),
                                     ALU.subtract).then_inc(self.lo_ready, 1)


def stage_experts(kit, io, scr, ex):
    nc, ps = kit.nc, kit.ps
    r = Routing(kit)
    XB, YB = kit.at(ex.rows, 2, D), kit.at(ex.rows + 2048, 2, D)
    AB = kit.at(ex.rows + 4096, FE)
    HB = [kit.rnd(O_MG + 1024 * i, KD, P) for i in range(2)]
    AT_ = [kit.rnd(O_MG + 2048 + 512 * i, 4, P) for i in range(2)]
    ident = kit.const("ident")
    rows_loaded, y_stored = ([kit.sem(f"e_{n}{u}") for u in range(2)] for n in ("rows_loaded", "y_stored"))
    (rows_turned, rows_hi, rows_lo, silu, product, product_turned, product_hi, product_lo, y_low, y_high, y_free) = (
        kit.sem("e_" + n) for n in ("rows_turned", "rows_hi", "rows_lo", "silu", "product", "product_turned",
                                    "product_hi", "product_lo", "y_low", "y_high", "y_free"))
    xs = scr["xs"].rearrange("(b p) d -> b p d", p=P)
    ys = scr["ys"].rearrange("(b p) d -> b p d", p=P)
    row = lambda ap: ap.rearrange("a p d -> (a p) d")
    inner = lambda eng: eng.value_load(r.table[0:1, NMB:NMB + 1], min_val=NE // 2 - 2, max_val=NMB // 2 - 2)
    expert = lambda eng, b: eng.value_load(r.table[0:1, bass.ds(b, 1)], min_val=0, max_val=NE - 1)
    after = lambda u, j: (1, j) if u == 0 else (0, j.plus(1))
    before = lambda u, j: (1, j.plus(-1)) if u == 0 else (0, j)
    count = lambda u, j, more=0: j.times(2, u + 1 + more)
    zero = Pair(None, 0)

    with nc.Block() as block:
        @block.sync
        def _(sp):
            n = inner(sp)
            last_pair = Pair(n, 1)
            sp.dma_start(XB[:, 0, :], xs[0]).then_inc(rows_loaded[0], 16)
            sp.dma_start(XB[:, 1, :], xs[1]).then_inc(rows_loaded[1], 16)
            sp.wait_ge(ex.lo_ready, 4)
            ex.load(sp, io, 1, 3)
            sp.wait_ge(rows_turned, 1)
            sp.dma_start(XB[:, 0, :], xs[2]).then_inc(rows_loaded[0], 16)

            def load_step(u, j, is_last=False):
                e = expert(sp, j.times(2, u))
                d = expert(sp, j.times(2, u - 1))
                for q in range(6):
                    sp.wait_ge(ex.lo_ready, ex.index(u, j, q, -5))
                    ex.load(sp, io, e if q < 4 else d, q)
                    if q == 3 and not is_last:
                        v, jv = after(u, j)
                        sp.wait_ge(rows_turned, count(u, j, -1))
                        sp.dma_start(XB[:, v, :], row(xs[bass.ds(j.times(2, u + 1), 1)])).then_inc(rows_loaded[v], 16)
                return e

            with sp.Fori(0, n) as i:
                for u in range(2):
                    load_step(u, Pair(i, 1))
            load_step(0, last_pair)
            e = load_step(1, last_pair, is_last=True)
            for q in (4, 5):
                sp.wait_ge(ex.lo_ready, last_pair.times(12, 5 + q))
                ex.load(sp, io, e, q)

        @block.gpsimd
        def _(pool):
            n = inner(pool)

            def store(u, j):
                pool.wait_ge(y_low, count(u, j))
                pool.wait_ge(y_high, count(u, j))
                pool.dma_start(row(ys[bass.ds(j.times(2, u), 1)]), YB[:, u, :]).then_inc(y_stored[u], 16)
                pool.wait_ge(y_stored[u], j.times(16, 16))
                pool.sem_inc(y_free, 1)

            store(0, zero)
            store(1, zero)
            with pool.Fori(0, n) as i:
                for u in range(2):
                    store(u, Pair(i, 1))
            store(0, Pair(n, 1))
            store(1, Pair(n, 1))

        @block.tensor
        def _(pe):
            n = inner(pe)
            last_pair = Pair(n, 1)

            def unit_ready(ready):
                pe.wait_ge(ex.hi_ready, ready)
                pe.wait_ge(ex.lo_ready, ready)

            def turn_rows(u, j):
                pe.wait_ge(rows_loaded[u], j.times(16, 16))
                if not (is_block(u, j, 0) or is_block(u, j, 1)):
                    pe.wait_ge(product_lo, count(u, j, -2))
                for k in range(KD):
                    last = nc.tensor.transpose(ps[:, 6 + k // 4, (k % 4) * P:(k % 4 + 1) * P], XB[:, u, k * P:(k + 1) * P], ident)
                last.then_inc(rows_turned, 1)

            def gate_and_up(u, j):
                pe.wait_ge(rows_hi, count(u, j))
                pe.wait_ge(rows_lo, count(u, j))
                if not (is_block(u, j, 0) or is_block(u, j, 1)):
                    pe.wait_ge(product, count(u, j, -2))
                for q in range(4):
                    unit_ready(ex.through(u, j, q))
                    hi, lo = ex.hi[:, q % 3, :], ex.lo[:, q % 3, :]
                    o = ps[:, 2 * u + q // 2, :]
                    for k in range(4):
                        kk, cols = 4 * (q % 2) + k, slice(k * FE, (k + 1) * FE)
                        nc.tensor.matmul(o, HB[0][:, kk, :], hi[:, cols], start=(kk == 0), stop=False)
                        nc.tensor.matmul(o, HB[0][:, kk, :], lo[:, cols], start=False, stop=False)
                        last = nc.tensor.matmul(o, HB[1][:, kk, :], hi[:, cols], start=False, stop=(kk == KD - 1))
                    last.then_inc(ex.used, 1)

            def turn_product(u, j, is_last=False):
                if not is_last:
                    pe.wait_ge(rows_lo, count(u, j, 1))
                pe.wait_ge(product, count(u, j))
                for k in range(4):
                    last = nc.tensor.transpose(ps[:, 6, k * P:(k + 1) * P], AB[:, k * P:(k + 1) * P], ident)
                last.then_inc(product_turned, 1)

            def down(u, j, ready):
                pe.wait_ge(product_hi, count(u, j))
                pe.wait_ge(product_lo, count(u, j))
                if not is_block(u, j, 0):
                    pe.wait_ge(y_low, count(u, j, -1))
                    pe.wait_ge(y_high, count(u, j, -1))
                for q in (4, 5):
                    unit_ready(ready[q - 4])
                    hi, lo = ex.hi[:, q % 3, :], ex.lo[:, q % 3, :]
                    for k in range(2):
                        kk = 2 * (q - 4) + k
                        for h in range(2):
                            o, cols = ps[:, 4 + h, :], slice(k * D + h * 512, k * D + (h + 1) * 512)
                            nc.tensor.matmul(o, AT_[0][:, kk, :], hi[:, cols], start=(kk == 0), stop=False)
                            nc.tensor.matmul(o, AT_[0][:, kk, :], lo[:, cols], start=False, stop=False)
                            last = nc.tensor.matmul(o, AT_[1][:, kk, :], hi[:, cols], start=False, stop=(kk == 3))
                    last.then_inc(ex.used, 1)

            def step(u, j, is_last=False):
                gate_and_up(u, j)
                if not is_last:
                    turn_rows(*after(u, j))
                if not is_block(u, j, 0):
                    down(*before(u, j), [ex.through(u, j, q) for q in (4, 5)])
                turn_product(u, j, is_last)

            turn_rows(0, zero)
            step(0, zero)
            step(1, zero)
            with pe.Fori(0, n) as i:
                for u in range(2):
                    step(u, Pair(i, 1))
            step(0, last_pair)
            step(1, last_pair, is_last=True)
            down(1, last_pair, [last_pair.times(12, 11 + q) for q in range(2)])

        @block.scalar
        def _(act):
            n = inner(act)
            last_pair = Pair(n, 1)

            def take_rows(u, j):
                act.wait_ge(rows_turned, count(u, j))
                if not is_block(u, j, 0):
                    act.wait_ge(ex.used, ex.through(*before(u, j), 3))
                nc.scalar.activation(HB[0].rearrange("p k n -> p (k n)"), ps[:, 6:8, :].rearrange("p a b -> p (a b)"),
                                     ACT.Copy).then_inc(rows_hi, 1)

            def silu_gate(u, j):
                act.wait_ge(ex.used, ex.through(u, j, 3))
                if not is_block(u, j, 0):
                    act.wait_ge(product_turned, count(u, j, -1))
                nc.scalar.activation(AB, ps[:, 2 * u, :], ACT.Silu).then_inc(silu, 1)

            def take_product(u, j):
                act.wait_ge(product_turned, count(u, j))
                if not is_block(u, j, 0):
                    act.wait_ge(ex.used, ex.through(u, j, 5))
                nc.scalar.activation(AT_[0].rearrange("p k n -> p (k n)"), ps[:, 6, :], ACT.Copy).then_inc(product_hi, 1)

            def take_y(u, j, used):
                act.wait_ge(ex.used, used)
                if not (is_block(u, j, 0) or is_block(u, j, 1)):
                    act.wait_ge(y_free, count(u, j, -2))
                nc.scalar.activation(YB[:, u, 0:512], ps[:, 4, :], ACT.Copy).then_inc(y_low, 1)

            def step(u, j):
                ex.split_hi(act, u, j, 3)
                if not is_block(u, j, 0):
                    ex.split_hi(act, u, j, 4)
                    ex.split_hi(act, u, j, 5)
                silu_gate(u, j)
                ex.split_hi(act, *after(u, j), 0)
                take_rows(*after(u, j))
                ex.split_hi(act, *after(u, j), 1)
                if not is_block(u, j, 0):
                    take_y(*before(u, j), ex.through(u, j, 5))
                ex.split_hi(act, *after(u, j), 2)
                take_product(u, j)

            take_rows(0, zero)
            step(0, zero)
            step(1, zero)
            with act.Fori(0, n) as i:
                for u in range(2):
                    step(u, Pair(i, 1))
            step(0, last_pair)
            for q in (3, 4, 5):
                ex.split_hi(act, 1, last_pair, q)
            silu_gate(1, last_pair)
            ex.split_hi(act, 0, last_pair.plus(1), 4, free=last_pair.times(12, 9))
            take_y(0, last_pair, ex.through(1, last_pair, 5))
            ex.split_hi(act, 0, last_pair.plus(1), 5, free=last_pair.times(12, 10))
            take_product(1, last_pair)
            take_y(1, last_pair, last_pair.times(12, 12))

        @block.vector
        def _(dve):
            n = inner(dve)
            last_pair = Pair(n, 1)
            tt = nc.vector.tensor_tensor

            def take_rows(u, j):
                dve.wait_ge(rows_hi, count(u, j))
                tt(HB[1].rearrange("p k n -> p (k n)"), ps[:, 6:8, :].rearrange("p a b -> p (a b)"),
                   HB[0].rearrange("p k n -> p (k n)").bitcast(F32), ALU.subtract).then_inc(rows_lo, 1)

            def multiply(u, j):
                dve.wait_ge(silu, count(u, j))
                tt(AB, AB, ps[:, 2 * u + 1, :], ALU.mult).then_inc(product, 1)

            def take_product(u, j):
                dve.wait_ge(product_hi, count(u, j))
                tt(AT_[1].rearrange("p k n -> p (k n)"), ps[:, 6, :],
                   AT_[0].rearrange("p k n -> p (k n)").bitcast(F32), ALU.subtract).then_inc(product_lo, 1)

            def take_y(u, j, used):
                dve.wait_ge(ex.used, used)
                if not (is_block(u, j, 0) or is_block(u, j, 1)):
                    dve.wait_ge(y_free, count(u, j, -2))
                nc.vector.tensor_copy(YB[:, u, 512:1024], ps[:, 5, :]).then_inc(y_high, 1)

            def step(u, j):
                ex.split_lo(dve, u, j, 3)
                if not is_block(u, j, 0):
                    ex.split_lo(dve, u, j, 4)
                    ex.split_lo(dve, u, j, 5)
                multiply(u, j)
                ex.split_lo(dve, *after(u, j), 0)
                take_rows(*after(u, j))
                ex.split_lo(dve, *after(u, j), 1)
                if not is_block(u, j, 0):
                    take_y(*before(u, j), ex.through(u, j, 5))
                ex.split_lo(dve, *after(u, j), 2)
                take_product(u, j)

            take_rows(0, zero)
            step(0, zero)
            step(1, zero)
            with dve.Fori(0, n) as i:
                for u in range(2):
                    step(u, Pair(i, 1))
            step(0, last_pair)
            for q in (3, 4, 5):
                ex.split_lo(dve, 1, last_pair, q)
            multiply(1, last_pair)
            ex.split_lo(dve, 0, last_pair.plus(1), 4, free=last_pair.times(12, 9), hi_ready=last_pair.times(12, 11))
            take_y(0, last_pair, ex.through(1, last_pair, 5))
            ex.split_lo(dve, 0, last_pair.plus(1), 5, free=last_pair.times(12, 10), hi_ready=last_pair.times(12, 12))
            take_product(1, last_pair)
            take_y(1, last_pair, last_pair.times(12, 12))


def stage_combine(kit, io, scr, out):
    nc = kit.nc
    r = Routing(kit)
    x2 = kit.at(O_H, NC, D)
    G2, FN = kit.at(T_G2, 2, D), kit.at(T_FN, D)
    Y = kit.at(O_X, 2 * NC, D)
    sq, ssq, rr = kit.at(O_MG, D), kit.at(O_MG + 1024, NC), kit.at(O_MG + 1032, NC)
    O = kit.at(O_MG + 1040, 2, D)
    s_y = [kit.sem(f"f_rows{c}") for c in range(NC)]
    s_sq, s_rt = kit.sem("f_squares"), kit.sem("f_root")
    s_st = [kit.sem(f"f_stored{j}") for j in range(2)]
    s_a, s_m, s_g, s_x2, s_ms, s_n = (kit.sem("f_" + n) for n in ("weighted", "merged", "gated", "x", "mean", "normed"))
    with nc.Block() as block:
        @block.gpsimd
        def _(pool):
            for c in range(NC):
                for k in range(2):
                    pool.indirect_dma_start(out=Y[:, 2 * c + k, :], out_offset=None, in_=scr["ys"],
                                            in_offset=bass.IndirectOffsetOnAxis(ap=r.slot[k][:, c:c + 1], axis=0)).then_inc(s_y[c], 16)
            for c in range(NC):
                pool.wait_ge(s_m, c + 1)
                nc.gpsimd.tensor_tensor(Y[:, 2 * c, :], Y[:, 2 * c, :], G2[:, min(c, 1), :], ALU.mult).then_inc(s_g, 1)

        @block.vector
        def _(dve):
            def merge(c):
                dve.wait_ge(s_a, c + 1)
                nc.vector.scalar_tensor_tensor(out=Y[:, 2 * c, :], in0=Y[:, 2 * c + 1, :], scalar=r.weight[:, 1, c:c + 1],
                                               in1=Y[:, 2 * c, :], op0=ALU.mult, op1=ALU.add).then_inc(s_m, 1)

            def add(c):
                dve.wait_ge(s_g, c + 1)
                nc.vector.tensor_tensor(x2[:, c, :], x2[:, c, :], Y[:, 2 * c, :], ALU.add).then_inc(s_x2, 1)

            def mean(c):
                dve.wait_ge(s_sq, c + 1)
                nc.vector.tensor_scalar(ssq[:, c:c + 1], ssq[:, c:c + 1], 1.0 / D, EPS, ALU.mult, ALU.add).then_inc(s_ms, 1)
                dve.wait_ge(s_ms, 2 * c + 1)
                nc.vector.reciprocal(rr[:, c:c + 1], ssq[:, c:c + 1]).then_inc(s_ms, 1)

            def norm(c):
                dve.wait_ge(s_rt, c + 1)
                if c >= 2:
                    dve.wait_ge(s_st[c % 2], 16 * (c // 2))
                nc.vector.scalar_tensor_tensor(out=O[:, c % 2, :], in0=x2[:, c, :], scalar=rr[:, c:c + 1], in1=FN,
                                               op0=ALU.mult, op1=ALU.mult).then_inc(s_n, 1)

            merge(0)
            for c in range(NC):
                if c + 1 < NC:
                    merge(c + 1)
                add(c)
                if c:
                    norm(c - 1)
                mean(c)
            norm(NC - 1)

        @block.scalar
        def _(act):
            def weigh(c):
                act.wait_ge(s_y[c], 32)
                nc.scalar.activation(Y[:, 2 * c, :], Y[:, 2 * c, :], ACT.Copy, scale=r.weight[:, 0, c:c + 1]).then_inc(s_a, 1)

            weigh(0)
            weigh(1)
            for c in range(NC):
                if c + 2 < NC:
                    weigh(c + 2)
                act.wait_ge(s_x2, c + 1)
                if c:
                    act.wait_ge(s_sq, c)
                nc.scalar.activation(sq, x2[:, c, :], ACT.Square, accum_out=ssq[:, c:c + 1]).then_inc(s_sq, 1)
                act.wait_ge(s_ms, 2 * c + 2)
                nc.scalar.activation(rr[:, c:c + 1], rr[:, c:c + 1], ACT.Sqrt).then_inc(s_rt, 1)

        @block.sync
        def _(sp):
            for c in range(NC):
                sp.wait_ge(s_n, c + 1)
                dst = out["y_prompt"] if c == 0 else out["y_sample"][(c - 1) * P:c * P, :]
                sp.dma_start(dst, O[:, c % 2, :]).then_inc(s_st[c % 2], 16)
            sp.wait_ge(s_st[0], 48)
            sp.wait_ge(s_st[1], 32)


def scratch(nc):
    dram = lambda name, shape: nc.dram_tensor(name, shape, F32, kind="Internal").ap()
    return dict(xp=dram("x_plus_pos", [T, D]), xs=dram("slot_rows", [(NMB + 1) * P, D]), ys=dram("expert_rows", [NMB * P, D]),
                z=dram("silu_z", [T, INNER]), gb=dram("gate_b", [KD, P, T]), mod=dram("modulation", [2, 4 * D]))


def run_stages(kit, io, scr, out, upto=99):
    stream = Weights(kit, "first", io["units"][0:40])
    ht = stage_modulate(kit, stream, io, scr)
    if upto < 1:
        return
    ya = stage_gmlp(kit, stream, io, scr, ht)
    if upto < 2:
        return
    stage_branch_a(kit, stream, io, scr, ya)
    if upto < 3:
        return
    stage_conv(kit, stream, io)
    if upto < 4:
        return
    stage_gates(kit, stream, io, scr)
    if upto < 5:
        return
    stage_ssd(kit, io, out)
    if upto < 6:
        return
    kit.recycle()
    stream = Weights(kit, "second", io["units"][40:52])
    stage_norm_y(kit, stream, io, scr)
    if upto < 7:
        return
    stage_branch_b(kit, stream, io, scr)
    if upto < 8:
        return
    ex = Experts(kit)
    stage_out(kit, stream, io, scr, ex)
    stage_route(kit, io, scr, ex)
    if upto < 9:
        return
    stage_experts(kit, io, scr, ex)
    if upto < 10:
        return
    stage_combine(kit, io, scr, out)


def build(nc, io, out):
    with ExitStack() as ctx:
        run_stages(Kit(nc, ctx), io, scratch(nc), out)


def host_layout(i):
    import numpy as np
    a = {k: np.asarray(v) for k, v in i.items()}
    w_in = a["w_in"][0]
    cut = [0, 1024, 2048, 3072, 4096, 6144, 9216, 9280]
    ga, gb, u, v, z, xbc, dt = [w_in[:, cut[j]:cut[j + 1]] for j in range(7)]

    def units(w, cols):
        r, n = w.shape
        return w.reshape(r // P, P, n // cols, cols).transpose(2, 1, 0, 3).reshape(n // cols, P, -1)

    stream = [units(v, UC), units(u, UC), units(ga, UC), units(a["w_branch_a"][0], UC), units(xbc, UC), units(z, UC),
              units(gb, UC), units(a["w_branch_b"][0], P), units(a["w_out"][0], UC)]
    o = {"units": np.concatenate(stream, 0)}
    o["w_dt"] = units(dt, 64)[0]
    o["w_mod"] = units(a["w_mod"][0], 512)
    o["b_mod"] = a["b_mod"][0][None]
    o["cond"] = np.stack([a["c_ctx"], a["c"][0]], 0).reshape(2, KD, P).transpose(2, 1, 0).reshape(P, 16)
    o["x"] = np.concatenate([a["x_prompt"][0], a["x_sample"][0]], 0)
    col = lambda w: w.reshape(-1, P).T
    o["norm1"] = col(a["norm1_w"][0])
    o["wsT"] = a["gmlp_ws"][0].transpose(2, 0, 1)
    o["gmlp_nw"] = col(a["gmlp_norm_w"][0])
    o["gmlp_bs"] = a["gmlp_bs"][0].reshape(1, -1)
    o["dt_bias"] = a["dt_bias"][0].reshape(64, 1)
    o["a_log"] = a["a_log"][0].reshape(1, 64)
    o["conv_w"] = a["conv_w"][0].reshape(TAPS, -1, P).transpose(2, 1, 0).reshape(P, -1)
    o["conv_b"] = col(a["conv_b"][0])
    o["state_t"] = a["state_ssd"][0, 0].reshape(2, INNER, P).transpose(0, 2, 1)
    o["d_skip"] = a["d_skip"].reshape(1, HEADS)
    o["ssd_nw"] = col(a["ssd_norm_w"][0])
    o["norm2"], o["fnorm"] = a["norm2_w"][0].reshape(1, D), a["final_norm_w"].reshape(1, D)
    o["router_w"], o["router_b"] = units(a["router_w"], NE)[0], a["router_bias"].reshape(1, NE)
    experts = lambda w: w.reshape(NE, w.shape[1] // P, P, w.shape[2]).transpose(0, 2, 1, 3).reshape(NE, P, -1)
    o["wg"], o["wu"], o["wd"] = experts(a["w_gate_e"][0]), experts(a["w_up_e"][0]), experts(a["w_down_e"][0])
    grid = 64
    omega = 1.0 / (10000.0 ** (np.arange(D // 4, dtype=np.float32) / np.float32(D // 4)))
    r = np.arange(LAT // grid, dtype=np.float32)[:, None] * omega
    cc = np.arange(grid, dtype=np.float32)[:, None] * omega
    r = np.concatenate([np.sin(r), np.cos(r)], -1)
    cc = np.concatenate([np.sin(cc), np.cos(cc)], -1)
    pos = np.concatenate([np.repeat(r, grid, 0), np.tile(cc, (LAT // grid, 1))], -1).astype(np.float32)
    o["pos"] = pos
    K = np.zeros((P, KOFF["end"]), np.float32)
    p, q = np.arange(P)[:, None], np.arange(P)[None]
    for name, m in (("ident", p == q), ("le", p <= q), ("ge", p >= q), ("gt", p > q), ("lt", p < q), ("one", p >= 0)):
        K[:, KOFF[name]:KOFF[name] + P] = m
    K[:, KOFF["e128"]:KOFF["e128"] + 16] = np.arange(16) * 128
    K[:, KOFF["pri16"]:KOFF["pri16"] + 16] = 16 - np.arange(16)
    K[:, KOFF["pri4"]:KOFF["pri4"] + 4] = 4 - np.arange(4)
    K[:, KOFF["thr"]:KOFF["thr"] + 5] = 2 * np.arange(5)
    K[:, KOFF["col"]:KOFF["col"] + 26] = np.arange(26)
    o["consts"] = K
    return {k: np.ascontiguousarray(v) for k, v in o.items()}


def kernel(**inputs):
    import numpy as np
    import concourse.bacc as bacc
    from concourse.bass_utils import run_bass_kernel_spmd

    nc = bacc.Bacc("TRN2", target_bir_lowering=False, num_devices=1)
    arrays = host_layout(inputs)
    io = {k: nc.dram_tensor("in_" + k, v.shape, mybir.dt.from_np(v.dtype), kind="ExternalInput").ap()
          for k, v in arrays.items()}
    shapes = dict(y_prompt=(P, D), y_sample=(LAT, D), state=(2, INNER, P))
    out = {k: nc.dram_tensor("out_" + k, s, F32, kind="ExternalOutput").ap() for k, s in shapes.items()}
    build(nc, io, out)
    r = run_bass_kernel_spmd(nc, [{"in_" + k: v for k, v in arrays.items()}], core_ids=[0]).results[0]
    return (np.asarray(r["out_y_prompt"]).reshape(1, P, D), np.asarray(r["out_y_sample"]).reshape(1, LAT, D),
            np.asarray(r["out_state"]).reshape(1, 1, 2, HEADS, HD, P))
```

```python
import concourse.bass as bass
from concourse import mybir
from contextlib import ExitStack

F32 = mybir.dt.float32
F32R = mybir.dt.float32r
BF16 = mybir.dt.bfloat16
I32 = mybir.dt.int32
U32 = mybir.dt.uint32
ALU = mybir.AluOpType
ACT = mybir.ActivationFunctionType
AX = mybir.AxisListType

P = 128
D = 1024
KD = D // P
NC = 5
T = NC * P
LAT = T - P
HALF = T // 2
G = 4
HPG = 8
HEADS = G * HPG
HD = 64
GW = HPG * HD
INNER = G * GW
KI = INNER // P
NE = 16
NG = 4
FE = 512
EPS = 1e-6
TAPS = 5
UNIT = 2048
UC = 256
NMB = 26
BIG = 1.0e30

O_H = 0
O_X = 10240
O_BC = 20480
O_TMP = 28160
O_MG = 33280
O_RAW = 38400
O_HL = 42496
O_K = 50688
ARENA = 52992
REGIONS = (O_H, O_X, O_BC, O_TMP, O_MG, O_RAW, O_HL, O_K)
KOFF = dict(ident=0, le=128, ge=256, gt=384, lt=512, one=640, e128=768, pri16=784, pri4=800, thr=804, col=812, end=840)


class Kit:

    def __init__(self, nc, ctx):
        self.nc, self.sems = nc, []
        self.arena = ctx.enter_context(nc.sbuf_tensor("arena", [P, ARENA], F32))
        self.base = nc.sbuf_base - 4 * ARENA
        self.tensors = {}
        self.ps = ctx.enter_context(nc.psum_tensor("banks", [P, 8, 512], F32))

    def sem(self, name):
        self.sems.append(self.nc.alloc_semaphore(name=name))
        return self.sems[-1]

    def recycle(self):
        self.nc.clear_and_free_semaphores(self.sems)
        self.nc.all_engine_barrier()
        self.sems = []

    def placed(self, name, off, n, dtype):
        if name not in self.tensors:
            self.tensors[name] = self.nc.alloc_sbuf_tensor_at(name, [P, n], dtype,
                                                              offset=self.base + 4 * off)
        return self.tensors[name]

    def at(self, off, *dims):
        n = 1
        for d in dims:
            n *= d
        first = max(o for o in REGIONS if o <= off)
        end = min(o for o in REGIONS + (ARENA,) if o >= off + n)
        t = self.placed(f"words_{first}_{end}", first, end - first, F32)
        return self.shaped(t[:, off - first:off - first + n], dims)

    def rnd(self, off, *dims):
        n = 1
        for d in dims:
            n *= d
        return self.shaped(self.placed(f"rounded_{off}_{n}", off, n, F32R)[:, :], dims)

    def shaped(self, v, dims):
        if len(dims) == 2:
            v = v.rearrange("p (a b) -> p a b", a=dims[0])
        if len(dims) == 3:
            v = v.rearrange("p (a b c) -> p a b c", a=dims[0], b=dims[1])
        return v

    def const(self, name, n=P):
        return self.at(O_K, KOFF["end"])[:, KOFF[name]:KOFF[name] + n]


class Chain:

    def __init__(self, eng, sem):
        self.eng, self.sem, self.n = eng, sem, 0

    def step(self, ins):
        ins.then_inc(self.sem, 1)
        self.n += 1

    def sync(self):
        self.eng.wait_ge(self.sem, self.n)


class Weights:

    def __init__(self, kit, stream, units):
        self.nc, self.units, self.count, self.first = kit.nc, units, units.shape[0], 0
        self.raw = kit.at(O_RAW, 2, UNIT)
        self.hi, self.lo = kit.rnd(O_HL, 2, UNIT), kit.rnd(O_HL + 2 * UNIT, 2, UNIT)
        self.raw_loaded = [kit.sem(f"{stream}_raw_loaded{s}") for s in range(2)]
        self.hi_ready = kit.sem(f"{stream}_hi_ready")
        self.lo_ready = kit.sem(f"{stream}_lo_ready")
        self.used = kit.sem(f"{stream}_unit_used")

    def section(self, n):
        w = Section(self, n)
        self.first += n
        return w


class Section(Weights):

    AHEAD = 2

    def __init__(self, stream, n):
        self.nc, self.units, self.count = stream.nc, stream.units, stream.count
        self.first, self.n = stream.first, n
        self.raw, self.hi, self.lo = stream.raw, stream.hi, stream.lo
        self.raw_loaded, self.hi_ready, self.lo_ready = stream.raw_loaded, stream.hi_ready, stream.lo_ready
        self.used = stream.used

    def to_load(self):
        return range(self.AHEAD if self.n else 0, min(self.n + self.AHEAD, self.count - self.first))

    def exists(self, i):
        return self.first + i < self.count

    def load(self, sp, i):
        i += self.first
        if i >= 2:
            sp.wait_ge(self.lo_ready, i - 1)
        sp.dma_start(self.raw[:, i % 2, :], self.units[i]).then_inc(self.raw_loaded[i % 2], 16)

    def split_hi(self, act, i):
        i += self.first
        act.wait_ge(self.raw_loaded[i % 2], 16 * (i // 2 + 1))
        if i >= 2:
            act.wait_ge(self.used, i - 1)
        self.nc.scalar.activation(self.hi[:, i % 2, :], self.raw[:, i % 2, :],
                                  ACT.Copy).then_inc(self.hi_ready, 1)

    def split_lo(self, dve, i):
        i += self.first
        dve.wait_ge(self.hi_ready, i + 1)
        if i >= 2:
            dve.wait_ge(self.used, i - 1)
        self.nc.vector.tensor_tensor(self.lo[:, i % 2, :], self.raw[:, i % 2, :],
                                     self.hi[:, i % 2, :].bitcast(F32), ALU.subtract).then_inc(self.lo_ready, 1)

    def parts(self, i, k):
        i += self.first
        return [x[:, i % 2, :].rearrange("p (k n) -> p k n", k=k)
                for x in (self.hi, self.lo)]

    def ready(self, pe, i):
        pe.wait_ge(self.hi_ready, self.first + i + 1)
        pe.wait_ge(self.lo_ready, self.first + i + 1)

    def done(self, i):
        return self.used, self.first + i + 1


def split3(nc, out, lhs, rhs, nk):
    for k in range(nk):
        nc.tensor.matmul(out, lhs[0](k), rhs[0](k), start=(k == 0), stop=False)
        nc.tensor.matmul(out, lhs[0](k), rhs[1](k), start=False, stop=False)
        last = nc.tensor.matmul(out, lhs[1](k), rhs[0](k), start=False, stop=(k == nk - 1))
    return last


def feature_tile(nc, w, t, moving, out, nk):
    for h in range(2):
        last = split3(nc, out(h), [lambda k, x=x: x[:, k, t * P:(t + 1) * P] for x in w],
                      [lambda k, x=x: x[:, k, h * HALF:(h + 1) * HALF] for x in moving], nk)
    return last


def token_tile(nc, w, c, stationary, out):
    return split3(nc, out, [lambda k, x=x: x[:, k, c * P:(c + 1) * P] for x in stationary],
                  [lambda k, x=x: x[:, k, :] for x in w], KD)


def halves(kit, pair):
    return kit.ps[:, 2 * pair:2 * pair + 2, 0:HALF]


def two(ap):
    return ap.rearrange("p (h n) -> p h n", h=2)


def stage_modulate(kit, stream, io, scr):
    nc, ps = kit.nc, kit.ps
    WM = [kit.at(o, 4096) for o in (O_H, O_H + 5120, O_MG, O_BC + 2304)]
    w = stream.section(0)
    RB = (4, 5, 7, 3)
    x = kit.at(O_X, NC, D)
    pos = kit.at(O_X + 5120, NC - 1, D)
    xn = kit.at(O_X + 5120, NC, D)
    cond = kit.at(O_TMP, 16)
    sc = kit.at(O_TMP + 16, 16)
    row = kit.at(O_TMP + 32, 2048)
    brow = kit.at(O_TMP + 2080, 2048)
    n1 = kit.at(O_TMP + 4128, KD)
    AS = kit.at(O_TMP + 4136, 2, KD, 2)
    ssq = kit.at(O_TMP + 4168, NC)
    rr = kit.at(O_TMP + 4173, NC)
    sq = kit.at(O_BC, D)
    full = kit.at(O_BC + 1024, 2, T)
    hi, lo = kit.rnd(O_H, KD, T), kit.rnd(O_H + 5120, KD, T)
    ident = kit.const("ident")
    s_small, s_x, s_w = kit.sem("m_small"), kit.sem("m_x"), [kit.sem(f"m_w{j}") for j in range(4)]
    s_c = kit.sem("m_consts")
    s_act, s_dve, s_row, s_cols = kit.sem("m_act"), kit.sem("m_dve"), kit.sem("m_row"), kit.sem("m_cols")
    s_xt, s_full, s_split, s_xp = kit.sem("m_xt"), kit.sem("m_full"), kit.sem("m_split"), kit.sem("m_xp")

    with nc.Block() as block:
        @block.sync
        def _(sp):
            sp.dma_start(kit.at(O_K, KOFF["end"]), io["consts"]).then_inc(s_c, 16)
            sp.dma_start(cond, io["cond"]).then_inc(s_small, 16)
            sp.dma_start(n1, io["norm1"]).then_inc(s_small, 16)
            sp.dma_start(brow[0:2, :], io["b_mod"][:, 0:2048].partition_broadcast(2)).then_inc(s_small, 16)
            sp.dma_start(WM[0], io["w_mod"][0]).then_inc(s_w[0], 16)
            sp.dma_start(x, io["x"].rearrange("(c p) d -> p c d", p=P)).then_inc(s_x, 16)
            sp.dma_start(pos, io["pos"].rearrange("(c p) d -> p c d", p=P)).then_inc(s_x, 16)
            for j in range(1, 4):
                sp.dma_start(WM[j], io["w_mod"][j]).then_inc(s_w[j], 16)
            for i in w.to_load():
                w.load(sp, i)
            sp.wait_ge(s_dve, 2)
            sp.dma_start(scr["xp"].rearrange("(c p) d -> p c d", p=P), x).then_inc(s_xp, 16)
            sp.wait_ge(s_xp, 16)

        @block.scalar
        def _(act):
            act.wait_ge(s_small, 48)
            nc.scalar.activation(sc, cond, ACT.Silu).then_inc(s_act, 1)
            act.wait_ge(s_dve, 2)
            for c in range(NC):
                if c:
                    act.wait_ge(s_act, c + 1)
                nc.scalar.activation(sq, x[:, c, :], ACT.Square, accum_out=ssq[:, c:c + 1]).then_inc(s_act, 1)
            act.wait_ge(s_dve, 4)
            nc.scalar.activation(rr, rr, ACT.Sqrt).then_inc(s_act, 1)
            w.split_hi(act, 0)
            for k in range(KD):
                act.wait_ge(s_xt, k + 1)
                act.wait_ge(s_cols, 2)
                if k >= 2:
                    act.wait_ge(s_split, 2 * (k - 1))
                for st, lo_, hi_ in ((0, 0, P), (1, P, T)):
                    b = 2 * (k % 2)
                    src = ps[:, b:b + 2, :].rearrange("p a b -> p (a b)")[:, lo_:hi_]
                    nc.scalar.activation(full[:, k % 2, lo_:hi_], src, ACT.Identity,
                                         scale=AS[:, 1, k, st:st + 1],
                                         bias=AS[:, 0, k, st:st + 1]).then_inc(s_full, 1)

        @block.vector
        def _(dve):
            ch = Chain(dve, s_dve)
            dve.wait_ge(s_x, 32)
            ch.step(nc.vector.tensor_tensor(x[:, 1:3, :], x[:, 1:3, :], pos[:, 0:2, :], ALU.add))
            ch.step(nc.vector.tensor_tensor(x[:, 3:5, :], x[:, 3:5, :], pos[:, 2:4, :], ALU.add))
            dve.wait_ge(s_act, 1 + NC)
            ch.step(nc.vector.tensor_scalar(ssq, ssq, 1.0 / D, EPS, ALU.mult, ALU.add))
            ch.sync()
            ch.step(nc.vector.reciprocal(rr, ssq))
            dve.wait_ge(s_act, 2 + NC)
            for c in range(NC):
                ch.step(nc.vector.tensor_scalar(xn[:, c, :], x[:, c, :], rr[:, c:c + 1], None, ALU.mult))
            for j in range(4):
                dve.wait_ge(s_row, j + 1)
                ch.step(nc.vector.tensor_tensor(row[0:2, j * 512:(j + 1) * 512], ps[0:2, RB[j], :],
                                                brow[0:2, j * 512:(j + 1) * 512], ALU.add))
            dve.wait_ge(s_row, 5)
            v = ps[:, 6, 0:32].rearrange("p (q k s) -> p q k s", q=2, k=KD)
            nc.vector.tensor_copy(AS[:, 0, :, :], v[:, 0, :, :]).then_inc(s_cols, 1)
            nc.vector.scalar_tensor_tensor(out=AS[:, 1, :, :], in0=v[:, 1, :, :], scalar=1.0,
                                           in1=n1.unsqueeze(2).broadcast_to([P, KD, 2]),
                                           op0=ALU.add, op1=ALU.mult).then_inc(s_cols, 1)
            w.split_lo(dve, 0)
            for k in range(KD):
                dve.wait_ge(s_full, 2 * k + 2)
                nc.vector.tensor_copy(hi[:, k, :], full[:, k % 2, :]).then_inc(s_split, 1)
                dve.wait_ge(s_split, 2 * k + 1)
                nc.vector.tensor_tensor(lo[:, k, :], full[:, k % 2, :], hi[:, k, :].bitcast(F32),
                                        ALU.subtract).then_inc(s_split, 1)

        @block.tensor
        def _(pe):
            pe.wait_ge(s_c, 16)
            pe.wait_ge(s_act, 1)
            for j in range(4):
                pe.wait_ge(s_w[j], 16)
                for k in range(KD):
                    last = nc.tensor.matmul(ps[0:2, RB[j], :], sc.rearrange("p (k s) -> p k s", s=2)[:, k, :],
                                            WM[j][:, k * 512:(k + 1) * 512], start=(k == 0), stop=(k == KD - 1))
                last.then_inc(s_row, 1)
            pe.wait_ge(s_dve, 4 + NC + 4)
            for j in range(16):
                last = nc.tensor.transpose(ps[:, 6, 2 * j:2 * j + 2], row[0:2, j * P:(j + 1) * P], ident[0:2, 0:2])
            last.then_inc(s_row, 1)
            for k in range(KD):
                if k >= 2:
                    pe.wait_ge(s_full, 2 * (k - 1))
                b = 2 * (k % 2)
                for c in range(NC):
                    o = ps[:, b, c * P:(c + 1) * P] if c < 4 else ps[:, b + 1, 0:P]
                    last = nc.tensor.transpose(o, xn[:, c, k * P:(k + 1) * P], ident)
                last.then_inc(s_xt, 1)
    return hi, lo


def stage_gmlp(kit, stream, io, scr, ht):
    nc, ps = kit.nc, kit.ps
    V = kit.at(O_X, NC, D)
    ya = kit.at(O_X + 5120, KD, T)
    ya_hi, ya_lo = kit.rnd(O_X + 5120, KD, T), kit.rnd(O_X + 10240, KD, T)
    full = kit.at(O_TMP, 2, T)
    wsT = kit.at(O_TMP + 1280, KD, P)
    bsb = kit.at(O_TMP + 2304, KD, P)
    nw = kit.at(O_TMP + 3328, KD)
    ssq = kit.at(O_TMP + 3336, NC)
    rr = kit.at(O_TMP + 3341, NC)
    sq = kit.at(O_TMP + 3400, D)
    gate = kit.at(O_MG, KD, T)
    nv, nu, ng = 4, 4, 4
    w = stream.section(nv + nu + ng)
    s_c = kit.sem("g_consts")
    s_gt, s_gate = kit.sem("g_gate_tile"), kit.sem("g_gate")
    s_v, s_vev = kit.sem("g_v"), kit.sem("g_v_taken")
    s_u, s_uev = kit.sem("g_u"), kit.sem("g_u_taken")
    s_sq, s_n = kit.sem("g_squares"), kit.sem("g_norm")
    s_mix, s_m, s_split = kit.sem("g_mixed"), kit.sem("g_product"), kit.sem("g_split")
    s_zero, s_zo = kit.sem("g_zero"), kit.sem("g_zeros_stored")

    with nc.Block() as block:
        @block.sync
        def _(sp):
            sp.dma_start(wsT, io["wsT"]).then_inc(s_c, 16)
            sp.dma_start(nw, io["gmlp_nw"]).then_inc(s_c, 16)
            sp.dma_start(bsb, io["gmlp_bs"].partition_broadcast(P)).then_inc(s_c, 16)
            for i in w.to_load():
                w.load(sp, i)

        @block.gpsimd
        def _(pool):
            zero = kit.at(O_TMP + 4600, 512)
            nc.gpsimd.memset(zero, 0.0).then_inc(s_zero, 1)
            pool.wait_ge(s_zero, 1)
            rows = [(scr["xs"], b) for b in range(NMB + 1)] + [(scr["ys"], b) for b in range(NE, NMB)]
            for dst, b in rows:
                pool.dma_start(dst[b * P:(b + 1) * P, :].rearrange("p (a d) -> p a d", a=2),
                               zero.unsqueeze(1).broadcast_to([P, 2, 512])).then_inc(s_zo, 16)
            pool.wait_ge(s_zo, 16 * len(rows))

        @block.tensor
        def _(pe):
            for i in range(4):
                w.ready(pe, i)
                for c in range(NC):
                    if i:
                        pe.wait_ge(s_vev, NC * (i - 1) + c + 1)
                    last = token_tile(nc, w.parts(i, KD), c, ht, ps[:, c, 0:UC])
                    if c < NC - 1:
                        last.then_inc(s_v, 1)
                last.then_inc(w.used, 1)
            pe.wait_ge(s_vev, NC * 4)
            for i in range(4, 8):
                w.ready(pe, i)
                for t in range(2):
                    if i > 4:
                        pe.wait_ge(s_uev, 2 * (i - 5) + t + 1)
                    last = feature_tile(nc, w.parts(i, KD), t, ht, lambda h: halves(kit, t)[:, h, :], KD)
                    if t == 0:
                        last.then_inc(s_u, 1)
                last.then_inc(w.used, 1)
            for g in range(KD):
                i, t = nv + nu + g // 2, g % 2
                if t == 0:
                    w.ready(pe, i)
                if g < 2:
                    pe.wait_ge(s_uev, 6 + g + 1)
                else:
                    pe.wait_ge(s_gate, g - 1)
                last = feature_tile(nc, w.parts(i, KD), t, ht, lambda h: halves(kit, t)[:, h, :], KD)
                last.then_inc(w.used if t else s_gt, 1)
                if g == 0:
                    pe.wait_ge(s_c, 48)
                    pe.wait_ge(s_n, 2 + NC)
                if g >= 2:
                    pe.wait_ge(s_m, 3 * (g - 2) + 1)
                b = 4 + 2 * (g % 2)
                for c in range(NC):
                    o = ps[:, b, c * P:(c + 1) * P] if c < 4 else ps[:, b + 1, 0:P]
                    last = nc.tensor.matmul(o, V[:, c, g * P:(g + 1) * P], wsT[:, g, :], start=True, stop=True)
                last.then_inc(s_mix, 1)

        @block.scalar
        def _(act):
            for i in range(4):
                w.split_hi(act, i + 1)
                for c in range(NC):
                    if c < NC - 1:
                        act.wait_ge(s_v, (NC - 1) * i + c + 1)
                    else:
                        act.wait_ge(*w.done(i))
                    nc.scalar.activation(V[:, c, i * UC:(i + 1) * UC], ps[:, c, 0:UC],
                                         ACT.Gelu_apprx_tanh).then_inc(s_vev, 1)
            act.wait_ge(s_vev, NC * 4)
            for i in range(4, 8):
                w.split_hi(act, i + 1)
                for t in range(2):
                    if t == 0:
                        act.wait_ge(s_u, i - 4 + 1)
                    else:
                        act.wait_ge(*w.done(i))
                    nc.scalar.activation(two(ya[:, 2 * (i - 4) + t, :]), halves(kit, t),
                                         ACT.Gelu_apprx_tanh).then_inc(s_uev, 1)
                if i == 4:
                    for c in range(NC):
                        if c:
                            act.wait_ge(s_sq, c)
                        nc.scalar.activation(sq, V[:, c, :], ACT.Square,
                                             accum_out=ssq[:, c:c + 1]).then_inc(s_sq, 1)
            act.wait_ge(s_n, 2)
            nc.scalar.activation(rr, rr, ACT.Sqrt).then_inc(s_sq, 1)
            for g in range(KD):
                i, t = nv + nu + g // 2, g % 2
                if t == 0:
                    w.split_hi(act, i + 1)
                act.wait_ge(*(w.done(i) if t else (s_gt, g // 2 + 1)))
                nc.scalar.activation(two(gate[:, g, :]), halves(kit, t), ACT.Sigmoid).then_inc(s_gate, 1)
                act.wait_ge(s_m, 3 * g + 3)
                nc.scalar.activation(ya_hi[:, g, :], full[:, g % 2, :], ACT.Copy).then_inc(s_split, 1)

        @block.vector
        def _(dve):
            for i in range(4):
                w.split_lo(dve, i + 1)
            w.split_lo(dve, 5)
            dve.wait_ge(s_sq, NC)
            nc.vector.tensor_scalar(ssq, ssq, 1.0 / D, EPS, ALU.mult, ALU.add).then_inc(s_n, 1)
            dve.wait_ge(s_n, 1)
            nc.vector.reciprocal(rr, ssq).then_inc(s_n, 1)
            w.split_lo(dve, 6)
            w.split_lo(dve, 7)
            w.split_lo(dve, 8)
            dve.wait_ge(s_sq, NC + 1)
            for c in range(NC):
                nc.vector.tensor_scalar(V[:, c, :], V[:, c, :], rr[:, c:c + 1], None, ALU.mult).then_inc(s_n, 1)
            dve.wait_ge(s_c, 48)
            dve.wait_ge(s_uev, 8)
            for g in range(KD):
                if g % 2 == 0:
                    w.split_lo(dve, nv + nu + g // 2 + 1)
                dve.wait_ge(s_mix, g + 1)
                b = 4 + 2 * (g % 2)
                mixed = ps[:, b:b + 2, :].rearrange("p a b -> p (a b)")[:, 0:T].rearrange("p (c t) -> p c t", c=NC)
                f = full[:, g % 2, :]
                nc.vector.scalar_tensor_tensor(out=f.rearrange("p (c t) -> p c t", c=NC), in0=mixed, scalar=nw[:, g:g + 1],
                                               in1=bsb[:, g, :].unsqueeze(1).broadcast_to([P, NC, P]),
                                               op0=ALU.mult, op1=ALU.add).then_inc(s_m, 1)
                dve.wait_ge(s_m, 3 * g + 1)
                nc.vector.tensor_tensor(f, f, ya[:, g, :], ALU.mult).then_inc(s_m, 2)
                dve.wait_ge(s_split, g + 1)
                nc.vector.tensor_tensor(ya_lo[:, g, :], f, ya_hi[:, g, :].bitcast(F32), ALU.subtract).then_inc(s_n, 1)
                dve.wait_ge(s_n, 2 + NC + g + 1)
    return ya_hi, ya_lo


def stage_branch_a(kit, stream, ya):
    nc = kit.nc
    MG = kit.at(O_MG, KD, T)
    w = stream.section(4)
    s_t0, s_mg = kit.sem("a_tile0"), kit.sem("a_merged")
    with nc.Block() as block:
        @block.sync
        def _(sp):
            for i in w.to_load():
                w.load(sp, i)

        @block.tensor
        def _(pe):
            for i in range(4):
                w.ready(pe, i)
                for t in range(2):
                    if i:
                        pe.wait_ge(s_mg, 2 * (i - 1) + t + 1)
                    last = feature_tile(nc, w.parts(i, KD), t, ya, lambda h: halves(kit, t)[:, h, :], KD)
                    last.then_inc(w.used if t else s_t0, 1)

        @block.scalar
        def _(act):
            for i in range(4):
                w.split_hi(act, i + 1)

        @block.vector
        def _(dve):
            for i in range(4):
                w.split_lo(dve, i + 1)
                for t in range(2):
                    dve.wait_ge(*(w.done(i) if t else (s_t0, i + 1)))
                    tile = MG[:, 2 * i + t, :]
                    nc.vector.tensor_tensor(two(tile), halves(kit, t), two(tile), ALU.mult).then_inc(s_mg, 1)


def stage_conv(kit, stream, io):
    nc, ps = kit.nc, kit.ps
    nt = (INNER + 2 * G * P) // P
    n, W0 = nt // 2, 2 + T + 4
    pre, acc, post = kit.at(O_TMP, 2, W0), kit.at(O_TMP + 2 * W0, 2, W0 - 4), kit.at(O_TMP + 4 * W0 - 8, 2, T)
    cw, cb = kit.at(O_TMP + 4 * W0 + 1280, nt, TAPS), kit.at(O_TMP + 4 * W0 + 1400, nt)
    X, Bt = kit.at(O_X, NC, INNER), kit.at(O_BC + 5120, NC, G * P)
    BCT = kit.at(O_BC, 2 * G, T)
    ht = [kit.rnd(o, KD, T) for o in (O_H, O_H + 5120)]
    ident = kit.const("ident")
    w = stream.section(n)
    s_in, s_pad, s_t0 = kit.sem("c_in"), kit.sem("c_pad"), kit.sem("c_tile0")
    s_pre, s_cv, s_silu, s_tr, s_x = (kit.sem("c_" + x) for x in ("pre", "conv", "silu", "turned", "x"))
    turned = lambda tile: tile < 20
    dest = lambda tile: post[:, tile % 2, :] if tile < 16 else BCT[:, tile - 16, :]
    raw, whi, wlo = kit.at(O_BC, 512), kit.rnd(O_BC + 512, 512), kit.rnd(O_BC + 1024, 512)
    bias = kit.at(O_BC + 1536, 1)[0:64]
    alog = kit.at(O_BC + 1600, 64)
    dtT = kit.at(O_BC + 1700, T)[0:64]
    dx, e, r, sden, s, s2, q = (kit.at(O_BC + 2400 + 320 * j, 320) for j in range(7))
    DT, A = kit.at(O_TMP + 4480, NC, 64), kit.at(O_TMP + 4800, NC, 64)
    d_in, d_hl, d_pe, d_act, d_dve = (kit.sem("d_" + x) for x in ("in", "split", "pe", "act", "dve"))
    DT_STEPS = 16
    with nc.Block() as block:
        @block.sync
        def _(sp):
            sp.dma_start(raw, io["w_dt"]).then_inc(d_in, 16)
            sp.dma_start(bias, io["dt_bias"]).then_inc(d_in, 16)
            sp.dma_start(alog, io["a_log"].partition_broadcast(P)).then_inc(d_in, 16)
            sp.dma_start(cw, io["conv_w"].rearrange("p (t k) -> p t k", k=TAPS)).then_inc(s_in, 16)
            sp.dma_start(cb, io["conv_b"]).then_inc(s_in, 16)
            for i in w.to_load():
                w.load(sp, i)

        @block.tensor
        def _(pe):
            def turn(i):
                for t in range(2):
                    tile = 2 * i + t
                    if not turned(tile):
                        continue
                    pe.wait_ge(s_silu, 2 * tile + 2)
                    if tile >= 2:
                        pe.wait_ge(s_x, tile - 1)
                    for c in range(NC):
                        o = ps[:, 4 + 2 * t + c // 4, (c % 4) * P:(c % 4 + 1) * P]
                        last = nc.tensor.transpose(o, dest(tile)[:, c * P:(c + 1) * P], ident)
                    last.then_inc(s_tr, 1)

            pe.wait_ge(d_hl, 2)
            wd = [v.rearrange("p (k n) -> p k n", k=KD) for v in (whi, wlo)]
            for h in range(2):
                last = split3(nc, ps[0:64, h, 0:HALF], [lambda k, v=v: v[:, k, :] for v in wd],
                              [lambda k, v=v: v[:, k, h * HALF:(h + 1) * HALF] for v in ht], KD)
            last.then_inc(d_pe, 1)
            pe.wait_ge(d_act, 1)
            for c in range(NC):
                last = nc.tensor.transpose(ps[:, 2, c * 64:(c + 1) * 64], dtT[:, c * P:(c + 1) * P], ident[0:64, 0:64])
            last.then_inc(d_pe, 1)
            for i in range(n):
                w.ready(pe, i)
                for t in range(2):
                    if i:
                        pe.wait_ge(s_pre, 3 * (2 * i + t - 1))
                    elif t:
                        pe.wait_ge(d_act, 3)
                    last = feature_tile(nc, w.parts(i, KD), t, ht, lambda h: halves(kit, t)[:, h, :], KD)
                    if t == 0:
                        last.then_inc(s_t0, 1)
                last.then_inc(w.used, 1)
                if i:
                    turn(i - 1)
            turn(n - 1)

        @block.scalar
        def _(act):
            act.wait_ge(d_in, 48)
            nc.scalar.activation(whi, raw, ACT.Copy).then_inc(d_hl, 1)
            act.wait_ge(d_pe, 1)
            nc.scalar.activation(dtT.rearrange("p (h n) -> p h n", h=2), ps[0:64, 0:2, 0:HALF], ACT.Identity,
                                 bias=bias).then_inc(d_act, 1)
            act.wait_ge(d_pe, 2)
            nc.scalar.activation(dx, ps[:, 2, 0:320], ACT.Copy).then_inc(d_act, 1)
            nc.scalar.activation(e, ps[:, 2, 0:320], ACT.Abs).then_inc(d_act, 1)
            act.wait_ge(d_act, 3)
            nc.scalar.activation(e, e, ACT.Exp, scale=-1.0).then_inc(d_act, 1)
            nc.scalar.activation(alog, alog, ACT.Exp).then_inc(d_act, 1)
            act.wait_ge(s_in, 32)
            act.wait_ge(s_pad, 3)

            def take_turned(i):
                for t in range(2):
                    tile = 2 * i + t
                    if not turned(tile):
                        continue
                    act.wait_ge(s_tr, tile + 1)
                    src = ps[:, 4 + 2 * t:6 + 2 * t, :].rearrange("p a b -> p (a b)")[:, 0:T].rearrange("p (c n) -> p c n", c=NC)
                    d = X[:, :, tile * P:(tile + 1) * P] if tile < 16 else Bt[:, :, (tile - 16) * P:(tile - 15) * P]
                    nc.scalar.activation(d, src, ACT.Copy).then_inc(s_x, 1)

            for i in range(n):
                if w.exists(i + 1):
                    w.split_hi(act, i + 1)
                for t in range(2):
                    act.wait_ge(*((s_t0, i + 1) if t == 0 else w.done(i)))
                    if i:
                        act.wait_ge(s_cv, TAPS * (2 * i + t - 1))
                    for a, b, o in ((0, P, 2), (P, HALF, 4)):
                        nc.scalar.activation(pre[:, t, a + o:b + o], ps[:, 2 * t, a:b], ACT.Copy).then_inc(s_pre, 1)
                    nc.scalar.activation(pre[:, t, HALF + 4:T + 4], ps[:, 2 * t + 1, 0:HALF], ACT.Copy).then_inc(s_pre, 1)
                if i:
                    take_turned(i - 1)
                for t in range(2):
                    tile = 2 * i + t
                    if tile == 16:
                        act.wait_ge(d_dve, DT_STEPS)
                    act.wait_ge(s_cv, TAPS * (tile + 1))
                    for a, b, o in ((0, P, 0), (P, T, 2)):
                        nc.scalar.activation(dest(tile)[:, a:b], acc[:, t, a + o:b + o], ACT.Silu,
                                             bias=cb[:, tile:tile + 1]).then_inc(s_silu, 1)
            take_turned(n - 1)

        @block.vector
        def _(dve):
            ch = Chain(dve, d_dve)
            dve.wait_ge(d_hl, 1)
            nc.vector.tensor_tensor(wlo, raw, whi.bitcast(F32), ALU.subtract).then_inc(d_hl, 1)
            dve.wait_ge(d_act, 5)
            ch.step(nc.vector.tensor_scalar(r, dx, 0.0, None, ALU.max))
            ch.step(nc.vector.tensor_scalar(sden, e, 2.0, None, ALU.add))
            ch.sync()
            ch.step(nc.vector.reciprocal(sden, sden))
            ch.sync()
            ch.step(nc.vector.tensor_tensor(s, e, sden, ALU.mult))
            ch.sync()
            ch.step(nc.vector.tensor_tensor(s2, s, s, ALU.mult))
            ch.sync()
            ch.step(nc.vector.tensor_scalar(q, s2, 1.0 / 17, None, ALU.mult))
            for odd in range(15, 1, -2):
                ch.sync()
                ch.step(nc.vector.scalar_tensor_tensor(out=q, in0=q, scalar=1.0 / odd, in1=s2, op0=ALU.add, op1=ALU.mult))
            ch.sync()
            ch.step(nc.vector.scalar_tensor_tensor(out=q, in0=q, scalar=1.0, in1=s, op0=ALU.add, op1=ALU.mult))
            ch.sync()
            dt = DT.rearrange("p c h -> p (c h)")
            ch.step(nc.vector.scalar_tensor_tensor(out=dt, in0=q, scalar=2.0, in1=r, op0=ALU.mult, op1=ALU.add))
            ch.sync()
            ch.step(nc.vector.scalar_tensor_tensor(out=A, in0=DT, scalar=-1.0,
                                                   in1=alog.unsqueeze(1).broadcast_to([P, NC, 64]),
                                                   op0=ALU.mult, op1=ALU.mult))
            assert ch.n == DT_STEPS
            for a, b in ((0, 2), (P + 2, P + 4), (W0 - 2, W0)):
                nc.vector.memset(pre[:, :, a:b], 0.0).then_inc(s_pad, 1)
            dve.wait_ge(s_in, 32)
            dve.wait_ge(s_pad, 3)
            for i in range(n):
                if w.exists(i + 1):
                    w.split_lo(dve, i + 1)
                for t in range(2):
                    tile = 2 * i + t
                    dve.wait_ge(s_pre, 3 * (tile + 1))
                    if i:
                        dve.wait_ge(s_silu, 2 * (tile - 1))
                    for k in range(TAPS):
                        src, tap = pre[:, t, k:k + W0 - 4], cw[:, tile, k:k + 1]
                        if k == 0:
                            nc.vector.tensor_scalar(acc[:, t, :], src, tap, None, ALU.mult).then_inc(s_cv, 1)
                        else:
                            dve.wait_ge(s_cv, TAPS * tile + k)
                            nc.vector.scalar_tensor_tensor(out=acc[:, t, :], in0=src, scalar=tap, in1=acc[:, t, :],
                                                           op0=ALU.mult, op1=ALU.add).then_inc(s_cv, 1)


def stage_gates(kit, stream, scr):
    nc, ps = kit.nc, kit.ps
    zs = kit.at(O_TMP, NC, UC)
    gs = kit.at(O_TMP + NC * UC, 2, T)
    ht = [kit.rnd(o, KD, T) for o in (O_H, O_H + 5120)]
    s_pe, s_silu, s_t0, s_sig = kit.sem("z_chunk"), kit.sem("z_silu"), kit.sem("z_tile0"), kit.sem("z_sigmoid")
    s_out = [kit.sem(f"z_stored{c}") for c in range(NC)]
    s_gout = [kit.sem(f"z_gate_stored{t}") for t in range(2)]
    nz, ng = 8, 4
    w = stream.section(nz + ng)
    with nc.Block() as block:
        @block.sync
        def _(sp):
            for i in w.to_load():
                w.load(sp, i)

        @block.tensor
        def _(pe):
            for i in range(nz):
                w.ready(pe, i)
                for c in range(NC):
                    if i:
                        pe.wait_ge(s_silu, NC * (i - 1) + c + 1)
                    last = token_tile(nc, w.parts(i, KD), c, ht, ps[:, c, 0:UC])
                    if c < NC - 1:
                        last.then_inc(s_pe, 1)
                last.then_inc(w.used, 1)
            pe.wait_ge(s_silu, NC * nz)
            for i in range(nz, nz + ng):
                w.ready(pe, i)
                for t in range(2):
                    if i > nz:
                        pe.wait_ge(s_sig, 2 * (i - nz - 1) + t + 1)
                    last = feature_tile(nc, w.parts(i, KD), t, ht, lambda h: halves(kit, t)[:, h, :], KD)
                    if t == 0:
                        last.then_inc(s_t0, 1)
                last.then_inc(w.used, 1)

        @block.scalar
        def _(act):
            for i in range(nz):
                w.split_hi(act, i + 1)
                for c in range(NC):
                    act.wait_ge(*((s_pe, (NC - 1) * i + c + 1) if c < NC - 1 else w.done(i)))
                    if i:
                        act.wait_ge(s_out[c], 16 * i)
                    nc.scalar.activation(zs[:, c, :], ps[:, c, 0:UC], ACT.Silu).then_inc(s_silu, 1)
            for i in range(nz, nz + ng):
                if w.exists(i + 1):
                    w.split_hi(act, i + 1)
                for t in range(2):
                    act.wait_ge(*((s_t0, i + 1 - nz) if t == 0 else w.done(i)))
                    if i > nz:
                        act.wait_ge(s_gout[t], 16 * (i - nz))
                    nc.scalar.activation(two(gs[:, t, :]), halves(kit, t), ACT.Sigmoid).then_inc(s_sig, 1)

        @block.vector
        def _(dve):
            for i in range(1, nz + ng):
                w.split_lo(dve, i)

        @block.gpsimd
        def _(pool):
            for i in range(nz):
                for c in range(NC):
                    pool.wait_ge(s_silu, NC * i + c + 1)
                    pool.dma_start(scr["z"][c * P:(c + 1) * P, i * UC:(i + 1) * UC], zs[:, c, :]).then_inc(s_out[c], 16)
            for i in range(ng):
                for t in range(2):
                    pool.wait_ge(s_sig, 2 * i + t + 1)
                    pool.dma_start(scr["gb"][2 * i + t], gs[:, t, :]).then_inc(s_gout[t], 16)
            for c in range(NC):
                pool.wait_ge(s_out[c], 16 * nz)
            for t in range(2):
                pool.wait_ge(s_gout[t], 16 * ng)


def stage_ssd(kit, io, scr, out):
    nc, ps = kit.nc, kit.ps
    hF, hB0 = kit.at(O_H, 4, INNER), kit.at(O_H + 4 * INNER, INNER)
    hB1 = kit.at(O_HL, INNER)
    RH, RL = kit.rnd(O_HL + 2048, 4, 512), kit.rnd(O_HL + 4096, 4, 512)
    GX, TT = (kit.at(O_HL + 6144 + 1024 * j, 2, 512) for j in range(2))
    M = GX
    SO = TT
    XD = kit.at(O_K + 848, 2, 512)
    gtr, ltr = kit.rnd(O_K + 1872, P), kit.rnd(O_K + 2000, P)
    AH = kit.rnd(O_TMP + 3360, NC, 64)
    EX = kit.at(O_TMP, 6, NC, 32)
    DD = kit.at(O_TMP + 960, 2, NC, 32)
    CB = kit.at(O_TMP + 1280, 2, 2, P)
    OF = kit.at(O_TMP + 1792, 2, 2, 256)
    YK = kit.at(O_TMP + 2816, 2, 256)
    DSK = kit.at(O_TMP + 3328, 32)
    HT_ = kit.at(O_RAW, 2, 512)
    V1 = kit.at(O_RAW + 1024, 2, 256)
    WM, BM, MR = kit.at(O_RAW + 1536, 2, 1024), kit.at(O_RAW + 3584, 2, P), kit.at(O_RAW + 3840, 2, P)
    cond, sc = kit.at(O_TMP + 4384, 16), kit.at(O_TMP + 4400, 16)
    DT, A = kit.at(O_TMP + 4480, NC, 64), kit.at(O_TMP + 4800, NC, 64)
    X, Bt = kit.at(O_X, NC, INNER), kit.at(O_BC + 5120, NC, G * P)
    BT, CT = kit.at(O_BC, G, T), kit.at(O_BC + 2560, G, T)
    sums = [(kit.const(m), d) for m, d in (("le", 0), ("gt", 0), ("one", 0), ("ge", 1), ("lt", 1), ("one", 1))]
    le, ge, gt, lt = (kit.const(m) for m in ("le", "ge", "gt", "lt"))

    names = ("states_loaded", "sums_done", "exps_done", "scales_done", "low_decays", "seg_done", "seg_exp",
             "upper_scaled", "cb_done", "cb_masked", "both_scaled", "matrix_ready", "y_done", "skip_ready",
             "y_steps", "state_product", "state_carried", "context_state")
    (states_loaded, sums_done, exps_done, scales_done, low_decays, seg_done, seg_exp, upper_scaled,
     cb_done, cb_masked, both_scaled, matrix_ready, y_done, skip_ready, y_steps, state_product,
     state_carried, context_state) = (
        kit.sem("s_" + x) for x in names)
    state_stored = [kit.sem(f"s_state_stored{j}") for j in range(2)]
    y_whole = kit.sem("y_whole")
    rows_weighed = [kit.sem(f"s_weighed{j}") for j in range(2)]
    a_split, high_decays = kit.sem("s_a_split"), kit.sem("s_r_high")
    cond_loaded, cond_silu, mod_done, mod_taken = (kit.sem("s_" + x) for x in ("cond", "cond_silu", "mod", "mod_row"))
    mod_weights, mod_stored = ([kit.sem(f"s_{x}{j}") for j in range(2)] for x in ("mod_weights", "mod_stored"))

    chunks = [4, 3, 2, 1, 0]
    subs = [(c, g, q) for c in chunks for g in range(G) for q in range(2)]
    NS, NL = len(subs), 32
    ev = lambda j: 5 * j if j <= NL else 5 * NL + 2 * (j - NL)
    ctx_states = [(d, 0, g) for d in range(2) for g in range(G)]
    fwd = [(0, c, g) for c in (1, 2, 3) for g in range(G)]
    bwd = [(1, c, g) for c in (4, 3, 2) for g in range(G)]
    states = ctx_states + fwd + bwd
    NX, NF = len(ctx_states), len(ctx_states) + len(fwd)
    bank_of = lambda x: 7 if x >= NF or x % 2 else 6
    hb = lambda c: (hB0, hB1)[(4 - c) % 2]
    x_at = {}
    for x, (d, c, g) in enumerate(bwd):
        x_at[subs.index((c, g, 0))] = NF + x
    cols = lambda g: slice(g * GW, (g + 1) * GW)
    heads4 = lambda g, q: slice(g * HPG + 4 * q, g * HPG + 4 * q + 4)
    byhead = lambda v, n: v.rearrange("p (h n) -> p h n", h=n)


    def weigh(eng, ops, x):
        d, c, g = states[x]
        if x >= 2:
            eng.wait_ge(state_product, x - 1)
        ops.tensor_tensor(byhead(XD[:, x % 2, :], HPG), byhead(X[:, c, cols(g)], HPG),
                          DD[:, d, c, g * HPG:(g + 1) * HPG].unsqueeze(2).broadcast_to([P, HPG, HD]),
                          ALU.mult).then_inc(rows_weighed[x % 2], 1)

    NP = 3 * D // P
    early = {x: i for i, x in enumerate(range(3, NF, 4))}
    EARLY = len(early)
    at_sub = {}
    for i in range(NP - EARLY):
        at_sub[i * NS // (NP - EARLY)] = EARLY + i
    with nc.Block() as block:
        @block.sync
        def _(sp):
            def load_piece(i):
                if i >= 2:
                    sp.wait_ge(mod_done, i - 1)
                sp.dma_start(WM[:, i % 2, :], io["w_mod_rest"][i]).then_inc(mod_weights[i % 2], 16)
                sp.dma_start(BM[0:1, i % 2, :], io["b_mod"][:, 2 * D + i * P:2 * D + (i + 1) * P]).then_inc(mod_weights[i % 2], 16)

            sp.dma_start(cond, io["cond"]).then_inc(cond_loaded, 16)
            load_piece(0)
            load_piece(1)
            sp.dma_start(hF[:, 0, :], io["state_t"][0]).then_inc(states_loaded, 16)
            sp.dma_start(hB0, io["state_t"][1]).then_inc(states_loaded, 16)
            sp.dma_start(DSK, io["d_skip"].partition_broadcast(P)).then_inc(states_loaded, 16)
            for x, (d, c, g) in enumerate(ctx_states):
                sp.wait_ge(context_state, x + 1)
                sp.dma_start(out["state"][d, cols(g), :].rearrange("(q p) n -> p q n", p=P),
                             SO[:, x % 2, :].rearrange("p (q n) -> p q n", q=4)).then_inc(state_stored[x % 2], 16)
            for i in range(NP):
                if i + 2 < NP:
                    load_piece(i + 2)
                sp.wait_ge(mod_taken, i + 1)
                sp.dma_start(scr["mod"][:, P * i:P * (i + 1)], MR[0:2, i % 2, :]).then_inc(mod_stored[i % 2], 16)
            for j in range(2):
                sp.wait_ge(state_stored[j], 16 * NX // 2)
                sp.wait_ge(mod_stored[j], 16 * NP // 2)

        @block.gpsimd
        def _(pool):
            def decays(j):
                c, g, q = subs[j]
                if j >= 2:
                    pool.wait_ge(seg_done, j - 1)
                for d, mask in ((0, le), (1, ge)):
                    hs = heads4(g, q)
                    av = A[:, c, 32 * d + hs.start:32 * d + hs.stop]
                    nc.gpsimd.tensor_tensor(byhead(RL[:, 2 * d + j % 2, :], 4), av.unsqueeze(2).broadcast_to([P, 4, P]),
                                            mask.unsqueeze(1).broadcast_to([P, 4, P]), ALU.mult).then_inc(low_decays, 1)

            def finish_y(j):
                c, g, q = subs[j]
                pool.wait_ge(y_steps, ev(j + 1))
                nc.gpsimd.tensor_tensor(X[:, c, g * GW + q * 256:g * GW + (q + 1) * 256], V1[:, j % 2, :],
                                        OF[:, j % 2, 1, :], ALU.add).then_inc(y_whole, 1)

            pool.wait_ge(scales_done, 2)
            pool.wait_ge(a_split, 4)
            for x in range(0, NF, 2):
                weigh(pool, nc.gpsimd, x)
            decays(0)
            decays(1)
            pool.wait_ge(states_loaded, 48)
            for j, (c, g, q) in enumerate(subs):
                if j + 2 < NS:
                    decays(j + 2)
                if j in x_at:
                    weigh(pool, nc.gpsimd, x_at[j])
                if j >= 2:
                    pool.wait_ge(y_steps, ev(j - 1))
                nc.gpsimd.tensor_tensor(byhead(YK[:, j % 2, :], 4), byhead(X[:, c, g * GW + q * 256:g * GW + (q + 1) * 256], 4),
                                        DSK[:, heads4(g, q)].unsqueeze(2).broadcast_to([P, 4, HD]),
                                        ALU.mult).then_inc(skip_ready, 1)
                if 2 <= j < NL + 2:
                    finish_y(j - 2)

        @block.tensor
        def _(pe):
            def state(x):
                d, c, g = states[x]
                pe.wait_ge(rows_weighed[x % 2], x // 2 + 1)
                if x >= NF:
                    pe.wait_ge(state_carried, x - NX)
                elif x >= NX + 2:
                    pe.wait_ge(state_carried, x - NX - 1)
                elif x >= 2:
                    pe.wait_ge(context_state, x - 1)
                b, bt = bank_of(x), Bt[:, c, g * P:(g + 1) * P]
                if x < NX:
                    for q in range(4):
                        last = nc.tensor.matmul(ps[:, b, q * P:(q + 1) * P], XD[:, x % 2, q * P:(q + 1) * P], bt,
                                                start=True, stop=True)
                else:
                    last = nc.tensor.matmul(ps[:, b, :], bt, XD[:, x % 2, :], start=True, stop=True)
                last.then_inc(state_product, 1)

            def prepare(j):
                c, g, q = subs[j]
                pe.wait_ge(low_decays, 2 * j + 2)
                if j >= 2:
                    pe.wait_ge(seg_exp, j - 1)
                pe.wait_ge(high_decays, 8 * (j + 1))
                for n, (mask, R) in enumerate(((gtr, RH[:, j % 2, :]), (gtr, RL[:, j % 2, :]),
                                               (ltr, RH[:, 2 + j % 2, :]), (ltr, RL[:, 2 + j % 2, :]))):
                    last = nc.tensor.matmul(ps[:, j % 2, :], mask, R, start=(n == 0), stop=(n == 3))
                last.then_inc(seg_done, 1)
                if q == 0:
                    gi = j // 2
                    if gi >= 2:
                        pe.wait_ge(cb_masked, 2 * (gi - 1))
                    pe.wait_ge(mod_taken, EARLY + sum(i < j - 1 for i in at_sub))
                    nc.tensor.matmul(ps[:, 4, (gi % 2) * P:(gi % 2 + 1) * P], BT[:, g, c * P:(c + 1) * P],
                                     CT[:, g, c * P:(c + 1) * P], start=True, stop=True).then_inc(cb_done, 1)

            def modulate(i, masked=0):
                pe.wait_ge(mod_weights[i % 2], 32 * (i // 2 + 1))
                if i:
                    pe.wait_ge(mod_taken, i)
                if masked:
                    pe.wait_ge(cb_masked, 2 * masked)
                o = ps[0:2, 4, 256 + (i % 2) * P:256 + (i % 2 + 1) * P]
                for k in range(KD):
                    nc.tensor.matmul(o, sc.rearrange("p (k s) -> p k s", s=2)[:, k, :], WM[:, i % 2, k * P:(k + 1) * P],
                                     start=(k == 0), stop=False)
                nc.tensor.matmul(o, kit.const("one")[0:1, 0:2], BM[0:1, i % 2, :], start=False, stop=True).then_inc(mod_done, 1)

            for n, (mask, d) in enumerate(sums):
                o = ps[:, n // 3, (n % 3) * 160:(n % 3 + 1) * 160]
                last = nc.tensor.matmul(o, mask, A[:, :, 32 * d:32 * d + 32], start=True, stop=True)
            last.then_inc(sums_done, 1)
            pe.wait_ge(cond_silu, 1)
            for x in range(NF):
                state(x)
                if x in early:
                    modulate(early[x])
            pe.wait_ge(exps_done, 2)
            prepare(0)
            for j, (c, g, q) in enumerate(subs):
                if j + 1 < NS:
                    prepare(j + 1)
                if j in x_at:
                    state(x_at[j])
                if j in at_sub:
                    modulate(at_sub[j], min((j + 1) // 2, NS // 2 - 1) + 1)
                if j >= 2:
                    pe.wait_ge(y_steps, ev(j - 1))
                elif j == 0:
                    pe.wait_ge(states_loaded, 48)
                    pe.wait_ge(state_carried, NF - NX)
                if c:
                    pe.wait_ge(state_carried, NF - NX + 4 * (4 - c))
                    ct = CT[:, g, c * P:(c + 1) * P]
                    w4 = slice(g * GW + q * 256, g * GW + (q + 1) * 256)
                    nc.tensor.matmul(ps[:, 5 + j % 2, 0:256], ct, hF[:, c - 1, w4], start=True, stop=True)
                    nc.tensor.matmul(ps[:, 5 + j % 2, 256:512], ct, hb(c)[:, w4], start=True, stop=True)
                pe.wait_ge(matrix_ready, j + 1)
                for h in range(4):
                    x0 = g * GW + q * 256 + (h // 2) * P
                    last = nc.tensor.matmul(ps[:, 2 + j % 2, h * P:(h + 1) * P], M[:, j % 2, h * P:(h + 1) * P],
                                            X[:, c, x0:x0 + P], start=True, stop=True)
                last.then_inc(y_done, 1)

        @block.scalar
        def _(act):
            act.wait_ge(cond_loaded, 16)
            nc.scalar.activation(sc, cond, ACT.Silu).then_inc(cond_silu, 1)
            nc.scalar.activation(AH, A, ACT.Copy).then_inc(a_split, 1)
            act.wait_ge(sums_done, 1)
            for n in range(2):
                nc.scalar.activation(EX[:, 3 * n:3 * n + 3, :, :].rearrange("p a b c -> p (a b c)"), ps[:, n, 0:480],
                                     ACT.Exp).then_inc(exps_done, 1)
            for x in range(NX):
                act.wait_ge(state_product, x + 1)
                if x >= 2:
                    act.wait_ge(state_stored[x % 2], 16 * (x // 2))
                nc.scalar.activation(SO[:, x % 2, :], ps[:, bank_of(x), :], ACT.Copy).then_inc(context_state, 1)

            def decays(j):
                c, g, q = subs[j]
                if j >= 2:
                    act.wait_ge(seg_done, j - 1)
                for d, mask in ((0, le), (1, ge)):
                    for h in range(4):
                        hs = 32 * d + heads4(g, q).start + h
                        nc.scalar.activation(RH[:, 2 * d + j % 2, h * P:(h + 1) * P], mask, ACT.Copy,
                                             scale=AH[:, c, hs:hs + 1].bitcast(F32)).then_inc(high_decays, 1)

            act.wait_ge(a_split, 1)
            decays(0)
            decays(1)
            for j in range(2):
                act.wait_ge(state_stored[j], 16 * NX // 2)
            for j, (c, g, q) in enumerate(subs):
                act.wait_ge(seg_done, j + 1)
                if j >= 2:
                    act.wait_ge(y_done, j - 1)
                nc.scalar.activation(GX[:, j % 2, :], ps[:, j % 2, :], ACT.Exp).then_inc(seg_exp, 1)
                act.wait_ge(cb_masked, 2 * (j // 2) + 2)
                for h in range(4):
                    dt = DT[:, c, g * HPG + 4 * q + h:g * HPG + 4 * q + h + 1]
                    nc.scalar.activation(TT[:, j % 2, h * P:(h + 1) * P], CB[:, (j // 2) % 2, 0, :], ACT.Copy,
                                         scale=dt).then_inc(upper_scaled, 1)
                if j + 2 < NS:
                    decays(j + 2)

        @block.vector
        def _(dve):
            nc.vector.tensor_copy(gtr, gt).then_inc(a_split, 1)
            nc.vector.tensor_copy(ltr, lt).then_inc(a_split, 1)
            dve.wait_ge(sums_done, 1)
            dve.wait_ge(a_split, 3)
            nc.vector.tensor_tensor(A, A, AH.bitcast(F32), ALU.subtract).then_inc(a_split, 1)
            dve.wait_ge(exps_done, 2)
            for d in range(2):
                nc.vector.tensor_tensor(DD[:, d, :, :], DT[:, :, 32 * d:32 * d + 32], EX[:, 3 * d + 1, :, :],
                                        ALU.mult).then_inc(scales_done, 1)

            def carry(x):
                d, c, g = states[x]
                if d == 0:
                    src, dst = hF[:, c - 1, cols(g)], hF[:, c, cols(g)]
                else:
                    src, dst = hb(c)[:, cols(g)], hb(c - 1)[:, cols(g)]
                    dve.wait_ge(y_done, 8 * (4 - c))
                dec = EX[:, 3 * d + 2, c, g * HPG:(g + 1) * HPG].unsqueeze(2).broadcast_to([P, HPG, HD])
                n = x - NX
                nc.vector.tensor_tensor(byhead(HT_[:, x % 2, :], HPG), byhead(src, HPG), dec, ALU.mult).then_inc(scales_done, 1)
                dve.wait_ge(scales_done, 3 + n)
                dve.wait_ge(state_product, x + 1)
                nc.vector.tensor_tensor(dst, HT_[:, x % 2, :], ps[:, bank_of(x), :], ALU.add).then_inc(state_carried, 1)

            def take_modulation(i):
                dve.wait_ge(mod_done, i + 1)
                if i >= 2:
                    dve.wait_ge(mod_stored[i % 2], 16 * (i // 2))
                nc.vector.tensor_copy(MR[0:2, i % 2, :], ps[0:2, 4, 256 + (i % 2) * P:256 + (i % 2 + 1) * P]).then_inc(mod_taken, 1)

            dve.wait_ge(scales_done, 2)
            for x in range(NX):
                if x % 2:
                    weigh(dve, nc.vector, x)
                if x in early:
                    take_modulation(early[x])
            weigh(dve, nc.vector, NX + 1)
            dve.wait_ge(states_loaded, 48)
            for x in range(NX, NF):
                if x >= NX + 4:
                    dve.wait_ge(state_carried, x - NX - 3)
                carry(x)
                if x % 2 and x + 2 < NF:
                    weigh(dve, nc.vector, x + 2)
                if x in early:
                    take_modulation(early[x])

            def masks(gi):
                dve.wait_ge(cb_done, gi + 1)
                src = ps[:, 4, (gi % 2) * P:(gi % 2 + 1) * P]
                if gi >= 2:
                    dve.wait_ge(upper_scaled, 8 * (gi - 1))
                    dve.wait_ge(both_scaled, 8 * (gi - 1))
                nc.vector.tensor_tensor(CB[:, gi % 2, 0, :], src, le, ALU.mult).then_inc(cb_masked, 1)
                nc.vector.tensor_tensor(CB[:, gi % 2, 1, :], src, ge, ALU.mult).then_inc(cb_masked, 1)

            def take_y(j):
                c, g, q = subs[j]
                w4 = slice(g * GW + q * 256, g * GW + (q + 1) * 256)
                v = ps[:, 2 + j % 2, :].rearrange("p (a n) -> p a n", a=2)
                n = ev(j)
                dve.wait_ge(y_done, j + 1)
                dve.wait_ge(skip_ready, j + 1)
                dst = V1[:, j % 2, :] if c else X[:, c, w4]
                if c and j >= 2:
                    dve.wait_ge(y_whole, j - 1)
                if c:
                    for d in range(2):
                        nc.vector.tensor_tensor(byhead(OF[:, j % 2, d, :], 4), byhead(ps[:, 5 + j % 2, 256 * d:256 * d + 256], 4),
                                                EX[:, 3 * d, c, heads4(g, q)].unsqueeze(2).broadcast_to([P, 4, HD]),
                                                ALU.mult).then_inc(y_steps, 1)
                for e in range(2):
                    o = e * (P + HD)
                    nc.vector.tensor_tensor(dst.rearrange("p (a e n) -> p a e n", a=2, e=2)[:, :, e, :], v[:, :, o:o + HD],
                                            YK[:, j % 2, :].rearrange("p (a e n) -> p a e n", a=2, e=2)[:, :, e, :],
                                            ALU.add).then_inc(y_steps, 1)
                if c:
                    dve.wait_ge(y_steps, n + 4)
                    nc.vector.tensor_tensor(dst, dst, OF[:, j % 2, 0, :], ALU.add).then_inc(y_steps, 1)

            masks(0)
            for j, (c, g, q) in enumerate(subs):
                if j % 2 and j + 1 < NS:
                    masks((j + 1) // 2)
                dve.wait_ge(upper_scaled, 4 * j + 4)
                dve.wait_ge(cb_masked, 2 * (j // 2) + 2)
                for h in range(4):
                    dt = DT[:, c, 32 + g * HPG + 4 * q + h:32 + g * HPG + 4 * q + h + 1]
                    tt = TT[:, j % 2, h * P:(h + 1) * P]
                    nc.vector.scalar_tensor_tensor(out=tt, in0=CB[:, (j // 2) % 2, 1, :], scalar=dt, in1=tt,
                                                   op0=ALU.mult, op1=ALU.add).then_inc(both_scaled, 1)
                dve.wait_ge(both_scaled, 4 * j + 4)
                dve.wait_ge(seg_exp, j + 1)
                if j >= 2:
                    dve.wait_ge(y_done, j - 1)
                nc.vector.tensor_tensor(M[:, j % 2, :], TT[:, j % 2, :], GX[:, j % 2, :], ALU.mult).then_inc(matrix_ready, 1)
                if j:
                    take_y(j - 1)
                if j in at_sub:
                    take_modulation(at_sub[j])
                if j in x_at:
                    x = x_at[j]
                    dve.wait_ge(state_carried, x - NX - 3)
                    carry(x)
            take_y(NS - 1)


def stage_norm_y(kit, stream, io, scr):
    nc, ps = kit.nc, kit.ps
    X = kit.at(O_X, NC, INNER)
    Z = [kit.at(O_HL + o, INNER) for o in (UNIT, 3 * UNIT)]
    hi, lo = kit.rnd(O_H, KI, T), kit.rnd(O_BC, KI, T)
    nw, ssq, rr = kit.at(O_TMP + 2560, KI), kit.at(O_TMP + 2580, NC * G), kit.at(O_TMP + 2600, NC * G)
    sq = kit.at(O_TMP + 2656, GW)
    ident = kit.const("ident")
    (s_in, s_y, s_ms, s_root, s_r, s_sq, s_tr, s_hi, s_lo) = (
        kit.sem("n_" + x) for x in ("in", "y", "mean", "root", "scaled", "squares", "turned", "hi", "lo"))
    s_z = [kit.sem(f"n_z{j}") for j in range(2)]
    w = stream.section(0)
    bank = lambda c, g: 4 * (c % 2) + g

    with nc.Block() as block:
        @block.sync
        def _(sp):
            for c in range(NC):
                if c >= 2:
                    sp.wait_ge(s_y, c - 1)
                sp.dma_start(Z[c % 2], scr["z"][c * P:(c + 1) * P, :]).then_inc(s_z[c % 2], 16)
                if c == 1:
                    sp.dma_start(nw, io["ssd_nw"]).then_inc(s_in, 16)
            for i in w.to_load():
                w.load(sp, i)

        @block.gpsimd
        def _(pool):
            pool.wait_ge(s_y, 1)
            for c in range(1, NC):
                pool.wait_ge(s_z[c % 2], 16 * (c // 2 + 1))
                nc.gpsimd.tensor_tensor(X[:, c, :], X[:, c, :], Z[c % 2], ALU.mult).then_inc(s_y, 1)

        @block.tensor
        def _(pe):
            for c in range(NC):
                for g in range(G):
                    pe.wait_ge(s_r, G * c + g + 1)
                    if c >= 2:
                        pe.wait_ge(s_lo, KI * (c - 2) + 4 * g + 4)
                    for q in range(4):
                        k = 4 * g + q
                        last = nc.tensor.transpose(ps[:, bank(c, g), q * P:(q + 1) * P], X[:, c, k * P:(k + 1) * P], ident)
                    last.then_inc(s_tr, 1)

        @block.scalar
        def _(act):
            def squares(c):
                act.wait_ge(s_y, c + 1)
                for g in range(G):
                    if c or g:
                        act.wait_ge(s_sq, G * c + g)
                    nc.scalar.activation(sq, X[:, c, g * GW:(g + 1) * GW], ACT.Square,
                                         accum_out=ssq[:, c * G + g:c * G + g + 1]).then_inc(s_sq, 1)

            def root(c):
                act.wait_ge(s_ms, 2 * c + 2)
                nc.scalar.activation(rr[:, c * G:(c + 1) * G], rr[:, c * G:(c + 1) * G], ACT.Sqrt).then_inc(s_root, 1)

            squares(0)
            root(0)
            act.wait_ge(s_in, 16)
            for c in range(NC):
                if c + 1 < NC:
                    squares(c + 1)
                for g in range(G):
                    act.wait_ge(s_tr, G * c + g + 1)
                    for q in range(4):
                        k = 4 * g + q
                        nc.scalar.activation(hi[:, k, c * P:(c + 1) * P], ps[:, bank(c, g), q * P:(q + 1) * P],
                                             ACT.Copy, scale=nw[:, k:k + 1]).then_inc(s_hi, 1)
                    if g == 1 and c + 1 < NC:
                        root(c + 1)
            w.split_hi(act, 0)

        @block.vector
        def _(dve):
            def mean(c):
                sl = slice(c * G, (c + 1) * G)
                dve.wait_ge(s_sq, G * (c + 1))
                nc.vector.tensor_scalar(ssq[:, sl], ssq[:, sl], 1.0 / GW, EPS, ALU.mult, ALU.add).then_inc(s_ms, 1)
                dve.wait_ge(s_ms, 2 * c + 1)
                nc.vector.reciprocal(rr[:, sl], ssq[:, sl]).then_inc(s_ms, 1)

            def scale(c):
                dve.wait_ge(s_root, c + 1)
                for g in range(G):
                    v = X[:, c, g * GW:(g + 1) * GW]
                    nc.vector.tensor_scalar(v, v, rr[:, c * G + g:c * G + g + 1], None, ALU.mult).then_inc(s_r, 1)

            dve.wait_ge(s_z[0], 16)
            nc.vector.tensor_tensor(X[:, 0, :], X[:, 0, :], Z[0], ALU.mult).then_inc(s_y, 1)
            mean(0)
            scale(0)
            for c in range(NC):
                if c + 1 < NC:
                    mean(c + 1)
                for g in range(G):
                    dve.wait_ge(s_hi, KI * c + 4 * g + 4)
                    for q in range(4):
                        k, src = 4 * g + q, slice(c * P, (c + 1) * P)
                        nc.vector.scalar_tensor_tensor(out=lo[:, k, src], in0=ps[:, bank(c, g), q * P:(q + 1) * P],
                                                       scalar=nw[:, k:k + 1], in1=hi[:, k, src].bitcast(F32),
                                                       op0=ALU.mult, op1=ALU.subtract).then_inc(s_lo, 1)
                    if g == 1 and c + 1 < NC:
                        scale(c + 1)
            w.split_lo(dve, 0)


def stage_branch_b(kit, stream, scr):
    nc = kit.nc
    y = [kit.rnd(o, KI, T) for o in (O_H, O_BC)]
    MG = kit.at(O_MG, KD, T)
    hi, lo = kit.rnd(O_X, KD, T), kit.rnd(O_X + 5120, KD, T)
    gate, v = kit.at(O_TMP + 2560, 2, T), kit.at(O_TMP + 3840, 2, T)
    w = stream.section(8)
    s_g = [kit.sem(f"b_gate{j}") for j in range(2)]
    s_v, s_hi, s_lo = kit.sem("b_merged"), kit.sem("b_hi"), kit.sem("b_lo")
    with nc.Block() as block:
        @block.sync
        def _(sp):
            for i in range(8):
                if i >= 2:
                    sp.wait_ge(s_v, 2 * (i - 2) + 1)
                sp.dma_start(gate[:, i % 2, :], scr["gb"][i]).then_inc(s_g[i % 2], 16)
                w.load(sp, i + 2)

        @block.tensor
        def _(pe):
            for i in range(8):
                w.ready(pe, i)
                if i >= 2:
                    pe.wait_ge(s_v, 2 * (i - 2) + 1)
                feature_tile(nc, w.parts(i, KI), 0, y, lambda h: halves(kit, i % 2)[:, h, :], KI).then_inc(w.used, 1)

        @block.scalar
        def _(act):
            for i in range(8):
                if w.exists(i + 1):
                    w.split_hi(act, i + 1)
                act.wait_ge(s_v, 2 * i + 2)
                nc.scalar.activation(hi[:, i, :], v[:, i % 2, :], ACT.Copy).then_inc(s_hi, 1)

        @block.vector
        def _(dve):
            for i in range(8):
                if w.exists(i + 1):
                    w.split_lo(dve, i + 1)
                dve.wait_ge(*w.done(i))
                dve.wait_ge(s_g[i % 2], 16 * (i // 2 + 1))
                nc.vector.tensor_tensor(two(v[:, i % 2, :]), halves(kit, i % 2), two(gate[:, i % 2, :]), ALU.mult).then_inc(s_v, 1)
                dve.wait_ge(s_v, 2 * i + 1)
                nc.vector.tensor_tensor(v[:, i % 2, :], v[:, i % 2, :], MG[:, i, :], ALU.add).then_inc(s_v, 1)
                dve.wait_ge(s_hi, i + 1)
                nc.vector.tensor_tensor(lo[:, i, :], v[:, i % 2, :], hi[:, i, :].bitcast(F32), ALU.subtract).then_inc(s_lo, 1)
                dve.wait_ge(s_lo, i + 1)


T_G2, T_FN, T_RT = O_TMP, O_TMP + 2048, O_TMP + 3072


class Routing:

    def __init__(self, kit):
        self.slot = [kit.at(T_RT + 8 * k, NC).bitcast(U32) for k in range(2)]
        self.weight = kit.at(T_RT + 16, 2, NC)
        self.table = kit.at(T_RT + 26, NMB + 1)[0:1].bitcast(I32)
        self.bias = kit.at(T_RT + 64, NE)
        self.work = T_RT + 64 + NE


def stage_out(kit, stream, io, scr, ex):
    nc, ps = kit.nc, kit.ps
    x2, h2 = kit.at(O_H, NC, D), kit.at(O_H + 5120, NC, D)
    merged = [kit.rnd(o, KD, T) for o in (O_X, O_X + 5120)]
    G1, S2, A2, N2 = kit.at(O_BC, 2, D), kit.at(O_BC + 2048, 2, D), kit.at(O_BC + 4096, 2, D), kit.at(O_BC + 6144, D)
    FN = kit.at(T_FN, D)
    hT = kit.at(O_MG, 2, KD, P)
    rw = kit.at(O_MG + 2048, KD, NE)
    sq = kit.at(O_MG + 2176, D)
    prod = kit.at(O_MG + 3200, 2, UC)
    ssq, rr = kit.at(O_MG + 3712, NC), kit.at(O_MG + 3720, NC)
    score = kit.at(O_MG + 3728, NC, NE)
    ident = kit.const("ident")
    w = stream.section(4)
    (s_in, s_x, s_pe, s_x2, s_p, s_a2, s_sq, s_rt, s_ms, s_h2, s_tr, s_ht, s_rr, s_sc) = (
        kit.sem("o_" + v) for v in ("in", "x", "chunk", "x2", "product", "scale", "squares", "root", "mean", "h2",
                                    "turned", "ht", "router", "scores"))
    with nc.Block() as block:
        @block.sync
        def _(sp):
            sp.dma_start(x2, scr["xp"].rearrange("(c p) d -> p c d", p=P)).then_inc(s_x, 16)
            for q, dst in enumerate((G1, S2, A2)):
                for st in range(2):
                    sp.dma_start(dst[:, st, :], scr["mod"][st:st + 1, q * D:(q + 1) * D].partition_broadcast(P)).then_inc(s_in, 16)
            sp.dma_start(N2, io["norm2"].partition_broadcast(P)).then_inc(s_in, 16)
            sp.dma_start(FN, io["fnorm"].partition_broadcast(P)).then_inc(s_in, 16)
            sp.dma_start(Routing(kit).bias, io["router_b"].partition_broadcast(P)).then_inc(s_in, 16)
            sp.dma_start(rw, io["router_w"].rearrange("p (k e) -> p k e", k=KD)).then_inc(s_in, 16)
            for i in w.to_load():
                w.load(sp, i)
            sp.wait_ge(*w.done(3))
            for q in range(6):
                ex.load(sp, io, 0, q)

        @block.tensor
        def _(pe):
            def project(i, c):
                if i:
                    pe.wait_ge(s_p, NC * (i - 1) + c + 1)
                last = token_tile(nc, w.parts(i, KD), c, merged, ps[:, c, 0:UC])
                last.then_inc(s_pe if c < NC - 1 else w.used, 1)

            def turn(c):
                pe.wait_ge(s_h2, 2 * c + 2)
                if c:
                    pe.wait_ge(s_ht, c)
                for k in range(KD):
                    last = nc.tensor.transpose(ps[:, 5 + k // 4, (k % 4) * P:(k % 4 + 1) * P], h2[:, c, k * P:(k + 1) * P], ident)
                last.then_inc(s_tr, 1)

            def route(c):
                pe.wait_ge(s_ht, c + 1)
                for k in range(KD):
                    last = nc.tensor.matmul(ps[:, 7, c * NE:(c + 1) * NE], hT[:, c % 2, k, :], rw[:, k, :],
                                            start=(k == 0), stop=(k == KD - 1))
                last.then_inc(s_rr, 1)

            for i in range(3):
                w.ready(pe, i)
                for c in range(NC):
                    project(i, c)
            w.ready(pe, 3)
            pe.wait_ge(s_in, 160)
            for c in range(NC):
                project(3, c)
                if c >= 2:
                    turn(c - 2)
                if c >= 3:
                    route(c - 3)
            turn(3)
            route(2)
            turn(4)
            route(3)
            route(4)

        @block.scalar
        def _(act):
            for i in range(3):
                w.split_hi(act, i + 1)

            def take_turned(c):
                act.wait_ge(s_tr, c + 1)
                if c >= 2:
                    act.wait_ge(s_rr, c - 1)
                nc.scalar.activation(hT[:, c % 2, :, :].rearrange("p k n -> p (k n)"),
                                     ps[:, 5:7, :].rearrange("p a b -> p (a b)"), ACT.Copy).then_inc(s_ht, 1)

            for c in range(NC):
                act.wait_ge(s_x2, NC * 3 + c + 1)
                if c:
                    act.wait_ge(s_sq, c)
                nc.scalar.activation(sq, x2[:, c, :], ACT.Square, accum_out=ssq[:, c:c + 1]).then_inc(s_sq, 1)
                act.wait_ge(s_ms, 2 * c + 2)
                nc.scalar.activation(rr[:, c:c + 1], rr[:, c:c + 1], ACT.Sqrt).then_inc(s_rt, 1)
                if c >= 2:
                    take_turned(c - 2)
            take_turned(3)
            take_turned(4)
            act.wait_ge(s_rr, NC)
            nc.scalar.activation(score.rearrange("p c e -> p (c e)"), ps[:, 7, 0:NC * NE], ACT.Sigmoid).then_inc(s_sc, 1)

        @block.vector
        def _(dve):
            w.split_lo(dve, 1)
            dve.wait_ge(s_in, 160)
            dve.wait_ge(s_x, 16)
            for st in range(2):
                nc.vector.scalar_tensor_tensor(out=A2[:, st, :], in0=A2[:, st, :], scalar=1.0, in1=N2,
                                               op0=ALU.add, op1=ALU.mult).then_inc(s_a2, 1)

            def norm(c):
                st = min(c, 1)
                dve.wait_ge(s_sq, c + 1)
                nc.vector.tensor_scalar(ssq[:, c:c + 1], ssq[:, c:c + 1], 1.0 / D, EPS, ALU.mult, ALU.add).then_inc(s_ms, 1)
                dve.wait_ge(s_ms, 2 * c + 1)
                nc.vector.reciprocal(rr[:, c:c + 1], ssq[:, c:c + 1]).then_inc(s_ms, 1)
                dve.wait_ge(s_rt, c + 1)
                dve.wait_ge(s_a2, 2)
                nc.vector.scalar_tensor_tensor(out=h2[:, c, :], in0=x2[:, c, :], scalar=rr[:, c:c + 1], in1=A2[:, st, :],
                                               op0=ALU.mult, op1=ALU.mult).then_inc(s_h2, 1)
                dve.wait_ge(s_h2, 2 * c + 1)
                nc.vector.tensor_tensor(h2[:, c, :], h2[:, c, :], S2[:, st, :], ALU.add).then_inc(s_h2, 1)

            for i in range(4):
                if i and i + 1 < 4:
                    w.split_lo(dve, i + 1)
                cols = slice(i * UC, (i + 1) * UC)
                for c in range(NC):
                    n = NC * i + c
                    if c < NC - 1:
                        dve.wait_ge(s_pe, (NC - 1) * i + c + 1)
                    else:
                        dve.wait_ge(*w.done(i))
                    nc.vector.tensor_tensor(prod[:, n % 2, :], ps[:, c, 0:UC], G1[:, min(c, 1), cols], ALU.mult).then_inc(s_p, 1)
                    dve.wait_ge(s_p, n + 1)
                    nc.vector.tensor_tensor(x2[:, c, cols], x2[:, c, cols], prod[:, n % 2, :], ALU.add).then_inc(s_x2, 1)
                    if i == 3 and c:
                        norm(c - 1)
            norm(NC - 1)


def stage_route(kit, io, scr, ex):
    nc, ps = kit.nc, kit.ps
    r = Routing(kit)
    h2 = kit.at(O_H + 5120, NC, D)
    score = kit.at(O_MG + 3728, NC, NE)
    at = [r.work]

    def take(*dims):
        n = 1
        for d in dims:
            n *= d
        at[0] += n
        return kit.at(at[0] - n, *dims)

    sel, selm, m1, m2, tmp, slot = (take(NC, NE) for _ in range(6))
    q20 = [take(NC * NG) for _ in range(7)]
    five, gmax = take(NC), take(NC)
    cnt, ext, pre, ca, cb = (take(NE) for _ in range(5))
    over = take(10, NE)
    tabf = take(NMB + 1)
    w12 = r.weight
    sbf = take(NC * NE // 2).bitcast(BF16).rearrange("p (c e) -> p c e", c=NC)
    ltb, oneb = take(P // 2).bitcast(BF16), take(P // 2).bitcast(BF16)
    assert at[0] <= O_MG
    s_v, s_pe, s_ready, s_mask = kit.sem("r_steps"), kit.sem("r_ranks"), kit.sem("r_slots"), kit.sem("r_chosen")
    s_sc = kit.sem("r_scattered")
    pri16, pri4, e128, thr = (kit.const(n, k) for n, k in (("pri16", NE), ("pri4", NG), ("e128", NE), ("thr", 5)))
    col = kit.const("col", 26)
    bc = lambda v, n: v.unsqueeze(2).broadcast_to([P, v.shape[1], n])
    over_c = lambda v: v.unsqueeze(1).broadcast_to([P, NC, v.shape[1]])

    ex.parts()
    zero = Pair(None, 0)
    NP, SLOTS = D // P, 5
    WM, G2 = kit.at(ex.rows, SLOTS, D), kit.at(T_G2, 2, D)
    BM, MR = kit.at(O_MG, D), kit.at(O_MG + D, D)
    cond, sc = kit.at(O_MG + 2 * D, 16), kit.at(O_MG + 2 * D + 16, 16)
    s_w = [kit.sem(f"r_mod_weights{j}") for j in range(SLOTS)]
    s_cond, s_silu, s_bias, s_mod, s_row, s_stored, s_g2 = (
        kit.sem("r_" + n) for n in ("cond", "cond_silu", "mod_bias", "mod", "mod_row", "mod_stored", "gate"))
    with nc.Block() as block:
        @block.sync
        def _(sp):
            def load_piece(i):
                if i >= SLOTS:
                    sp.wait_ge(s_mod, i - SLOTS + 1)
                sp.dma_start(WM[:, i % SLOTS, :], io["w_mod_rest"][3 * NP + i]).then_inc(s_w[i % SLOTS], 16)

            sp.dma_start(cond, io["cond"]).then_inc(s_cond, 16)
            for i in range(SLOTS):
                load_piece(i)
            sp.dma_start(BM[0:1], io["b_mod"][:, 5 * D:6 * D]).then_inc(s_bias, 16)
            for q in range(3):
                sp.wait_ge(ex.lo_ready, q + 1)
                ex.load(sp, io, 1, q)
                load_piece(SLOTS + q)
            sp.wait_ge(s_row, 2)
            sp.dma_start(scr["mod"][:, 3 * D:4 * D], MR[0:2]).then_inc(s_stored, 16)
            sp.wait_ge(s_stored, 16)
            for st in range(2):
                sp.dma_start(G2[:, st, :], scr["mod"][st:st + 1, 3 * D:4 * D].partition_broadcast(P)).then_inc(s_g2, 16)
            sp.wait_ge(s_g2, 32)

        @block.scalar
        def _(act):
            act.wait_ge(s_cond, 16)
            nc.scalar.activation(sc, cond, ACT.Silu).then_inc(s_silu, 1)
            for q in range(3):
                ex.split_hi(act, 0, zero, q)
            for h in range(2):
                act.wait_ge(s_mod, (h + 1) * NP // 2)
                nc.scalar.activation(MR[0:2, h * 512:(h + 1) * 512], ps[0:2, 2 + h, :], ACT.Copy).then_inc(s_row, 1)

        @block.vector
        def _(dve):
            ch = Chain(dve, s_v)
            tt = nc.vector.tensor_tensor

            def do(ins):
                ch.step(ins)
                ch.sync()

            def first_of(out, values, pri, width):
                do(nc.vector.tensor_reduce(five, values, AX.X, ALU.max))
                do(tt(out, values, bc(five, width), ALU.is_equal))
                do(tt(out, out, over_c(pri), ALU.mult))
                do(nc.vector.tensor_reduce(gmax, out, AX.X, ALU.max))
                do(tt(out, out, bc(gmax, width), ALU.is_equal))

            do(nc.vector.tensor_copy(ltb, kit.const("lt")))
            do(nc.vector.tensor_copy(oneb, kit.const("one")))
            do(tt(sel, score, over_c(r.bias), ALU.add))
            v = sel.rearrange("p c (g e) -> p (c g) e", e=4)
            hi1, hi2, lo1, lo2, best, gs, keep = q20
            for o, a, op in ((hi1, 0, ALU.max), (lo1, 0, ALU.min), (hi2, 2, ALU.max), (lo2, 2, ALU.min)):
                do(tt(o, v[:, :, a], v[:, :, a + 1], op))
            do(tt(gs, hi1, hi2, ALU.min))
            do(tt(lo1, lo1, lo2, ALU.max))
            do(tt(gs, gs, lo1, ALU.max))
            do(tt(hi1, hi1, hi2, ALU.max))
            do(tt(gs, hi1, gs, ALU.add))
            best3 = best.rearrange("p (c g) -> p c g", c=NC)
            first_of(best3, gs.rearrange("p (c g) -> p c g", c=NC), pri4, NG)
            do(nc.vector.tensor_scalar(keep, best, BIG, -BIG, ALU.mult, ALU.add))
            sm = selm.rearrange("p c (g e) -> p (c g) e", e=4)
            do(tt(sm, v, bc(best, 4), ALU.mult))
            do(tt(sm, sm, bc(keep, 4), ALU.add))
            first_of(m1, selm, pri16, NE)
            do(nc.vector.scalar_tensor_tensor(out=selm, in0=m1, scalar=-2.0 * BIG, in1=selm, op0=ALU.mult, op1=ALU.add))
            first_of(m2, selm, pri16, NE)
            do(tt(tmp, m1, m2, ALU.add))
            nc.vector.tensor_copy(sbf, tmp).then_inc(s_mask, 1)
            for k, m in enumerate((m1, m2)):
                do(tt(tmp, m, score, ALU.mult) if k else tt(slot, m, score, ALU.mult))
            do(nc.vector.tensor_reduce(w12[:, 0, :], slot, AX.X, ALU.add))
            do(nc.vector.tensor_reduce(w12[:, 1, :], tmp, AX.X, ALU.add))
            do(tt(five, w12[:, 0, :], w12[:, 1, :], ALU.add))
            do(nc.vector.reciprocal(five, five))
            do(tt(w12, w12, five.unsqueeze(1).broadcast_to([P, 2, NC]), ALU.mult))
            dve.wait_ge(s_pe, 1)
            do(nc.vector.tensor_copy(cnt, ps[:, 1, 0:NE]))
            do(nc.vector.tensor_scalar(ext, cnt, 128.0, None, ALU.is_gt))
            for m in range(2, NC):
                do(nc.vector.scalar_tensor_tensor(out=ext, in0=cnt, scalar=128.0 * m, in1=ext, op0=ALU.is_gt, op1=ALU.add))
            src, dst = ext, ca
            for sh in (1, 2, 4, 8):
                do(nc.vector.tensor_copy(dst[:, 0:sh], src[:, 0:sh]))
                do(tt(dst[:, sh:NE], src[:, sh:NE], src[:, 0:NE - sh], ALU.add))
                src, dst = dst, (cb if dst is ca else ca)
            cum = src
            do(tt(pre, cum, ext, ALU.subtract))
            do(nc.vector.tensor_scalar(pre, pre, 128.0, 16.0 * 128 - 128, ALU.mult, ALU.add))
            rank = ps[:, 0, 0:NC * NE].rearrange("p (c e) -> p c e", c=NC)
            do(nc.vector.tensor_copy(tmp, rank))
            do(tt(slot, tmp, over_c(pre), ALU.add))
            do(tt(pre, e128, pre, ALU.subtract))
            do(nc.vector.scalar_tensor_tensor(out=tmp, in0=tmp, scalar=128.0, in1=over_c(pre), op0=ALU.is_lt, op1=ALU.mult))
            do(tt(slot, slot, tmp, ALU.add))
            for k, m in enumerate((m1, m2)):
                do(tt(tmp, m, slot, ALU.mult))
                do(nc.vector.tensor_reduce(five, tmp, AX.X, ALU.add))
                do(nc.vector.tensor_copy(r.slot[k], five))
            one = lambda v: v[0:1]
            do(tt(one(over), one(col)[:, 0:10].unsqueeze(2).broadcast_to([1, 10, NE]),
                  one(cum).unsqueeze(1).broadcast_to([1, 10, NE]), ALU.is_ge))
            do(nc.vector.tensor_reduce(one(tabf)[:, NE:NMB], one(over), AX.X, ALU.add))
            do(nc.vector.tensor_scalar(one(tabf)[:, NE:NMB], one(tabf)[:, NE:NMB], NE - 1.0, None, ALU.min))
            do(nc.vector.tensor_copy(one(tabf)[:, 0:NE], one(col)[:, 0:NE]))
            do(nc.vector.tensor_scalar(one(five), one(thr), one(cum)[:, NE - 1:NE], None, ALU.is_lt))
            do(nc.vector.tensor_reduce(one(tabf)[:, NMB:NMB + 1], one(five), AX.X, ALU.add))
            do(nc.vector.tensor_scalar(one(tabf)[:, NMB:NMB + 1], one(tabf)[:, NMB:NMB + 1], NE / 2.0 - 2.0, None, ALU.add))
            nc.vector.tensor_copy(r.table, one(tabf)).then_inc(s_ready, 1)

        @block.tensor
        def _(pe):
            def modulate(i):
                pe.wait_ge(s_w[i % SLOTS], 16 * (i // SLOTS + 1))
                o = ps[0:2, 2 + i // 4, (i % 4) * P:(i % 4 + 1) * P]
                for k in range(KD):
                    nc.tensor.matmul(o, sc.rearrange("p (k s) -> p k s", s=2)[:, k, :],
                                     WM[:, i % SLOTS, k * P:(k + 1) * P], start=(k == 0), stop=False)
                nc.tensor.matmul(o, kit.const("one")[0:1, 0:2], BM[0:1, i * P:(i + 1) * P],
                                 start=False, stop=True).then_inc(s_mod, 1)

            pe.wait_ge(s_mask, 1)
            for c in range(NC):
                for d in range(c):
                    nc.tensor.matmul(ps[:, 0, c * NE:(c + 1) * NE], oneb, sbf[:, d, :], start=(d == 0), stop=False)
                nc.tensor.matmul(ps[:, 0, c * NE:(c + 1) * NE], ltb, sbf[:, c, :], start=(c == 0), stop=True)
            for c in range(NC):
                last = nc.tensor.matmul(ps[:, 1, 0:NE], oneb, sbf[:, c, :], start=(c == 0), stop=(c == NC - 1))
            last.then_inc(s_pe, 1)
            pe.wait_ge(s_silu, 1)
            pe.wait_ge(s_bias, 16)
            for i in range(NP):
                modulate(i)

        @block.gpsimd
        def _(pool):
            for q in range(3):
                ex.split_lo(pool, 0, zero, q, ops=nc.gpsimd)
            pool.wait_ge(s_ready, 1)
            for c in range(NC):
                for k in range(2):
                    pool.indirect_dma_start(out=scr["xs"], out_offset=bass.IndirectOffsetOnAxis(ap=r.slot[k][:, c:c + 1], axis=0),
                                            in_=h2[:, c, :], in_offset=None).then_inc(s_sc, 16)
            pool.wait_ge(s_sc, 16 * 2 * NC)


class Pair:

    def __init__(self, register, constant):
        self.register, self.constant = register, constant

    def times(self, a, b):
        b += a * self.constant
        return b if self.register is None else self.register * a + b

    def plus(self, n):
        return Pair(self.register, self.constant + n)


def is_block(u, j, b):
    return j.register is None and 2 * j.constant + u == b


class Experts:

    def __init__(self, kit):
        self.kit, self.nc = kit, kit.nc
        self.raw = [kit.at(O_RAW + UNIT * q, UNIT) for q in range(6)]
        self.rows = O_X + 6 * UNIT
        self.loaded = [kit.sem(f"e_unit_loaded{q}") for q in range(6)]
        self.hi_ready, self.lo_ready, self.used = (kit.sem("e_" + n) for n in ("hi_ready", "lo_ready", "unit_used"))

    def parts(self):
        self.hi, self.lo = self.kit.rnd(O_X, 3, UNIT), self.kit.rnd(O_X + 3 * UNIT, 3, UNIT)

    def source(self, io, e, q):
        w = io[("wg", "wu", "wd")[q // 2]]
        src = w[e] if isinstance(e, int) else w[bass.ds(e, 1)].rearrange("a p d -> (a p) d")
        return src[:, (q % 2) * UNIT:(q % 2 + 1) * UNIT]

    def load(self, eng, io, e, q):
        eng.dma_start(self.raw[q], self.source(io, e, q)).then_inc(self.loaded[q], 16)

    def index(self, u, j, q, more=0):
        return q + more if is_block(u, j, 0) else j.times(12, 6 * u + q - 2 + more)

    def through(self, u, j, q):
        return self.index(u, j, q, 1)

    def slot_free(self, u, j, q):
        if q < 3 and (is_block(u, j, 0) or is_block(u, j, 1)):
            return (4, 2, 3)[q] if u else None
        return self.index(u, j, q, -2)

    def split_hi(self, act, u, j, q, free=None):
        if free is None:
            free = self.slot_free(u, j, q)
        act.wait_ge(self.loaded[q], j.times(32, 16 * (u + 1 if q < 4 else u)))
        if free is not None:
            act.wait_ge(self.used, free)
        self.nc.scalar.activation(self.hi[:, q % 3, :], self.raw[q], ACT.Copy).then_inc(self.hi_ready, 1)

    def split_lo(self, dve, u, j, q, free=None, hi_ready=None, ops=None):
        if free is None:
            free = self.slot_free(u, j, q)
            hi_ready = self.index(u, j, q, 1)
        dve.wait_ge(self.hi_ready, hi_ready)
        if free is not None:
            dve.wait_ge(self.used, free)
        (ops or self.nc.vector).tensor_tensor(self.lo[:, q % 3, :], self.raw[q], self.hi[:, q % 3, :].bitcast(F32),
                                     ALU.subtract).then_inc(self.lo_ready, 1)


def stage_experts(kit, io, scr, ex):
    nc, ps = kit.nc, kit.ps
    r = Routing(kit)
    XB, YB = kit.at(ex.rows, 2, D), kit.at(ex.rows + 2048, 2, D)
    AB = kit.at(ex.rows + 4096, FE)
    HB = [kit.rnd(O_MG + 1024 * i, KD, P) for i in range(2)]
    AT_ = [kit.rnd(O_MG + 2048 + 512 * i, 4, P) for i in range(2)]
    ident = kit.const("ident")
    rows_loaded, y_stored = ([kit.sem(f"e_{n}{u}") for u in range(2)] for n in ("rows_loaded", "y_stored"))
    (rows_turned, rows_hi, rows_lo, silu, product, product_turned, product_hi, product_lo, y_low, y_high, y_free) = (
        kit.sem("e_" + n) for n in ("rows_turned", "rows_hi", "rows_lo", "silu", "product", "product_turned",
                                    "product_hi", "product_lo", "y_low", "y_high", "y_free"))
    xs = scr["xs"].rearrange("(b p) d -> b p d", p=P)
    ys = scr["ys"].rearrange("(b p) d -> b p d", p=P)
    row = lambda ap: ap.rearrange("a p d -> (a p) d")
    inner = lambda eng: eng.value_load(r.table[0:1, NMB:NMB + 1], min_val=NE // 2 - 2, max_val=NMB // 2 - 2)
    expert = lambda eng, b: eng.value_load(r.table[0:1, bass.ds(b, 1)], min_val=0, max_val=NE - 1)
    after = lambda u, j: (1, j) if u == 0 else (0, j.plus(1))
    before = lambda u, j: (1, j.plus(-1)) if u == 0 else (0, j)
    count = lambda u, j, more=0: j.times(2, u + 1 + more)
    zero = Pair(None, 0)

    with nc.Block() as block:
        @block.sync
        def _(sp):
            n = inner(sp)
            last_pair = Pair(n, 1)
            sp.dma_start(XB[:, 0, :], xs[0]).then_inc(rows_loaded[0], 16)
            sp.dma_start(XB[:, 1, :], xs[1]).then_inc(rows_loaded[1], 16)
            sp.wait_ge(ex.lo_ready, 4)
            ex.load(sp, io, 1, 3)
            sp.wait_ge(rows_turned, 1)
            sp.dma_start(XB[:, 0, :], xs[2]).then_inc(rows_loaded[0], 16)

            def load_step(u, j, is_last=False):
                e = expert(sp, j.times(2, u))
                d = expert(sp, j.times(2, u - 1))
                for q in range(6):
                    sp.wait_ge(ex.lo_ready, ex.index(u, j, q, -5))
                    ex.load(sp, io, e if q < 4 else d, q)
                    if q == 3 and not is_last:
                        v, _ = after(u, j)
                        sp.wait_ge(rows_turned, count(u, j, -1))
                        sp.dma_start(XB[:, v, :], row(xs[bass.ds(j.times(2, u + 1), 1)])).then_inc(rows_loaded[v], 16)
                return e

            with sp.Fori(0, n) as i:
                for u in range(2):
                    load_step(u, Pair(i, 1))
            load_step(0, last_pair)
            e = load_step(1, last_pair, is_last=True)
            for q in (4, 5):
                sp.wait_ge(ex.lo_ready, last_pair.times(12, 5 + q))
                ex.load(sp, io, e, q)

        @block.gpsimd
        def _(pool):
            n = inner(pool)

            def store(u, j):
                pool.wait_ge(y_low, count(u, j))
                pool.wait_ge(y_high, count(u, j))
                pool.dma_start(row(ys[bass.ds(j.times(2, u), 1)]), YB[:, u, :]).then_inc(y_stored[u], 16)
                pool.wait_ge(y_stored[u], j.times(16, 16))
                pool.sem_inc(y_free, 1)

            store(0, zero)
            store(1, zero)
            with pool.Fori(0, n) as i:
                for u in range(2):
                    store(u, Pair(i, 1))
            store(0, Pair(n, 1))
            store(1, Pair(n, 1))

        @block.tensor
        def _(pe):
            n = inner(pe)
            last_pair = Pair(n, 1)

            def unit_ready(ready):
                pe.wait_ge(ex.hi_ready, ready)
                pe.wait_ge(ex.lo_ready, ready)

            def turn_rows(u, j):
                pe.wait_ge(rows_loaded[u], j.times(16, 16))
                if not (is_block(u, j, 0) or is_block(u, j, 1)):
                    pe.wait_ge(product_lo, count(u, j, -2))
                for k in range(KD):
                    last = nc.tensor.transpose(ps[:, 6 + k // 4, (k % 4) * P:(k % 4 + 1) * P], XB[:, u, k * P:(k + 1) * P], ident)
                last.then_inc(rows_turned, 1)

            def gate_and_up(u, j):
                pe.wait_ge(rows_hi, count(u, j))
                pe.wait_ge(rows_lo, count(u, j))
                if not (is_block(u, j, 0) or is_block(u, j, 1)):
                    pe.wait_ge(product, count(u, j, -2))
                for q in range(4):
                    unit_ready(ex.through(u, j, q))
                    hi, lo = ex.hi[:, q % 3, :], ex.lo[:, q % 3, :]
                    o = ps[:, 2 * u + q // 2, :]
                    for k in range(4):
                        kk, cols = 4 * (q % 2) + k, slice(k * FE, (k + 1) * FE)
                        nc.tensor.matmul(o, HB[0][:, kk, :], hi[:, cols], start=(kk == 0), stop=False)
                        nc.tensor.matmul(o, HB[0][:, kk, :], lo[:, cols], start=False, stop=False)
                        last = nc.tensor.matmul(o, HB[1][:, kk, :], hi[:, cols], start=False, stop=(kk == KD - 1))
                    last.then_inc(ex.used, 1)

            def turn_product(u, j, is_last=False):
                if not is_last:
                    pe.wait_ge(rows_lo, count(u, j, 1))
                pe.wait_ge(product, count(u, j))
                for k in range(4):
                    last = nc.tensor.transpose(ps[:, 6, k * P:(k + 1) * P], AB[:, k * P:(k + 1) * P], ident)
                last.then_inc(product_turned, 1)

            def down(u, j, ready):
                pe.wait_ge(product_hi, count(u, j))
                pe.wait_ge(product_lo, count(u, j))
                if not is_block(u, j, 0):
                    pe.wait_ge(y_low, count(u, j, -1))
                    pe.wait_ge(y_high, count(u, j, -1))
                for q in (4, 5):
                    unit_ready(ready[q - 4])
                    hi, lo = ex.hi[:, q % 3, :], ex.lo[:, q % 3, :]
                    for k in range(2):
                        kk = 2 * (q - 4) + k
                        for h in range(2):
                            o, cols = ps[:, 4 + h, :], slice(k * D + h * 512, k * D + (h + 1) * 512)
                            nc.tensor.matmul(o, AT_[0][:, kk, :], hi[:, cols], start=(kk == 0), stop=False)
                            nc.tensor.matmul(o, AT_[0][:, kk, :], lo[:, cols], start=False, stop=False)
                            last = nc.tensor.matmul(o, AT_[1][:, kk, :], hi[:, cols], start=False, stop=(kk == 3))
                    last.then_inc(ex.used, 1)

            def step(u, j, is_last=False):
                gate_and_up(u, j)
                if not is_last:
                    turn_rows(*after(u, j))
                if not is_block(u, j, 0):
                    down(*before(u, j), [ex.through(u, j, q) for q in (4, 5)])
                turn_product(u, j, is_last)

            turn_rows(0, zero)
            step(0, zero)
            step(1, zero)
            with pe.Fori(0, n) as i:
                for u in range(2):
                    step(u, Pair(i, 1))
            step(0, last_pair)
            step(1, last_pair, is_last=True)
            down(1, last_pair, [last_pair.times(12, 11 + q) for q in range(2)])

        @block.scalar
        def _(act):
            n = inner(act)
            last_pair = Pair(n, 1)

            def take_rows(u, j):
                act.wait_ge(rows_turned, count(u, j))
                if not is_block(u, j, 0):
                    act.wait_ge(ex.used, ex.through(*before(u, j), 3))
                nc.scalar.activation(HB[0].rearrange("p k n -> p (k n)"), ps[:, 6:8, :].rearrange("p a b -> p (a b)"),
                                     ACT.Copy).then_inc(rows_hi, 1)

            def silu_gate(u, j):
                act.wait_ge(ex.used, ex.through(u, j, 3))
                if not is_block(u, j, 0):
                    act.wait_ge(product_turned, count(u, j, -1))
                nc.scalar.activation(AB, ps[:, 2 * u, :], ACT.Silu).then_inc(silu, 1)

            def take_product(u, j):
                act.wait_ge(product_turned, count(u, j))
                if not is_block(u, j, 0):
                    act.wait_ge(ex.used, ex.through(u, j, 5))
                nc.scalar.activation(AT_[0].rearrange("p k n -> p (k n)"), ps[:, 6, :], ACT.Copy).then_inc(product_hi, 1)

            def take_y(u, j, used):
                act.wait_ge(ex.used, used)
                if not (is_block(u, j, 0) or is_block(u, j, 1)):
                    act.wait_ge(y_free, count(u, j, -2))
                nc.scalar.activation(YB[:, u, 0:512], ps[:, 4, :], ACT.Copy).then_inc(y_low, 1)

            def step(u, j):
                ex.split_hi(act, u, j, 3)
                if not is_block(u, j, 0):
                    ex.split_hi(act, u, j, 4)
                    ex.split_hi(act, u, j, 5)
                silu_gate(u, j)
                ex.split_hi(act, *after(u, j), 0)
                take_rows(*after(u, j))
                ex.split_hi(act, *after(u, j), 1)
                if not is_block(u, j, 0):
                    take_y(*before(u, j), ex.through(u, j, 5))
                ex.split_hi(act, *after(u, j), 2)
                take_product(u, j)

            take_rows(0, zero)
            step(0, zero)
            step(1, zero)
            with act.Fori(0, n) as i:
                for u in range(2):
                    step(u, Pair(i, 1))
            step(0, last_pair)
            for q in (3, 4, 5):
                ex.split_hi(act, 1, last_pair, q)
            silu_gate(1, last_pair)
            ex.split_hi(act, 0, last_pair.plus(1), 4, free=last_pair.times(12, 9))
            take_y(0, last_pair, ex.through(1, last_pair, 5))
            ex.split_hi(act, 0, last_pair.plus(1), 5, free=last_pair.times(12, 10))
            take_product(1, last_pair)
            take_y(1, last_pair, last_pair.times(12, 12))

        @block.vector
        def _(dve):
            n = inner(dve)
            last_pair = Pair(n, 1)
            tt = nc.vector.tensor_tensor

            def take_rows(u, j):
                dve.wait_ge(rows_hi, count(u, j))
                tt(HB[1].rearrange("p k n -> p (k n)"), ps[:, 6:8, :].rearrange("p a b -> p (a b)"),
                   HB[0].rearrange("p k n -> p (k n)").bitcast(F32), ALU.subtract).then_inc(rows_lo, 1)

            def multiply(u, j):
                dve.wait_ge(silu, count(u, j))
                tt(AB, AB, ps[:, 2 * u + 1, :], ALU.mult).then_inc(product, 1)

            def take_product(u, j):
                dve.wait_ge(product_hi, count(u, j))
                tt(AT_[1].rearrange("p k n -> p (k n)"), ps[:, 6, :],
                   AT_[0].rearrange("p k n -> p (k n)").bitcast(F32), ALU.subtract).then_inc(product_lo, 1)

            def take_y(u, j, used):
                dve.wait_ge(ex.used, used)
                if not (is_block(u, j, 0) or is_block(u, j, 1)):
                    dve.wait_ge(y_free, count(u, j, -2))
                nc.vector.tensor_copy(YB[:, u, 512:1024], ps[:, 5, :]).then_inc(y_high, 1)

            def step(u, j):
                ex.split_lo(dve, u, j, 3)
                if not is_block(u, j, 0):
                    ex.split_lo(dve, u, j, 4)
                    ex.split_lo(dve, u, j, 5)
                multiply(u, j)
                ex.split_lo(dve, *after(u, j), 0)
                take_rows(*after(u, j))
                ex.split_lo(dve, *after(u, j), 1)
                if not is_block(u, j, 0):
                    take_y(*before(u, j), ex.through(u, j, 5))
                ex.split_lo(dve, *after(u, j), 2)
                take_product(u, j)

            take_rows(0, zero)
            step(0, zero)
            step(1, zero)
            with dve.Fori(0, n) as i:
                for u in range(2):
                    step(u, Pair(i, 1))
            step(0, last_pair)
            for q in (3, 4, 5):
                ex.split_lo(dve, 1, last_pair, q)
            multiply(1, last_pair)
            ex.split_lo(dve, 0, last_pair.plus(1), 4, free=last_pair.times(12, 9), hi_ready=last_pair.times(12, 11))
            take_y(0, last_pair, ex.through(1, last_pair, 5))
            ex.split_lo(dve, 0, last_pair.plus(1), 5, free=last_pair.times(12, 10), hi_ready=last_pair.times(12, 12))
            take_product(1, last_pair)
            take_y(1, last_pair, last_pair.times(12, 12))


def stage_combine(kit, scr, out):
    nc = kit.nc
    r = Routing(kit)
    x2 = kit.at(O_H, NC, D)
    G2, FN = kit.at(T_G2, 2, D), kit.at(T_FN, D)
    Y = kit.at(O_X, 2 * NC, D)
    sq, ssq, rr = kit.at(O_MG, D), kit.at(O_MG + 1024, NC), kit.at(O_MG + 1032, NC)
    O = kit.at(O_MG + 1040, 2, D)
    s_y = [kit.sem(f"f_rows{c}") for c in range(NC)]
    s_sq, s_rt = kit.sem("f_squares"), kit.sem("f_root")
    s_st = [kit.sem(f"f_stored{j}") for j in range(2)]
    s_a, s_m, s_g, s_x2, s_ms, s_n = (kit.sem("f_" + n) for n in ("weighted", "merged", "gated", "x", "mean", "normed"))
    with nc.Block() as block:
        @block.gpsimd
        def _(pool):
            for c in range(NC):
                for k in range(2):
                    pool.indirect_dma_start(out=Y[:, 2 * c + k, :], out_offset=None, in_=scr["ys"],
                                            in_offset=bass.IndirectOffsetOnAxis(ap=r.slot[k][:, c:c + 1], axis=0)).then_inc(s_y[c], 16)
            for c in range(NC):
                pool.wait_ge(s_m, c + 1)
                nc.gpsimd.tensor_tensor(Y[:, 2 * c, :], Y[:, 2 * c, :], G2[:, min(c, 1), :], ALU.mult).then_inc(s_g, 1)

        @block.vector
        def _(dve):
            def merge(c):
                dve.wait_ge(s_a, c + 1)
                nc.vector.scalar_tensor_tensor(out=Y[:, 2 * c, :], in0=Y[:, 2 * c + 1, :], scalar=r.weight[:, 1, c:c + 1],
                                               in1=Y[:, 2 * c, :], op0=ALU.mult, op1=ALU.add).then_inc(s_m, 1)

            def add(c):
                dve.wait_ge(s_g, c + 1)
                nc.vector.tensor_tensor(x2[:, c, :], x2[:, c, :], Y[:, 2 * c, :], ALU.add).then_inc(s_x2, 1)

            def mean(c):
                dve.wait_ge(s_sq, c + 1)
                nc.vector.tensor_scalar(ssq[:, c:c + 1], ssq[:, c:c + 1], 1.0 / D, EPS, ALU.mult, ALU.add).then_inc(s_ms, 1)
                dve.wait_ge(s_ms, 2 * c + 1)
                nc.vector.reciprocal(rr[:, c:c + 1], ssq[:, c:c + 1]).then_inc(s_ms, 1)

            def norm(c):
                dve.wait_ge(s_rt, c + 1)
                if c >= 2:
                    dve.wait_ge(s_st[c % 2], 16 * (c // 2))
                nc.vector.scalar_tensor_tensor(out=O[:, c % 2, :], in0=x2[:, c, :], scalar=rr[:, c:c + 1], in1=FN,
                                               op0=ALU.mult, op1=ALU.mult).then_inc(s_n, 1)

            merge(0)
            for c in range(NC):
                if c + 1 < NC:
                    merge(c + 1)
                add(c)
                if c:
                    norm(c - 1)
                mean(c)
            norm(NC - 1)

        @block.scalar
        def _(act):
            def weigh(c):
                act.wait_ge(s_y[c], 32)
                nc.scalar.activation(Y[:, 2 * c, :], Y[:, 2 * c, :], ACT.Copy, scale=r.weight[:, 0, c:c + 1]).then_inc(s_a, 1)

            weigh(0)
            weigh(1)
            for c in range(NC):
                if c + 2 < NC:
                    weigh(c + 2)
                act.wait_ge(s_x2, c + 1)
                if c:
                    act.wait_ge(s_sq, c)
                nc.scalar.activation(sq, x2[:, c, :], ACT.Square, accum_out=ssq[:, c:c + 1]).then_inc(s_sq, 1)
                act.wait_ge(s_ms, 2 * c + 2)
                nc.scalar.activation(rr[:, c:c + 1], rr[:, c:c + 1], ACT.Sqrt).then_inc(s_rt, 1)

        @block.sync
        def _(sp):
            for c in range(NC):
                sp.wait_ge(s_n, c + 1)
                dst = out["y_prompt"] if c == 0 else out["y_sample"][(c - 1) * P:c * P, :]
                sp.dma_start(dst, O[:, c % 2, :]).then_inc(s_st[c % 2], 16)
            sp.wait_ge(s_st[0], 48)
            sp.wait_ge(s_st[1], 32)


def scratch(nc):
    dram = lambda name, shape: nc.dram_tensor(name, shape, F32, kind="Internal").ap()
    return dict(xp=dram("x_plus_pos", [T, D]), xs=dram("slot_rows", [(NMB + 1) * P, D]), ys=dram("expert_rows", [NMB * P, D]),
                z=dram("silu_z", [T, INNER]), gb=dram("gate_b", [KD, P, T]), mod=dram("modulation", [2, 4 * D]))


def build(nc, io, out):
    with ExitStack() as ctx:
        kit, scr = Kit(nc, ctx), scratch(nc)
        stream = Weights(kit, "first", io["units"][0:40])
        ht = stage_modulate(kit, stream, io, scr)
        ya = stage_gmlp(kit, stream, io, scr, ht)
        stage_branch_a(kit, stream, ya)
        stage_conv(kit, stream, io)
        stage_gates(kit, stream, scr)
        stage_ssd(kit, io, scr, out)
        kit.recycle()
        stream = Weights(kit, "second", io["units"][40:52])
        stage_norm_y(kit, stream, io, scr)
        stage_branch_b(kit, stream, scr)
        ex = Experts(kit)
        stage_out(kit, stream, io, scr, ex)
        stage_route(kit, io, scr, ex)
        stage_experts(kit, io, scr, ex)
        stage_combine(kit, scr, out)


def host_layout(i):
    import numpy as np
    a = {k: np.asarray(v) for k, v in i.items()}
    w_in = a["w_in"][0]
    cut = [0, 1024, 2048, 3072, 4096, 6144, 9216, 9280]
    ga, gb, u, v, z, xbc, dt = [w_in[:, cut[j]:cut[j + 1]] for j in range(7)]

    def units(w, cols):
        r, n = w.shape
        return w.reshape(r // P, P, n // cols, cols).transpose(2, 1, 0, 3).reshape(n // cols, P, -1)

    stream = [units(v, UC), units(u, UC), units(ga, UC), units(a["w_branch_a"][0], UC), units(xbc, UC), units(z, UC),
              units(gb, UC), units(a["w_branch_b"][0], P), units(a["w_out"][0], UC)]
    o = {"units": np.concatenate(stream, 0)}
    o["w_dt"] = units(dt, 64)[0]
    o["w_mod"] = units(a["w_mod"][0][:, :2 * D], 512)
    o["w_mod_rest"] = units(a["w_mod"][0][:, 2 * D:], P)
    o["b_mod"] = a["b_mod"][0][None]
    o["cond"] = np.stack([a["c_ctx"], a["c"][0]], 0).reshape(2, KD, P).transpose(2, 1, 0).reshape(P, 16)
    o["x"] = np.concatenate([a["x_prompt"][0], a["x_sample"][0]], 0)
    col = lambda w: w.reshape(-1, P).T
    o["norm1"] = col(a["norm1_w"][0])
    o["wsT"] = a["gmlp_ws"][0].transpose(2, 0, 1)
    o["gmlp_nw"] = col(a["gmlp_norm_w"][0])
    o["gmlp_bs"] = a["gmlp_bs"][0].reshape(1, -1)
    o["dt_bias"] = a["dt_bias"][0].reshape(64, 1)
    o["a_log"] = a["a_log"][0].reshape(1, 64)
    o["conv_w"] = a["conv_w"][0].reshape(TAPS, -1, P).transpose(2, 1, 0).reshape(P, -1)
    o["conv_b"] = col(a["conv_b"][0])
    o["state_t"] = a["state_ssd"][0, 0].reshape(2, INNER, P).transpose(0, 2, 1)
    o["d_skip"] = a["d_skip"].reshape(1, HEADS)
    o["ssd_nw"] = col(a["ssd_norm_w"][0])
    o["norm2"], o["fnorm"] = a["norm2_w"][0].reshape(1, D), a["final_norm_w"].reshape(1, D)
    o["router_w"], o["router_b"] = units(a["router_w"], NE)[0], a["router_bias"].reshape(1, NE)
    experts = lambda w: w.reshape(NE, w.shape[1] // P, P, w.shape[2]).transpose(0, 2, 1, 3).reshape(NE, P, -1)
    o["wg"], o["wu"], o["wd"] = experts(a["w_gate_e"][0]), experts(a["w_up_e"][0]), experts(a["w_down_e"][0])
    grid = 64
    omega = 1.0 / (10000.0 ** (np.arange(D // 4, dtype=np.float32) / np.float32(D // 4)))
    r = np.arange(LAT // grid, dtype=np.float32)[:, None] * omega
    cc = np.arange(grid, dtype=np.float32)[:, None] * omega
    r = np.concatenate([np.sin(r), np.cos(r)], -1)
    cc = np.concatenate([np.sin(cc), np.cos(cc)], -1)
    pos = np.concatenate([np.repeat(r, grid, 0), np.tile(cc, (LAT // grid, 1))], -1).astype(np.float32)
    o["pos"] = pos
    K = np.zeros((P, KOFF["end"]), np.float32)
    p, q = np.arange(P)[:, None], np.arange(P)[None]
    for name, m in (("ident", p == q), ("le", p <= q), ("ge", p >= q), ("gt", p > q), ("lt", p < q), ("one", p >= 0)):
        K[:, KOFF[name]:KOFF[name] + P] = m
    K[:, KOFF["e128"]:KOFF["e128"] + 16] = np.arange(16) * 128
    K[:, KOFF["pri16"]:KOFF["pri16"] + 16] = 16 - np.arange(16)
    K[:, KOFF["pri4"]:KOFF["pri4"] + 4] = 4 - np.arange(4)
    K[:, KOFF["thr"]:KOFF["thr"] + 5] = 2 * np.arange(5)
    K[:, KOFF["col"]:KOFF["col"] + 26] = np.arange(26)
    o["consts"] = K
    return {k: np.ascontiguousarray(v) for k, v in o.items()}


def kernel(**inputs):
    import numpy as np
    import concourse.bacc as bacc
    from concourse.bass_utils import run_bass_kernel_spmd

    nc = bacc.Bacc("TRN2", target_bir_lowering=False, num_devices=1)
    arrays = host_layout(inputs)
    io = {k: nc.dram_tensor("in_" + k, v.shape, mybir.dt.from_np(v.dtype), kind="ExternalInput").ap()
          for k, v in arrays.items()}
    shapes = dict(y_prompt=(P, D), y_sample=(LAT, D), state=(2, INNER, P))
    out = {k: nc.dram_tensor("out_" + k, s, F32, kind="ExternalOutput").ap() for k, s in shapes.items()}
    build(nc, io, out)
    r = run_bass_kernel_spmd(nc, [{"in_" + k: v for k, v in arrays.items()}], core_ids=[0]).results[0]
    return (np.asarray(r["out_y_prompt"]).reshape(1, P, D), np.asarray(r["out_y_sample"]).reshape(1, LAT, D),
            np.asarray(r["out_state"]).reshape(1, 1, 2, HEADS, HD, P))
```
